# Optimizing a Trainium2 kernel written in Bass

```python
import jax, jax.numpy as jnp
from jax import lax
import numpy as np

D_MODEL = 1024
BATCH = 1
SEQ = 1024
DEPTH = 1

SB_HEADS = 8
SB_HEAD_DIM = 64
SB_WIDTH = SB_HEADS * SB_HEAD_DIM
MLA_HEADS = 4
MLA_NOPE_DIM = 128
MLA_ROPE_DIM = 64
MLA_QK_DIM = MLA_NOPE_DIM + MLA_ROPE_DIM
MLA_V_DIM = 128
MLA_Q_RANK = 384
MLA_KV_RANK = 256
MLA_WIDTH = MLA_HEADS * MLA_V_DIM
MIX_WIDTH = SB_WIDTH + MLA_WIDTH
IN_PROJ_WIDTH = 3 * SB_WIDTH + MLA_Q_RANK + MLA_KV_RANK + MLA_ROPE_DIM
D_FF = -(-8 * D_MODEL // (3 * 256)) * 256
N_MOD = 6
BLOCK_Q = 128
ROPE_THETA = 10000.0
EPS = 1e-6

kernel_name = "hymba_sb_mla_adaln_layer"

def rms_norm(x, g):
    xf = x.astype(jnp.float32)
    y = xf * lax.rsqrt(jnp.mean(xf * xf, axis=-1, keepdims=True) + EPS)
    return (y * g.astype(jnp.float32)).astype(x.dtype)

def apply_rope(x, positions):
    half = x.shape[-1] // 2
    freqs = 1.0 / (ROPE_THETA ** (jnp.arange(half, dtype=jnp.float32) / half))
    ang = positions.astype(jnp.float32)[:, :, None, None] * freqs
    cos, sin = jnp.cos(ang), jnp.sin(ang)
    xf = x.astype(jnp.float32)
    x1, x2 = xf[..., :half], xf[..., half:]
    return jnp.concatenate([x1 * cos - x2 * sin, x2 * cos + x1 * sin], axis=-1).astype(x.dtype)

def stick_breaking_attention(q, k, v):
    S = q.shape[1]
    scale = SB_HEAD_DIM ** -0.5
    outs = []
    for i in range(S // BLOCK_Q):
        q0 = i * BLOCK_Q
        kend = q0 + BLOCK_Q
        z = jnp.einsum('bthd,bshd->bhts', q[:, q0:kend], k[:, :kend]).astype(jnp.float32) * scale
        t_idx = q0 + jnp.arange(BLOCK_Q)[:, None]
        s_idx = jnp.arange(kend)[None, :]
        strict = s_idx < t_idx
        log_beta = jax.nn.log_sigmoid(z)
        log_1m = jnp.where(strict, jax.nn.log_sigmoid(-z), 0.0)
        after = lax.cumsum(log_1m, axis=3, reverse=True) - log_1m
        w = jnp.where(strict, jnp.exp(log_beta + after), 0.0)
        outs.append(jnp.einsum('bhts,bshd->bthd', w.astype(v.dtype), v[:, :kend]))
    return jnp.concatenate(outs, axis=1)

def causal_softmax_attention(q, k, v):
    S = q.shape[1]
    scale = MLA_QK_DIM ** -0.5
    outs = []
    for i in range(S // BLOCK_Q):
        q0 = i * BLOCK_Q
        kend = q0 + BLOCK_Q
        s = jnp.einsum('bthd,bshd->bhts', q[:, q0:kend], k[:, :kend]).astype(jnp.float32) * scale
        causal = jnp.arange(kend)[None, :] <= (q0 + jnp.arange(BLOCK_Q))[:, None]
        p = jax.nn.softmax(jnp.where(causal, s, -jnp.inf), axis=-1)
        outs.append(jnp.einsum('bhts,bshd->bthd', p.astype(v.dtype), v[:, :kend]))
    return jnp.concatenate(outs, axis=1)

def setup_inputs(seed: int = 0) -> dict:
    key = jax.random.key(seed)
    ks = jax.random.split(key, 24)
    f32 = jnp.float32

    def w(k, shape, fan_in):
        return jax.random.normal(k, shape, f32) * (fan_in ** -0.5)

    def gain(k, n):
        return 1.0 + 0.01 * jax.random.normal(k, (DEPTH, n), f32)

    x = jax.random.normal(ks[0], (BATCH, SEQ, D_MODEL), f32)
    c = jax.random.normal(ks[1], (BATCH, D_MODEL), f32)
    offsets = jax.random.randint(ks[2], (BATCH, 1), 0, 512, dtype=jnp.int32)
    positions = offsets + jnp.arange(SEQ, dtype=jnp.int32)[None, :]
    return {
        "x": x,
        "c": c,
        "positions": positions,
        "w_ada": w(ks[3], (DEPTH, D_MODEL, N_MOD * D_MODEL), D_MODEL) * 0.5,
        "b_ada": 0.01 * jax.random.normal(ks[4], (DEPTH, N_MOD * D_MODEL), f32),
        "norm_attn": gain(ks[5], D_MODEL),
        "norm_ffn": gain(ks[6], D_MODEL),
        "w_in": w(ks[7], (DEPTH, D_MODEL, IN_PROJ_WIDTH), D_MODEL),
        "q_a_norm": gain(ks[8], MLA_Q_RANK),
        "w_q_up": w(ks[9], (DEPTH, MLA_Q_RANK, MLA_HEADS * MLA_QK_DIM), MLA_Q_RANK),
        "kv_a_norm": gain(ks[10], MLA_KV_RANK),
        "w_kv_up": w(ks[11], (DEPTH, MLA_KV_RANK, MLA_HEADS * (MLA_NOPE_DIM + MLA_V_DIM)), MLA_KV_RANK),
        "q_norm": gain(ks[12], MLA_QK_DIM),
        "k_nope_norm": gain(ks[13], MLA_NOPE_DIM),
        "k_rope_norm": gain(ks[14], MLA_ROPE_DIM),
        "out_norm_sb": gain(ks[15], SB_WIDTH),
        "out_norm_mla": gain(ks[16], MLA_WIDTH),
        "w_out": w(ks[17], (DEPTH, MIX_WIDTH, D_MODEL), MIX_WIDTH),
        "w_gate": w(ks[18], (DEPTH, D_MODEL, D_FF), D_MODEL),
        "w_up": w(ks[19], (DEPTH, D_MODEL, D_FF), D_MODEL),
        "w_down": w(ks[20], (DEPTH, D_FF, D_MODEL), D_FF),
    }

def reference(x, c, positions, w_ada, b_ada, norm_attn, norm_ffn, w_in, q_a_norm, w_q_up,
              kv_a_norm, w_kv_up, q_norm, k_nope_norm, k_rope_norm, out_norm_sb, out_norm_mla,
              w_out, w_gate, w_up, w_down):
    B, S, _ = x.shape
    for l in range(DEPTH):
        mod = jax.nn.silu(c) @ w_ada[l] + b_ada[l]
        shift1, scale1, gate1, shift2, scale2, gate2 = [m[:, None, :] for m in jnp.split(mod, N_MOD, axis=-1)]

        h = rms_norm(x, norm_attn[l]) * (1.0 + scale1) + shift1
        proj = h @ w_in[l]
        cuts = np.cumsum([SB_WIDTH, SB_WIDTH, SB_WIDTH, MLA_Q_RANK, MLA_KV_RANK]).tolist()
        q_sb, k_sb, v_sb, c_q, c_kv, k_rope = jnp.split(proj, cuts, axis=-1)

        q_sb = q_sb.reshape(B, S, SB_HEADS, SB_HEAD_DIM)
        k_sb = k_sb.reshape(B, S, SB_HEADS, SB_HEAD_DIM)
        v_sb = v_sb.reshape(B, S, SB_HEADS, SB_HEAD_DIM)
        o_sb = stick_breaking_attention(q_sb, k_sb, v_sb).reshape(B, S, SB_WIDTH)

        q = (rms_norm(c_q, q_a_norm[l]) @ w_q_up[l]).reshape(B, S, MLA_HEADS, MLA_QK_DIM)
        kv = (rms_norm(c_kv, kv_a_norm[l]) @ w_kv_up[l]).reshape(B, S, MLA_HEADS, MLA_NOPE_DIM + MLA_V_DIM)
        k_nope, v_mla = kv[..., :MLA_NOPE_DIM], kv[..., MLA_NOPE_DIM:]
        q = rms_norm(q, q_norm[l])
        k_nope = rms_norm(k_nope, k_nope_norm[l])
        k_rope = rms_norm(k_rope, k_rope_norm[l])[:, :, None, :]
        q = jnp.concatenate([q[..., :MLA_NOPE_DIM], apply_rope(q[..., MLA_NOPE_DIM:], positions)], axis=-1)
        k_rope = jnp.broadcast_to(apply_rope(k_rope, positions), (B, S, MLA_HEADS, MLA_ROPE_DIM))
        k = jnp.concatenate([k_nope, k_rope], axis=-1)
        o_mla = causal_softmax_attention(q, k, v_mla).reshape(B, S, MLA_WIDTH)

        mixed = jnp.concatenate([rms_norm(o_sb, out_norm_sb[l]), rms_norm(o_mla, out_norm_mla[l])], axis=-1)
        x = x + gate1 * (mixed @ w_out[l])

        h = rms_norm(x, norm_ffn[l]) * (1.0 + scale2) + shift2
        ffn = (jax.nn.silu(h @ w_gate[l]) * (h @ w_up[l])) @ w_down[l]
        x = x + gate2 * ffn
    return x


_drawn_inputs = setup_inputs


def setup_inputs(seed=0):
    import zlib

    import numpy as np

    out = dict(_drawn_inputs(seed))
    spreads = {}
    factors = {'b_ada': 3.931,
     'norm_attn': 8.0,
     'norm_ffn': 8.0,
     'q_a_norm': 8.0,
     'kv_a_norm': 8.0,
     'q_norm': 8.0,
     'k_nope_norm': 8.0,
     'k_rope_norm': 8.0,
     'out_norm_sb': 8.0,
     'out_norm_mla': 8.0}
    for name, (base, spread) in spreads.items():
        noise = np.random.default_rng([zlib.crc32(name.encode()), seed]).standard_normal(out[name].shape)
        drawn = base * np.exp(spread * noise) if base else spread * noise
        out[name] = __import__('jax').numpy.asarray(drawn.astype(out[name].dtype))
    for name, factor in factors.items():
        out[name] = (out[name] * factor).astype(out[name].dtype)
    return out
```

```python
import numpy as np
from contextlib import ExitStack
import concourse.bass as bass
from concourse import mybir

F32 = mybir.dt.float32
F32R = mybir.dt.float32r
BF16 = mybir.dt.bfloat16
I32 = mybir.dt.int32
ALU = mybir.AluOpType
ACT = mybir.ActivationFunctionType
AX = mybir.AxisListType

P = 128
S = 1024
D = 1024
NT = S // P
KD = D // P
SBH, SBD = 8, 64
MH, NOPE, ROPE, VD = 4, 128, 64, 128
QK = NOPE + ROPE
QR_, KVR = 384, 256
DFF = 2816
NF = DFF // P
EPS = 1e-6
HALF = ROPE // 2
NEG = -1e30
PRIME = 2

C_C, C_B, C_GA, C_GF, C_QA, C_KVA, C_KN = 0, 8, 56, 64, 72, 75, 77
NCOL = 78
R_Q, R_KR, R_FREQ = 0, QK, QK + ROPE
NROW = R_FREQ + HALF

W_COLS = [1536, 1664, 1792, 1920, 2048, 2112] + [128 * t for t in range(12)]
N_IN = len(W_COLS)
N_UP = 5
N_OUT = KD
H_OUT = N_IN
H_GU = H_OUT + N_OUT
H_DN = H_GU + 2 * NF


def raw_index(h):
    return h if h < N_IN else h + N_UP


class Chain:

    def __init__(self, eng, sem):
        self.eng, self.sem, self.base, self.n, self.at = eng, sem, 0, 0, 0

    def __call__(self, instruction):
        instruction.then_inc(self.sem, 1)
        self.n += 1
        return instruction

    def sync(self):
        self.eng.wait_ge(self.sem, self.at + self.n)

    def begin(self, i, per):
        self.base, self.n = self.base + self.n, 0
        self.at = self.base + i * per

    def end(self, times, per):
        assert self.n == per, (self.n, per)
        self.base, self.n = self.base + times * per, 0
        self.at = self.base


UNITS = [(0, i) for i in reversed(range(NT))] + [(1, i) for i in range(NT)]
NU = len(UNITS)
BLOCKS = [NT - i for _, i in UNITS]
G0 = [(b + 1) // 2 for b in BLOCKS]
G1_BEFORE = [sum(b > 1 for b in BLOCKS[:k]) for k in range(NU + 1)]
NG1 = G1_BEFORE[NU]


def build(nc, xT, cols_d, rows_d, grow_d, pos_d, ada1_d, ada2_d, win_d, qup_d, kvup_d, wout_d, gu_d, down_d, x2_d, out_d):
    ctx = ExitStack()
    base = 16512

    def at(name, shape, dt, kb):
        return nc.alloc_sbuf_tensor_at(name, shape, dt, offset=base + int(kb * 1024))

    ident = at("ident", [P, P], F32, 0)
    identb = at("identb", [P, P], BF16, 0.5)
    mask_sb = at("mask_sb", [P, P], BF16, 0.75)
    mask_mla = at("mask_mla", [P, P], BF16, 1.0)
    ones = at("ones", [P, P], F32, 1.5)
    cols = at("cols", [P, NCOL], F32, 2.0)
    rows = at("rows", [P, NROW], F32, 2.5)
    pos_i = at("pos_i", [P, NT], I32, 4.0)
    pos_f = at("pos_f", [P, NT], F32, 4.03125)
    trig = at("trig", [P, NT, 2, HALF], F32, 4.125)
    silu_c = at("silu_c", [P, KD], F32, 6.125)
    mod1 = at("mod1", [P, 16], F32, 6.25)
    a1 = at("a1", [P, KD], F32, 6.375)
    mod2 = at("mod2", [P, 32], F32, 6.5)
    a2 = at("a2", [P, KD], F32, 6.75)
    ssq = at("ssq", [P, 2, 16], F32, 7.0)
    rstd = at("rstd", [P, 2, 16], F32, 7.25)
    mx = at("mx", [P, NU], F32, 7.5)
    nmx = at("nmx", [P, NU], F32, 7.625)
    qms = at("qms", [P, 2, 16], F32, 8.125)
    den = at("den", [P, NU], F32, 7.75)
    rden = at("rden", [P, NU], F32, 7.875)
    oss = at("oss", [P, 2, 2], F32, 8.0)
    oms = at("oms", [P, 2, 2], F32, 8.0625)
    ors = at("ors", [P, 2, 2], F32, 8.03125)
    nhalf = at("nhalf", [P, 16], F32, 9.75)
    ms = at("ms", [P, 4, NT], F32, 9.8125)
    rms = at("rms", [P, 4, NT], F32, 8.25)
    WH = [at(f"WH{s}", [P, D], F32R, 10 + 8 * s) for s in range(2)]
    WL = [at(f"WL{s}", [P, D], F32R, 14 + 8 * s) for s in range(2)]
    raw = [at(f"raw{s}", [P, D], F32, 26 + 4 * s) for s in range(2)]
    hH = at("hH", [P, KD, S], F32R, 142)
    hL = at("hL", [P, KD, S], F32R, 174)
    qkT = at("qkT", [P, 8, S], F32, 34)
    vT = at("vT", [P, 4, S], F32, 66)
    lowT = at("lowT", [P, 6, S], F32, 82)
    ada1 = at("ada1", [P, KD, 2 * D], F32, 34)
    acc1 = at("acc1", [P, 2 * D], F32, 98)
    x_in = at("x_in", [P, KD, S], F32, 106)
    sq = [at(f"sq{s}", [P, S], F32, 198 + 4 * s) for s in range(2)]
    diag1 = at("diag1", [P, NT, P], F32, 34)
    xn = [at(f"xn{s}", [P, S], F32, 38 + 4 * s) for s in range(2)]
    ang = at("ang", [P, NT, 2, HALF], F32, 190)
    turns = at("turns", [P, NT, 2, HALF], F32, 192)
    ada2 = at("ada2", [P, 4 * D], F32, 106)
    acc2 = at("acc2", [P, 4 * D], F32, 122)
    sql = [at(f"sql{s}", [P, S], F32, 66 + 4 * s) for s in range(2)]
    diagl = at("diagl", [P, 2, NT, P], F32, 74)
    UQH = at("UQH", [P, 3, MH * QK], F32R, 106)
    UQL = at("UQL", [P, 3, MH * QK], F32R, 115)
    UKH = at("UKH", [P, 2, D], F32R, 124)
    UKL = at("UKL", [P, 2, D], F32R, 132)
    LH = [at(f"LH{s}", [P, 5, P], F32R, 10 + 2.5 * s) for s in range(2)]
    LL = [at(f"LL{s}", [P, 5, P], F32R, 15 + 2.5 * s) for s in range(2)]
    work = [at(f"work{s}", [P, 1408], F32, 20 + 5.5 * s) for s in range(2)]
    rot = [at("rot0", [P, 6, ROPE], F32, 140), at("rot1", [P, 6, ROPE], F32, 206)]
    rope_c = at("rope_c", [P, 5, 2, HALF], F32, 31)
    rope_s = at("rope_s", [P, 5, 2, HALF], F32, 32.25)
    QN = at("QN", [P, MH, S], F32, 142)
    KN = at("KN", [P, MH, S], F32, 158)
    VM = at("VM", [P, NT, MH * VD], F32, 174)
    QRK = at("QRK", [P, 3, S], F32, 190)
    VS = at("VS", [P, NT, SBH * SBD], F32, 82)
    pm = [at(f"pm{s}", [P, S], F32, 10 + 4 * s) for s in range(2)]
    pmT = [at(f"pmT{s}", [P, S], F32, 18 + 4 * s) for s in range(2)]
    KRH = [at("KRH0", [P, S], F32R, 26), at("KRH1", [P, S], F32R, 98)]
    KRL = [at("KRL0", [P, S], F32R, 30), at("KRL1", [P, S], F32R, 102)]
    mqH = [at(f"mqH{e}", [P, S], F32R, 106 + 16 * e) for e in range(2)]
    mqL = [at(f"mqL{e}", [P, S], F32R, 110 + 16 * e) for e in range(2)]
    mkH = [at(f"mkH{e}", [P, S], F32R, 114 + 16 * e) for e in range(2)]
    mkL = [at(f"mkL{e}", [P, S], F32R, 118 + 16 * e) for e in range(2)]
    mrH = at("mrH", [P, S], F32R, 138)
    mrL = at("mrL", [P, S], F32R, 202)
    o_mla = at("o_mla", [P, NT, MH * VD], F32, 66)
    skH = [at(f"skH{e}", [P, S], F32R, 106 + 8 * e) for e in range(2)]
    skL = [at(f"skL{e}", [P, S], F32R, 110 + 8 * e) for e in range(2)]
    sqH = at("sqH", [P, S], F32R, 122)
    sqL = at("sqL", [P, S], F32R, 126)
    beta = [at(f"beta{s}", [P, S], F32, 142 + 4 * s) for s in range(2)]
    omb = [at(f"omb{s}", [P, S], F32, 150 + 4 * s) for s in range(2)]
    left = [at(f"left{s}", [P, S + 8], F32, 158 + 4.5 * s) for s in range(2)]
    wT = [at(f"wT{s}", [P, S], F32, 167 + 4 * s) for s in range(2)]
    grow = at("grow", [P, 2, 512], F32, 176)
    o_sb = at("o_sb", [P, NT, SBH * SBD], F32, 190)
    mixH = at("mixH", [P, KD, S], F32R, 82)
    mixL = at("mixL", [P, KD, S], F32R, 114)
    junk = at("junk", [P, 512], F32, 146)
    ostage = [at(f"ostage{s}", [P, 2, 512], F32, 148 + 4 * s) for s in range(2)]
    x2 = at("x2", [P, KD, S], F32, 34)
    sq2 = [at(f"sq2{s}", [P, S], F32, 66 + 4 * s) for s in range(2)]
    sqa = at("sqa", [P, S], F32, 74)
    diag2 = at("diag2", [P, NT, P], F32, 78)
    xn2 = [at(f"xn2{s}", [P, S], F32, 82 + 4 * s) for s in range(2)]
    h2H = at("h2H", [P, KD, S], F32R, 142)
    h2L = at("h2L", [P, KD, S], F32R, 174)
    t_all = at("t_all", [P, NF, S], F32, 34)
    gs = [at(f"gs{s}", [P, S], F32, 122 + 4 * s) for s in range(2)]
    TH = [at(f"TH{s}", [P, 512], F32R, 130 + 2 * s) for s in range(2)]
    TL = [at(f"TL{s}", [P, 512], F32R, 134 + 2 * s) for s in range(2)]
    xres = at("xres", [P, KD, 512], F32, 142)
    yst = at("yst", [P, KD, 512], F32, 158)

    ps = ctx.enter_context(nc.psum_tensor("ps", [P, 8, 512], F32))

    def pair(b, n=S):
        return ps[:, b:b + 2, :].rearrange("p b n -> p (b n)")[:, 0:n]

    names = """small_in pool_const trig_args trig_done silu_c_done x_sq x_sqmm stat_ms stat_r stat_diag stat_bc acc1_done mod1_mm r1_done
        xn_done hH_done hL_done split_h split_l pe_tile in_evac ada2_in ada_acc mod2_mm low_sq low_mm low_done
        up_h up_l dve lh_done ll_done q_mm kv_mm q_sq k_sq q_ms q_r k_ms q_free kr_free rk_done kv_free work_done tr_done
        t_act t_dve vt_mm vt_even vt_odd low_over kr_zero kr_h kr_l
        m_h m_l m_qk m_max m_nm m_exp m_tr m_ta m_tv m_av m_o
        sk_zero s_h s_l s_qk s_nb s_b s_scan s_wd s_wp s_tr s_ta s_tv s_av s_o
        grow_in o_sq o_ms o_r o_scaled o_mm mix_h mix_l x2_in sqa_zero sqa_done x2_done x2_sq x2_spill r2_mm xn2_done h2H_done
        h2L_done silu_done t_done th_done tl_done d_mm xres_in y_done y_out""".split()
    sem = {n: ctx.enter_context(nc.semaphore(n)) for n in names}
    ada1_in = [ctx.enter_context(nc.semaphore(f"ada1_in{k}")) for k in range(4)]
    xin_in = [ctx.enter_context(nc.semaphore(f"xin_in{k}")) for k in range(4)]
    raw_in = [ctx.enter_context(nc.semaphore(f"raw_in{k}")) for k in range(2)]

    block = ctx.enter_context(nc.Block())

    def after(n):
        return n + 1 + PRIME

    def one(ap):
        return ap.rearrange("p o n -> p (o n)")

    def mix_banks(tt):
        b = 2 * (tt % 2)
        return ps[:, b:b + 2, :].rearrange("p b (j n) -> p (b j) n", j=4)

    SEGMENTS = [(0, 3), (6, 1), (8, 1), (10, 2), (14, 1), (16, 1)]

    def repeat(eng, n, body):
        if n == 1:
            body(0)
        else:
            with eng.Fori(0, n) as i:
                body(i)

    @block.sync
    def _(sp):
        def load_raw(r, par, i, src):
            if not (isinstance(r, int) and r < 2):
                sp.wait_ge(sem["split_h"], r - 1)
                sp.wait_ge(sem["split_l"], r - 1)
            sp.dma_start(raw[par % 2][:, 0:src.shape[-1]], src).then_inc(raw_in[par % 2], 16)

        sp.dma_start(cols[:], cols_d).then_inc(sem["small_in"], 16)
        sp.dma_start(rows[:], rows_d).then_inc(sem["small_in"], 16)
        sp.dma_start(pos_i[:], pos_d).then_inc(sem["small_in"], 16)
        for k in range(4):
            sp.dma_start(ada1[:, 2 * k:2 * k + 2, :], ada1_d[2 * k:2 * k + 2].rearrange("j p n -> p j n")).then_inc(ada1_in[k], 16)
            sp.dma_start(x_in[:, 2 * k:2 * k + 2, :], xT[2 * k:2 * k + 2].rearrange("j p n -> p j n")).then_inc(xin_in[k], 16)
        for h in range(2):
            load_raw(h, h, 0, win_d[h])
        step = 0
        for t0, n in SEGMENTS[:-1]:
            def body(i, t0=t0, step=step):
                for u in range(2):
                    load_raw(t0 + 2 + 2 * i + u, t0 + u, i, one(win_d[bass.ds(t0 + 2 + 2 * i + u, 1)].rearrange("o p n -> p o n")))
                sp.wait_ge(sem["ada_acc"], step + i + 1)
                sp.dma_start(ada2[:], one(ada2_d[bass.ds(step + i, 1)].rearrange("o p n -> p o n"))).then_inc(sem["ada2_in"], 16)
            repeat(sp, n, body)
            step += n
        for k in range(3):
            load_raw(N_IN + k, N_IN + k, 0, qup_d[k])
        for k in range(2):
            load_raw(N_IN + 3 + k, N_IN + 3 + k, 0, kvup_d[k])
        sp.wait_ge(sem["m_av"], after(2 * NU - 1))
        sp.dma_start(grow[:], grow_d).then_inc(sem["grow_in"], 16)
        for u in range(2):
            load_raw(raw_index(H_OUT) + u, raw_index(H_OUT) + u, 0, wout_d[u])
        sp.wait_ge(sem["s_h"], 3 * 4)
        sp.wait_ge(sem["s_l"], 3 * 4)
        sp.dma_start(x2[:], xT.rearrange("j p n -> p j n")).then_inc(sem["x2_in"], 16)
        with sp.Fori(0, N_OUT // 2 - 1) as i:
            for u in range(2):
                r = raw_index(H_OUT) + 2 + u
                load_raw(r + 2 * i, r, i, one(wout_d[bass.ds(2 + u + 2 * i, 1)].rearrange("o p n -> p o n")))
        for u in range(2):
            r = raw_index(H_GU) + u
            load_raw(r, r, 0, gu_d[u])
        sp.wait_ge(sem["x2_done"], after(N_OUT - 1))
        sp.dma_start(x2_d.rearrange("j p n -> p j n"), x2[:]).then_inc(sem["x2_spill"], 16)
        with sp.Fori(0, NF - 1) as i:
            for u in range(2):
                r = raw_index(H_GU) + 2 + u
                load_raw(r + 2 * i, r, i, one(gu_d[bass.ds(2 + u + 2 * i, 1)].rearrange("o p n -> p o n")))
        for hf in range(2):
            with sp.Fori(0, NF // 2) as i:
                for u in range(2):
                    r = raw_index(H_DN) + hf * NF + u
                    load_raw(r + 2 * i, r, i, one(down_d[bass.ds(u + 2 * i, 1)].rearrange("o p n -> p o n")))

    @block.gpsimd
    def _(pool):
        for n in ("s_wp", "q_r", "rk_done"):
            pool.sem_inc(sem[n], PRIME)
        k = 0

        def fill(ins):
            nonlocal k
            ins.then_inc(sem["pool_const"], 1)
            k += 1

        fill(pool.memset(ident[:], 0.0))
        fill(pool.memset(identb[:], 0.0))
        fill(pool.memset(mask_sb[:], 0.0))
        fill(pool.memset(mask_mla[:], 0.0))
        fill(pool.memset(ones[:], 1.0))
        fill(pool.memset(nhalf[:], -0.5))
        pool.wait_ge(sem["pool_const"], k)
        for m in (ident, identb):
            fill(pool.affine_select(out=m[:], in_=m[:], compare_op=ALU.not_equal, fill=1.0, base=0, pattern=[[-1, P]], channel_multiplier=1))
        fill(pool.affine_select(out=mask_sb[:], in_=mask_sb[:], compare_op=ALU.is_gt, fill=NEG, base=0, pattern=[[1, P]], channel_multiplier=-1))
        fill(pool.affine_select(out=mask_mla[:], in_=mask_mla[:], compare_op=ALU.is_ge, fill=NEG, base=0, pattern=[[1, P]], channel_multiplier=-1))

        def rsqrt(k):
            pool.wait_ge(sem["stat_ms"], k + 1)
            nc.gpsimd.tensor_tensor(rms[:, k, :], ms[:, k, :], nhalf[:, 0:NT], ALU.pow).then_inc(sem["stat_r"], 1)

        pool.wait_ge(sem["pool_const"], k)
        rsqrt(0)
        pool.wait_ge(sem["xn_done"], KD)
        pool.memset(acc2[:], 0.0).then_inc(sem["ada_acc"], 1)
        rsqrt(1)
        rsqrt(2)

        def head_rsqrt(i):
            for u in range(2):
                tt = 2 * i + u
                pool.wait_ge(sem["q_ms"], tt + 1)
                nc.gpsimd.tensor_tensor(rstd[:, u, 0:4], qms[:, u, 0:4], nhalf[:, 0:4], ALU.pow).then_inc(sem["q_r"], 1)
                pool.wait_ge(sem["k_ms"], tt + 1)
                nc.gpsimd.tensor_tensor(rstd[:, u, 4:9], qms[:, u, 4:9], nhalf[:, 0:5], ALU.pow).then_inc(sem["rk_done"], 1)
        repeat(pool, NT // 2, head_rsqrt)
        pool.wait_ge(sem["low_over"], 1)
        for e in range(2):
            o = 64 * (1 - e)
            pool.memset(KRH[e][o:o + 64, :].bitcast(F32), 0.0).then_inc(sem["kr_zero"], 1)
            pool.memset(KRL[e][o:o + 64, :].bitcast(F32), 0.0).then_inc(sem["kr_zero"], 1)
        pool.wait_ge(sem["m_o"], after(2 * NU - 1))
        for e in range(2):
            o = 64 * (1 - e)
            pool.memset(skH[e][o:o + 64, :].bitcast(F32), 0.0).then_inc(sem["sk_zero"], 1)
            pool.memset(skL[e][o:o + 64, :].bitcast(F32), 0.0).then_inc(sem["sk_zero"], 1)
        pool.wait_ge(sem["sk_zero"], 4)
        for s in range(2):
            pool.memset(left[s][:, 0:1], 1.0).then_inc(sem["sk_zero"], 1)
        pool.wait_ge(sem["sk_zero"], 6)

        def weights(i):
            for v, b in enumerate(BLOCKS):
                n, u = b * P, i * NU + v
                pool.wait_ge(sem["s_scan"], after(u))
                pool.wait_ge(sem["s_b"], after(u))
                nc.gpsimd.tensor_tensor(beta[v % 2][:, n // 2:n], beta[v % 2][:, n // 2:n], left[v % 2][:, n // 2:n], ALU.mult).then_inc(sem["s_wp"], 1)
        repeat(pool, 4, weights)
        for tt in range(NT):
            pool.wait_ge(sem["o_ms"], tt + 1)
            nc.gpsimd.tensor_tensor(ors[:, tt % 2, :], oms[:, tt % 2, :], nhalf[:, 0:2], ALU.pow).then_inc(sem["o_r"], 1)
        pool.wait_ge(sem["mix_l"], NT)
        pool.memset(sqa[:], 0.0).then_inc(sem["sqa_zero"], 1)
        rsqrt(3)
        for hf in range(2):
            if hf == 0:
                pool.wait_ge(sem["pe_tile"], after(H_DN - 1))
                pool.wait_ge(sem["x2_spill"], 16)
            else:
                pool.wait_ge(sem["y_done"], KD)
            pool.dma_start(xres[:], x2_d[:, :, 512 * hf:512 * hf + 512].rearrange("j p n -> p j n")).then_inc(sem["xres_in"], 16)
            for o in range(KD):
                pool.wait_ge(sem["y_done"], hf * KD + o + 1)
                pool.dma_start(out_d[o, :, 512 * hf:512 * hf + 512], yst[:, o, :]).then_inc(sem["y_out"], 16)
            pool.wait_ge(sem["y_out"], 16 * KD * (hf + 1))

    @block.scalar
    def _(act):
        for n in ("in_evac", "lh_done", "q_sq", "k_sq", "kv_free", "t_act", "m_exp", "m_ta", "s_nb", "s_b", "s_ta", "silu_done"):
            act.sem_inc(sem[n], PRIME)
        A = nc.scalar.activation

        def split(h, par, i):
            r = raw_index(par)
            act.wait_ge(raw_in[r % 2], 16 * (r // 2 + 1) + 16 * i)
            act.wait_ge(sem["pe_tile"], after(h - 2))
            A(WH[par % 2][:], raw[r % 2][:], ACT.Copy).then_inc(sem["split_h"], 1)

        act.wait_ge(sem["small_in"], 48)
        A(silu_c[:], cols[:, C_C:C_C + KD], ACT.Silu).then_inc(sem["silu_c_done"], 1)
        act.wait_ge(sem["trig_args"], 1)
        A(trig[:], ang[:], ACT.Sin).then_inc(sem["trig_done"], 1)
        for j in range(KD):
            act.wait_ge(xin_in[j // 2], 16)
            if j >= 2:
                act.wait_ge(sem["x_sqmm"], j - 1)
            if j == 0:
                act.wait_ge(sem["trig_done"], 1)
            A(sq[j % 2][:], x_in[:, j, :], ACT.Square).then_inc(sem["x_sq"], 1)
        split(0, 0, 0)
        for j in range(KD):
            act.wait_ge(sem["xn_done"], j + 1)
            act.wait_ge(sem["r1_done"], 1)
            A(hH[:, j, :], xn[j % 2][:], ACT.Identity, bias=mod1[:, j:j + 1]).then_inc(sem["hH_done"], 1)

        def in_tile(t, par, i, dst, last=False):
            if not last:
                split(t + 1, par + 1, i)
            act.wait_ge(sem["pe_tile"], after(t))
            A(dst, pair(2 * (par % 2)), ACT.Copy).then_inc(sem["in_evac"], 1)

        def in_pair(t0, i):
            for u in range(2):
                t = t0 + 2 * i + u
                if t0 == 0:
                    dst = one(lowT[:, bass.ds(2 * i + u, 1), :])
                elif t0 < 14:
                    dst = one(qkT[:, bass.ds(t0 - 6 + 2 * i + u, 1), :])
                else:
                    dst = vT[:, t0 - 14 + u, :]
                in_tile(t, t0 + u, i, dst)

        repeat(act, 3, lambda i: in_pair(0, i))
        in_pair(6, 0)
        for k in range(5):
            if k >= 2:
                act.wait_ge(sem["low_mm"], k - 1)
            A(sql[k % 2][:], lowT[:, k, :], ACT.Square).then_inc(sem["low_sq"], 1)
        in_pair(8, 0)
        repeat(act, 2, lambda i: in_pair(10, i))
        act.wait_ge(sem["low_done"], 5)
        in_pair(14, 0)
        split(17, 17, 0)
        act.wait_ge(sem["mod2_mm"], 1)
        for k in range(N_UP):
            r = N_IN + k
            act.wait_ge(raw_in[r % 2], 16 * (r // 2 + 1))
            dst, src = (UQH[:, k, :], raw[r % 2][:, 0:MH * QK]) if k < 3 else (UKH[:, k - 3, :], raw[r % 2][:])
            A(dst, src, ACT.Copy).then_inc(sem["split_h"], 1)
        in_tile(16, 16, 0, vT[:, 2, :], last=True)
        in_tile(17, 17, 0, vT[:, 3, :], last=True)

        def low_split(tt, s):
            act.wait_ge(sem["kv_mm"], after(tt - 2))
            A(LH[s][:], lowT[:, 0:5, bass.ds(tt * P, P)], ACT.Copy).then_inc(sem["lh_done"], 1)

        def turn_out(tt):
            act.wait_ge(sem["tr_done"], after(tt))
            A(QN[:, :, bass.ds(tt * P, P)], ps[:, 4, :].rearrange("p (h n) -> p h n", h=MH), ACT.Copy).then_inc(sem["t_act"], 1)
            A(QRK[:, :, bass.ds(tt * P, P)], ps[:, 6, 0:3 * P].rearrange("p (h n) -> p h n", h=3), ACT.Copy).then_inc(sem["t_act"], 1)

        def up_tile(tt, s, first=False, last=False):
            act.wait_ge(sem["q_mm"], after(tt))
            act.wait_ge(sem["tr_done"], after(tt - 2))
            A(work[s][:, 0:MH * QK].rearrange("p (b n) -> p b n", b=2), ps[:, 0:2, 0:384], ACT.Square).then_inc(sem["q_sq"], 1)
            if not last:
                low_split(tt + 1, 1 - s)
            act.wait_ge(sem["kv_mm"], after(tt))
            kv = ps[:, 2:4, :].rearrange("p b (h c n) -> p (b h) c n", h=2, c=2)
            A(work[s][:, 768:1280].rearrange("p (h n) -> p h n", h=MH), kv[:, :, 0, :], ACT.Square).then_inc(sem["k_sq"], 1)
            A(work[s][:, 1280:1344], ps[:, 7, 64:128], ACT.Square).then_inc(sem["k_sq"], 1)
            A(one3(VM[:, bass.ds(tt, 1), :]), kv[:, :, 1, :], ACT.Copy).then_inc(sem["kv_free"], 1)
            act.wait_ge(sem["rk_done"], after(tt))
            for h in range(MH):
                o = 768 if h == 0 else 896 + 128 * h
                A(work[s][:, o:o + P], kv[:, h, 0, :], ACT.Copy, scale=rstd[:, s, 4 + h:5 + h]).then_inc(sem["kv_free"], 1)
            if not first:
                turn_out(tt - 1)

        def one3(ap):
            return ap.rearrange("p o (h n) -> p (o h) n", h=MH)

        act.wait_ge(sem["pe_tile"], after(N_IN - 1))
        act.wait_ge(sem["split_l"], N_IN + N_UP)
        low_split(0, 0)
        up_tile(0, 0, first=True)

        def up_pair(i):
            for u in range(2):
                up_tile(1 + 2 * i + u, (1 + u) % 2)
        repeat(act, 3, up_pair)
        up_tile(NT - 1, 1, last=True)
        turn_out(NT - 1)
        for tt in range(0, NT, 2):
            act.wait_ge(sem["vt_mm"], tt + 1)
            A(VS[:, tt, :], ps[:, 0, :], ACT.Copy).then_inc(sem["vt_even"], 1)
        act.wait_ge(sem["vt_even"], NT // 2)
        act.wait_ge(sem["vt_odd"], NT // 2)
        act.wait_ge(sem["t_act"], 2 * NT + PRIME)
        act.wait_ge(sem["t_dve"], after(NT - 1))
        act.sem_inc(sem["low_over"], 1)

        for e in range(2):
            o = 64 * e
            A(KRH[e][o:o + 64, :], QRK[o:o + 64, 2, :], ACT.Copy).then_inc(sem["kr_h"], 1)

        def copy_out(pre, u, v, dst, b0=4):
            act.wait_ge(sem[pre + "_tr"], after(u))
            act.wait_ge(sem[pre + "_av"], after(u - 2))
            n = G0[v] * P
            A(dst[v % 2][:, 0:n], ps[:, b0, 0:n], ACT.Copy).then_inc(sem[pre + "_ta"], 1)

        def mla(i):
            act.wait_ge(sem["m_qk"], i * NU + PRIME)
            A(mrH[:], one(QRK[:, bass.ds(i, 1), :]), ACT.Copy).then_inc(sem["m_h"], 1)
            for e in range(2):
                A(mqH[e][:], one(QN[:, bass.ds(2 * i + e, 1), :]), ACT.Copy).then_inc(sem["m_h"], 1)
                A(mkH[e][:], one(KN[:, bass.ds(2 * i + e, 1), :]), ACT.Copy).then_inc(sem["m_h"], 1)
            for v in range(NU + 2):
                if v >= 2:
                    copy_out("m", i * NU + v - 2, v - 2, pmT)
                if v < NU:
                    u, n = i * NU + v, BLOCKS[v] * P
                    act.wait_ge(sem["m_nm"], after(u))
                    act.wait_ge(sem["m_tr"], after(u - 2))
                    A(pm[v % 2][:, 0:n], pair(2 * (v % 2), n), ACT.Exp, bias=nmx[:, v:v + 1], scale=QK ** -0.5,
                      accum_out=den[:, v:v + 1]).then_inc(sem["m_exp"], 1)
        repeat(act, MH // 2, mla)

        act.wait_ge(sem["m_o"], after(2 * NU - 1))

        def stick(i):
            act.wait_ge(sem["s_qk"], i * NU + PRIME)
            A(sqH[:], one(qkT[:, bass.ds(i, 1), :]), ACT.Copy).then_inc(sem["s_h"], 1)
            for e in range(2):
                o = 64 * e
                A(skH[e][o:o + 64, :], one(qkT[o:o + 64, bass.ds(4 + i, 1), :]), ACT.Copy).then_inc(sem["s_h"], 1)
            for v in range(NU + 2):
                if v >= 2:
                    copy_out("s", i * NU + v - 2, v - 2, wT)
                if v < NU:
                    u, n = i * NU + v, BLOCKS[v] * P
                    act.wait_ge(sem["s_qk"], after(u))
                    act.wait_ge(sem["s_scan"], after(u - 2))
                    A(omb[v % 2][:, 0:n], pair(2 * (v % 2), n), ACT.Sigmoid, scale=-(SBD ** -0.5)).then_inc(sem["s_nb"], 1)
                    act.wait_ge(sem["s_tr"], after(u - 2))
                    A(beta[v % 2][:, 0:n], pair(2 * (v % 2), n), ACT.Sigmoid, scale=SBD ** -0.5).then_inc(sem["s_b"], 1)
        repeat(act, 4, stick)

        act.wait_ge(sem["s_o"], after(4 * NU - 1))
        split(H_OUT, H_OUT, 0)
        for tt in range(NT + 1):
            if tt < NT:
                if tt >= 2:
                    act.wait_ge(sem["o_mm"], tt - 1)
                for g, o in ((0, o_sb), (1, o_mla)):
                    if tt or g:
                        act.wait_ge(sem["o_sq"], 2 * tt + g)
                    A(junk[:], o[:, tt, :], ACT.Square, accum_out=oss[:, tt % 2, g:g + 1]).then_inc(sem["o_sq"], 1)
            if tt >= 1:
                k = tt - 1
                act.wait_ge(sem["o_mm"], k + 1)
                A(mixH[:, :, k * P:(k + 1) * P], mix_banks(k), ACT.Copy).then_inc(sem["mix_h"], 1)

        def out_pair(i, last=False):
            for u in range(2):
                t = 2 * i + u
                split(H_OUT + t + 1, H_OUT + u + 1, i)
                act.wait_ge(sem["x2_done"], after(t))
                A(sq2[u][:], one(x2[:, bass.ds(t, 1), :]), ACT.Square).then_inc(sem["x2_sq"], 1)
        act.wait_ge(sem["mix_l"], NT)
        repeat(act, N_OUT // 2, out_pair)

        for j in range(KD):
            act.wait_ge(sem["xn2_done"], j + 1)
            A(h2H[:, j, :], xn2[j % 2][:], ACT.Identity, bias=mod2[:, 8 + j:9 + j]).then_inc(sem["h2H_done"], 1)

        def gate(i):
            for u in range(2):
                split(H_GU + 2 * i + u + 1, H_GU + u + 1, i)
                if u == 0:
                    act.wait_ge(sem["pe_tile"], after(H_GU + 2 * i))
                    act.wait_ge(sem["t_done"], after(i - 1))
                    A(gs[0][:], pair(0), ACT.Silu).then_inc(sem["silu_done"], 1)
        repeat(act, NF, gate)

        def t_split(d, f, hf, s):
            act.wait_ge(sem["pe_tile"], after(H_DN + d - 2))
            A(TH[s][:], one(t_all[:, bass.ds(f, 1), 512 * hf:512 * hf + 512]), ACT.Copy).then_inc(sem["th_done"], 1)

        act.wait_ge(sem["t_done"], after(NF - 1))
        for hf in range(2):
            def down(i, hf=hf):
                for u in range(2):
                    d = hf * NF + 2 * i + u
                    t_split(d, 2 * i + u, hf, u)
                    split(H_DN + d + 1, H_DN + hf * NF + u + 1, i)
            if hf == 0:
                repeat(act, NF // 2, down)
            else:
                repeat(act, NF // 2 - 1, down)
                d = 2 * NF - 2
                t_split(d, NF - 2, 1, 0)
                split(H_DN + d + 1, H_DN + d + 1, 0)
                t_split(d + 1, NF - 1, 1, 1)

    @block.vector
    def _(dve):
        for n in ("q_free", "kr_free", "work_done", "t_dve", "m_max", "m_nm", "m_tv", "m_o", "s_scan", "s_wd", "s_tv", "s_o", "t_done", "ll_done", "x2_done", "sqa_done"):
            dve.sem_inc(sem[n], PRIME)
        V = nc.vector
        ch = Chain(dve, sem["dve"])

        dve.wait_ge(sem["small_in"], 48)
        ch(V.tensor_copy(pos_f[:], pos_i[:]))
        ch.sync()
        fr = rows[:, R_FREQ:R_FREQ + HALF]
        for tt in range(NT):
            ch(V.tensor_scalar(ang[:, tt, 0, :], fr, pos_f[:, tt:tt + 1], None, ALU.mult))
            ch(V.tensor_scalar(ang[:, tt, 1, :], fr, pos_f[:, tt:tt + 1], None, ALU.mult))
        ch.sync()
        for c, off in ((0, 0.25), (1, 0.0)):
            ch(V.tensor_scalar(turns[:, :, c, :], ang[:, :, c, :], float(np.float32(1 / (2 * np.pi))), off, ALU.mult, ALU.add))
        ch.sync()
        magic = 1.5 * 2.0 ** 23
        ch(V.tensor_scalar(turns[:], turns[:], magic, None, ALU.add))
        ch.sync()
        ch(V.tensor_scalar(turns[:], turns[:], magic, None, ALU.subtract))
        ch.sync()
        c1 = 6.28125
        c2 = float(np.float32(round((2 * np.pi - c1) * 2 ** 20) / 2 ** 20))
        c3 = float(np.float32(2 * np.pi - c1 - c2))
        for c in (c1, c2, c3):
            ch(V.scalar_tensor_tensor(ang[:], turns[:], -c, ang[:], ALU.mult, ALU.add))
            ch.sync()
        ch(V.tensor_scalar(ang[:, :, 0, :], ang[:, :, 0, :], float(np.pi / 2), None, ALU.add))
        ch.sync()
        V.tensor_scalar(ang[:], ang[:], 3.1415925, -3.1415925, ALU.min, ALU.max).then_inc(sem["trig_args"], 1)

        dve.wait_ge(sem["silu_c_done"], 1)
        for j in range(KD):
            if j % 2 == 0:
                dve.wait_ge(ada1_in[j // 2], 16)
            if j == 0:
                ch(V.tensor_scalar(acc1[:], ada1[:, 0, :], silu_c[:, 0:1], None, ALU.mult))
            elif j < KD - 1:
                ch(V.scalar_tensor_tensor(acc1[:], ada1[:, j, :], silu_c[:, j:j + 1], acc1[:], ALU.mult, ALU.add))
            else:
                V.scalar_tensor_tensor(acc1[:], ada1[:, j, :], silu_c[:, j:j + 1], acc1[:], ALU.mult, ALU.add).then_inc(sem["acc1_done"], 1)
                dve.wait_ge(sem["acc1_done"], 1)
            ch.sync()

        def wsplit(h, par):
            r = raw_index(par)
            dve.wait_ge(sem["split_h"], h + (r - par) + 1)
            V.tensor_tensor(WL[par % 2][:], raw[r % 2][:], WH[par % 2][:], ALU.subtract).then_inc(sem["split_l"], 1)

        def mean_squares(k, bank, n):
            V.tensor_scalar(ms[:, k, :], ps[:, bank, 0:NT], 1.0 / n, EPS, ALU.mult, ALU.add).then_inc(sem["stat_ms"], 1)

        def diagonals(k, diag):
            dve.wait_ge(sem["stat_r"], k + 1)
            for tt in range(NT):
                ins = V.tensor_scalar(diag[:, tt, :], ident[:], rms[:, k, tt:tt + 1], None, ALU.mult)
            ins.then_inc(sem["stat_diag"], 1)

        dve.wait_ge(sem["x_sqmm"], KD)
        mean_squares(0, 4, D)
        diagonals(0, diag1)
        wsplit(0, 0)
        dve.wait_ge(sem["mod1_mm"], 1)
        ch(V.tensor_tensor(mod1[:], ps[:, 5, 0:16], cols[:, C_B:C_B + 16], ALU.add))
        ch.sync()
        V.scalar_tensor_tensor(a1[:], mod1[:, 8:16], 1.0, cols[:, C_GA:C_GA + KD], ALU.add, ALU.mult).then_inc(sem["r1_done"], 1)
        dve.wait_ge(sem["r1_done"], 1)

        def modulate(x, xns, a, r, shift, H, L, xn_s, hH_s, hL_s):
            for j in range(KD + 1):
                if j < KD:
                    if j >= 2:
                        dve.wait_ge(sem[hL_s], j - 1)
                    V.scalar_tensor_tensor(xns[j % 2][:], x[:, j, :], a[:, j:j + 1], r, ALU.mult, ALU.mult).then_inc(sem[xn_s], 1)
                if j >= 1:
                    k = j - 1
                    dve.wait_ge(sem[hH_s], k + 1)
                    V.scalar_tensor_tensor(L[:, k, :], xns[k % 2][:], shift[:, k:k + 1], H[:, k, :], ALU.add, ALU.subtract).then_inc(sem[hL_s], 1)

        dve.wait_ge(sem["stat_bc"], 1)
        modulate(x_in, xn, a1, pair(6), mod1, hH, hL, "xn_done", "hH_done", "hL_done")

        def in_pair(t0, i, step=None):
            for u in range(2):
                wsplit(t0 + 2 * i + u + 1, t0 + u + 1)
            if step is not None:
                dve.wait_ge(sem["ada2_in"], 16 * (step + 1))
                dve.wait_ge(sem["ada_acc"], step + 1)
                V.scalar_tensor_tensor(acc2[:], ada2[:], silu_c[:, bass.ds(step, 1)], acc2[:], ALU.mult, ALU.add).then_inc(sem["ada_acc"], 1)

        repeat(dve, 3, lambda i: in_pair(0, i, i))
        in_pair(6, 0, 3)
        dve.wait_ge(sem["low_mm"], 5)
        mean_squares(1, 6, QR_)
        mean_squares(2, 7, KVR)
        diagonals(1, diagl[:, 0])
        diagonals(2, diagl[:, 1])
        in_pair(8, 0, 4)
        for k in range(5):
            g = 0 if k < 3 else 1
            dve.wait_ge(sem["stat_bc"], 2 + g)
            V.scalar_tensor_tensor(lowT[:, k, :], lowT[:, k, :], cols[:, C_QA + k:C_QA + k + 1], pair(4 + 2 * g), ALU.mult, ALU.mult).then_inc(sem["low_done"], 1)
        repeat(dve, 2, lambda i: in_pair(10, i, 5 + i))
        in_pair(14, 0, 7)
        wsplit(17, 17)
        dve.wait_ge(sem["mod2_mm"], 1)
        ch(V.tensor_tensor(mod2[:], ps[:, 4, 0:32], cols[:, C_B + 16:C_B + 48], ALU.add))
        ch.sync()
        ch(V.scalar_tensor_tensor(a2[:], mod2[:, 16:24], 1.0, cols[:, C_GF:C_GF + KD], ALU.add, ALU.mult))
        for k in range(N_UP):
            r = N_IN + k
            dve.wait_ge(sem["split_h"], r + 1)
            if k < 3:
                V.tensor_tensor(UQL[:, k, :], raw[r % 2][:, 0:MH * QK], UQH[:, k, :], ALU.subtract).then_inc(sem["split_l"], 1)
            else:
                V.tensor_tensor(UKL[:, k - 3, :], raw[r % 2][:], UKH[:, k - 3, :], ALU.subtract).then_inc(sem["split_l"], 1)

        def low_split(tt, s):
            dve.wait_ge(sem["lh_done"], after(tt))
            V.tensor_tensor(LL[s][:], lowT[:, 0:5, bass.ds(tt * P, P)], LH[s][:], ALU.subtract).then_inc(sem["ll_done"], 1)

        def turn_out(tt):
            dve.wait_ge(sem["tr_done"], after(tt))
            V.tensor_scalar(KN[:, :, bass.ds(tt * P, P)], ps[:, 5, :].rearrange("p (h n) -> p h n", h=MH), cols[:, C_KN:C_KN + 1], None, ALU.mult).then_inc(sem["t_dve"], 1)

        def up_tile(tt, s, first=False, last=False):
            w = work[s]
            dve.wait_ge(sem["q_sq"], after(tt))
            ch(V.reduce_sum(ssq[:, s, 0:4], w[:, 0:MH * QK].rearrange("p (h n) -> p h n", h=MH), axis=AX.X))
            ch.sync()
            V.tensor_scalar(qms[:, s, 0:4], ssq[:, s, 0:4], 1.0 / QK, EPS, ALU.mult, ALU.add).then_inc(sem["q_ms"], 1)
            dve.wait_ge(sem["q_r"], after(tt))
            for h in range(MH):
                o = QK * (h % 2)
                V.scalar_tensor_tensor(w[:, QK * h:QK * (h + 1)], ps[:, h // 2, o:o + QK], rstd[:, s, h:h + 1], rows[:, R_Q:R_Q + QK],
                                       ALU.mult, ALU.mult).then_inc(sem["q_free"], 1)
            if not last:
                low_split(tt + 1, 1 - s)
            dve.wait_ge(sem["k_sq"], 2 * tt + 2 + PRIME)
            ch(V.reduce_sum(ssq[:, s, 4:8], w[:, 768:1280].rearrange("p (h n) -> p h n", h=MH), axis=AX.X))
            ch(V.reduce_sum(ssq[:, s, 8:9], w[:, 1280:1344], axis=AX.X))
            ch.sync()
            V.tensor_scalar(qms[:, s, 4:8], ssq[:, s, 4:8], 1.0 / NOPE, EPS, ALU.mult, ALU.add)
            V.tensor_scalar(qms[:, s, 8:9], ssq[:, s, 8:9], 1.0 / ROPE, EPS, ALU.mult, ALU.add).then_inc(sem["k_ms"], 1)
            dve.wait_ge(sem["rk_done"], after(tt))
            V.scalar_tensor_tensor(w[:, 896:960], ps[:, 7, 64:128], rstd[:, s, 8:9], rows[:, R_KR:R_KR + ROPE], ALU.mult, ALU.mult).then_inc(sem["kr_free"], 1)
            dve.wait_ge(sem["kr_free"], after(tt))
            dve.wait_ge(sem["q_free"], 4 * tt + 4 + PRIME)
            x = w[:, 0:5 * QK].rearrange("p (h n) -> p h n", h=5)[:, :, NOPE:QK].rearrange("p h (c n) -> p h c n", c=2)
            for c, dst in ((0, rope_c), (1, rope_s)):
                for hv in range(2):
                    tab = one(trig[:, bass.ds(tt, 1), c, :]).unsqueeze(1).broadcast_to([P, 5, HALF])
                    ch(V.tensor_tensor(dst[:, :, hv, :], x[:, :, hv, :], tab, ALU.mult))
            ch.sync()
            ch(V.tensor_tensor(rot[s][:, 0:5, 0:HALF], rope_c[:, :, 0, :], rope_s[:, :, 1, :], ALU.subtract))
            ch(V.tensor_tensor(rot[s][:, 0:5, HALF:ROPE], rope_c[:, :, 1, :], rope_s[:, :, 0, :], ALU.add))
            ch.sync()
            V.tensor_copy(rot[s][:, 5, :], rot[s][:, 4, :]).then_inc(sem["work_done"], 1)
            if not first:
                turn_out(tt - 1)

        dve.wait_ge(sem["pe_tile"], after(N_IN - 1))
        low_split(0, 0)
        up_tile(0, 0, first=True)

        def up_pair(i):
            for u in range(2):
                up_tile(1 + 2 * i + u, (1 + u) % 2)

        UPC = 9
        with dve.Fori(0, 3) as i:
            ch.begin(i, 2 * UPC)
            up_pair(i)
        ch.end(3, 2 * UPC)
        up_tile(NT - 1, 1, last=True)
        turn_out(NT - 1)
        for tt in range(1, NT, 2):
            dve.wait_ge(sem["vt_mm"], tt + 1)
            V.tensor_copy(VS[:, tt, :], ps[:, 1, :]).then_inc(sem["vt_odd"], 1)

        for e in range(2):
            o = 64 * e
            dve.wait_ge(sem["kr_h"], e + 1)
            V.tensor_tensor(KRL[e][o:o + 64, :], QRK[o:o + 64, 2, :], KRH[e][o:o + 64, :], ALU.subtract).then_inc(sem["kr_l"], 1)

        def copy_out(pre, i, v, dst, b=5):
            if BLOCKS[v] > 1:
                dve.wait_ge(sem[pre + "_tr"], after(i * NU + v))
                dve.wait_ge(sem[pre + "_av"], after(i * NU + v - 2))
                n0, n = G0[v] * P, BLOCKS[v] * P
                V.tensor_copy(dst[v % 2][:, n0:n], ps[:, b, 0:n - n0]).then_inc(sem[pre + "_tv"], 1)

        def mla(i):
            dve.wait_ge(sem["m_h"], 5 * i + 1)
            V.tensor_tensor(mrL[:], one(QRK[:, bass.ds(i, 1), :]), mrH[:], ALU.subtract).then_inc(sem["m_l"], 1)
            for e in range(2):
                dve.wait_ge(sem["m_h"], 5 * i + 2 + 2 * e)
                V.tensor_tensor(mqL[e][:], one(QN[:, bass.ds(2 * i + e, 1), :]), mqH[e][:], ALU.subtract).then_inc(sem["m_l"], 1)
                dve.wait_ge(sem["m_h"], 5 * i + 3 + 2 * e)
                V.tensor_tensor(mkL[e][:], one(KN[:, bass.ds(2 * i + e, 1), :]), mkH[e][:], ALU.subtract).then_inc(sem["m_l"], 1)
            for v in range(NU + 3):
                if v >= 3:
                    k = v - 3
                    e, qt = UNITS[k]
                    u = i * NU + k
                    dve.wait_ge(sem["m_av"], after(u))
                    V.reciprocal(rden[:, k:k + 1], den[:, k:k + 1]).then_inc(sem["m_max"], 1)
                    dve.wait_ge(sem["m_max"], MAXC(i, v, k + 1))
                    V.tensor_scalar(o_mla[:, qt, bass.ds((2 * i + e) * VD, VD)], ps[:, 6 + k % 2, 0:VD], rden[:, k:k + 1], None, ALU.mult).then_inc(sem["m_o"], 1)
                if 2 <= v < NU + 2:
                    copy_out("m", i, v - 2, pmT)
                if v < NU:
                    u, n = i * NU + v, BLOCKS[v] * P
                    dve.wait_ge(sem["m_qk"], after(u))
                    V.reduce_max(mx[:, v:v + 1], pair(2 * (v % 2), n), axis=AX.X).then_inc(sem["m_max"], 1)
                    dve.wait_ge(sem["m_max"], MAXC(i, v + 1, max(0, v - 2)))
                    V.tensor_scalar(nmx[:, v:v + 1], mx[:, v:v + 1], -(QK ** -0.5), None, ALU.mult).then_inc(sem["m_nm"], 1)

        def MAXC(i, maxima, recips):
            return 2 * NU * i + min(maxima, NU) + recips + PRIME
        repeat(dve, MH // 2, mla)

        dve.wait_ge(sem["sk_zero"], 6)

        def stick(i):
            dve.wait_ge(sem["s_h"], 3 * i + 1)
            V.tensor_tensor(sqL[:], one(qkT[:, bass.ds(i, 1), :]), sqH[:], ALU.subtract).then_inc(sem["s_l"], 1)
            for e in range(2):
                o = 64 * e
                dve.wait_ge(sem["s_h"], 3 * i + 2 + e)
                V.tensor_tensor(skL[e][o:o + 64, :], one(qkT[o:o + 64, bass.ds(4 + i, 1), :]), skH[e][o:o + 64, :], ALU.subtract).then_inc(sem["s_l"], 1)
            for v in range(NU + 3):
                if v >= 3:
                    k = v - 3
                    e, qt = UNITS[k]
                    dve.wait_ge(sem["s_av"], after(i * NU + k))
                    V.tensor_copy(o_sb[:, qt, bass.ds((2 * i + e) * SBD, SBD)], ps[:, 6 + k % 2, 0:SBD]).then_inc(sem["s_o"], 1)
                if 2 <= v < NU + 2:
                    copy_out("s", i, v - 2, wT)
                if v < NU:
                    u, n = i * NU + v, BLOCKS[v] * P
                    dve.wait_ge(sem["s_nb"], after(u))
                    dve.wait_ge(sem["s_wp"], after(u - 2))
                    V.tensor_tensor_scan(left[v % 2][:, 1:n], omb[v % 2][:, 0:n - 1], omb[v % 2][:, 0:n - 1], 1.0, ALU.mult, ALU.bypass).then_inc(sem["s_scan"], 1)
                    dve.wait_ge(sem["s_b"], after(u))
                    dve.wait_ge(sem["s_scan"], after(u))
                    V.tensor_tensor(beta[v % 2][:, 0:n // 2], beta[v % 2][:, 0:n // 2], left[v % 2][:, 0:n // 2], ALU.mult).then_inc(sem["s_wd"], 1)
        repeat(dve, 4, stick)

        wsplit(H_OUT, H_OUT)
        dve.wait_ge(sem["grow_in"], 16)
        for tt in range(NT + 1):
            if tt < NT:
                dve.wait_ge(sem["o_sq"], 2 * tt + 2)
                V.tensor_scalar(oms[:, tt % 2, :], oss[:, tt % 2, :], 1.0 / 512, EPS, ALU.mult, ALU.add).then_inc(sem["o_ms"], 1)
                dve.wait_ge(sem["o_r"], tt + 1)
                for g, o in ((0, o_sb), (1, o_mla)):
                    V.scalar_tensor_tensor(ostage[tt % 2][:, g, :], o[:, tt, :], ors[:, tt % 2, g:g + 1], grow[:, g, :], ALU.mult, ALU.mult).then_inc(sem["o_scaled"], 1)
            if tt >= 1:
                k = tt - 1
                dve.wait_ge(sem["mix_h"], k + 1)
                V.tensor_tensor(mixL[:, :, k * P:(k + 1) * P], mix_banks(k), mixH[:, :, k * P:(k + 1) * P], ALU.subtract).then_inc(sem["mix_l"], 1)

        dve.wait_ge(sem["x2_in"], 16)
        dve.wait_ge(sem["sqa_zero"], 1)
        def out_pair(i):
            for u in range(2):
                t = 2 * i + u
                wsplit(H_OUT + t + 1, H_OUT + u + 1)
                dve.wait_ge(sem["pe_tile"], after(H_OUT + t))
                xt = one(x2[:, bass.ds(t, 1), :])
                V.scalar_tensor_tensor(xt, pair(2 * u), mod2[:, bass.ds(t, 1)], xt, ALU.mult, ALU.add).then_inc(sem["x2_done"], 1)
                dve.wait_ge(sem["x2_sq"], t + 1)
                dve.wait_ge(sem["sqa_done"], after(t - 1))
                V.tensor_tensor(sqa[:], sqa[:], sq2[u][:], ALU.add).then_inc(sem["sqa_done"], 1)
        repeat(dve, N_OUT // 2, out_pair)
        dve.wait_ge(sem["r2_mm"], 1)
        mean_squares(3, 4, D)
        diagonals(3, diag2)
        dve.wait_ge(sem["stat_bc"], 4)
        modulate(x2, xn2, a2, pair(6), mod2[:, 8:16], h2H, h2L, "xn2_done", "h2H_done", "h2L_done")

        dve.wait_ge(sem["x2_spill"], 16)

        def gate(i):
            for u in range(2):
                wsplit(H_GU + 2 * i + u + 1, H_GU + u + 1)
            dve.wait_ge(sem["silu_done"], after(i))
            dve.wait_ge(sem["pe_tile"], after(H_GU + 2 * i + 1))
            V.tensor_tensor(one(t_all[:, bass.ds(i, 1), :]), pair(2), gs[0][:], ALU.mult).then_inc(sem["t_done"], 1)
        repeat(dve, NF, gate)

        def t_split(d, f, hf, s):
            dve.wait_ge(sem["th_done"], d + 1)
            V.tensor_tensor(TL[s][:], one(t_all[:, bass.ds(f, 1), 512 * hf:512 * hf + 512]), TH[s][:], ALU.subtract).then_inc(sem["tl_done"], 1)

        for hf in range(2):
            def down(i, hf=hf):
                for u in range(2):
                    d = hf * NF + 2 * i + u
                    t_split(d, 2 * i + u, hf, u)
                    wsplit(H_DN + d + 1, H_DN + hf * NF + u + 1)
            if hf == 0:
                repeat(dve, NF // 2, down)
            else:
                repeat(dve, NF // 2 - 1, down)
                d = 2 * NF - 2
                t_split(d, NF - 2, 1, 0)
                wsplit(H_DN + d + 1, H_DN + d + 1)
                t_split(d + 1, NF - 1, 1, 1)
            dve.wait_ge(sem["xres_in"], 16 * (hf + 1))
            if hf == 1:
                dve.wait_ge(sem["y_out"], 16 * KD)
            for o in range(KD):
                if o < KD - 1:
                    dve.wait_ge(sem["d_mm"], hf * (KD - 1) + o + 1)
                else:
                    dve.wait_ge(sem["pe_tile"], after(H_DN + (hf + 1) * NF - 1))
                V.scalar_tensor_tensor(yst[:, o, :], ps[:, o, :], mod2[:, 24 + o:25 + o], xres[:, o, :], ALU.mult, ALU.add).then_inc(sem["y_done"], 1)

    @block.tensor
    def _(pe):
        for n in ("pe_tile", "q_mm", "kv_mm", "tr_done", "m_qk", "m_tr", "m_av", "s_qk", "s_tr", "s_av"):
            pe.sem_inc(sem[n], PRIME)
        mm = nc.tensor.matmul

        def three(out, lh, ll, rh, rl_, first, last):
            mm(out, lh, rh, start=first, stop=False)
            mm(out, lh, rl_, start=False, stop=False)
            return mm(out, ll, rh, start=False, stop=last)

        def proj_tile(h, par, b, XH, XL, ready=None):
            pe.wait_ge(sem["split_l"], h + (raw_index(par) - par) + 1)
            s = par % 2
            for j in range(KD):
                if ready:
                    pe.wait_ge(sem[ready], j + 1)
                for k, (l, r) in enumerate(((WH, XH), (WH, XL), (WL, XH))):
                    for hf in range(2):
                        last = mm(ps[:, b + hf, :], l[s][:, j * P:(j + 1) * P], r[:, j, 512 * hf:512 * hf + 512],
                                  start=(j == 0 and k == 0), stop=(j == KD - 1 and k == 2))
            last.then_inc(sem["pe_tile"], 1)

        def token_sums(bank, squares, first, last):
            for tt in range(NT):
                ins = mm(ps[:, bank, tt:tt + 1], squares[:, tt * P:(tt + 1) * P], ones[:, 0:1], start=(first and tt == 0), stop=last, skip_group_check=True)
            return ins

        def broadcast(k, diag, b):
            pe.wait_ge(sem["stat_diag"], k + 1)
            for hf in range(2):
                ins = mm(ps[:, b + hf, :], ones[:], diag[:, 4 * hf:4 * hf + 4, :].rearrange("p t n -> p (t n)"), start=True, stop=True)
            ins.then_inc(sem["stat_bc"], 1)

        pe.wait_ge(sem["pool_const"], 10)
        for j in range(KD):
            pe.wait_ge(sem["x_sq"], j + 1)
            token_sums(4, sq[j % 2], j == 0, j == KD - 1).then_inc(sem["x_sqmm"], 1)
        pe.wait_ge(sem["acc1_done"], 1)
        for m in range(16):
            last = mm(ps[:, 5, m:m + 1], acc1[:, m * P:(m + 1) * P], ones[:, 0:1], start=True, stop=True)
        last.then_inc(sem["mod1_mm"], 1)
        broadcast(0, diag1, 6)

        def in_pair(t0, i):
            for u in range(2):
                t = t0 + 2 * i + u
                pe.wait_ge(sem["in_evac"], after(t - 2))
                proj_tile(t, t0 + u, 2 * u, hH, hL, "hL_done" if t0 == 0 else None)

        repeat(pe, 3, lambda i: in_pair(0, i))
        in_pair(6, 0)
        for k in range(5):
            pe.wait_ge(sem["low_sq"], k + 1)
            token_sums(6 if k < 3 else 7, sql[k % 2], k in (0, 3), k in (2, 4)).then_inc(sem["low_mm"], 1)
        in_pair(8, 0)
        broadcast(1, diagl[:, 0], 4)
        broadcast(2, diagl[:, 1], 6)
        repeat(pe, 2, lambda i: in_pair(10, i))
        in_pair(14, 0)
        pe.wait_ge(sem["ada_acc"], KD + 1)
        pe.wait_ge(sem["low_done"], 5)
        for m in range(32):
            last = mm(ps[:, 4, m:m + 1], acc2[:, m * P:(m + 1) * P], ones[:, 0:1], start=True, stop=True)
        last.then_inc(sem["mod2_mm"], 1)
        in_pair(16, 0)

        def turn(tt, s):
            pe.wait_ge(sem["work_done"], after(tt))
            pe.wait_ge(sem["kv_free"], 5 * tt + 5 + PRIME)
            pe.wait_ge(sem["t_act"], 2 * tt + PRIME)
            pe.wait_ge(sem["t_dve"], after(tt - 1))
            w = work[s]
            for h in range(MH):
                nc.tensor.transpose(ps[:, 4, h * P:(h + 1) * P], w[:, QK * h:QK * h + P], ident[:])
                o = 768 if h == 0 else 896 + 128 * h
                nc.tensor.transpose(ps[:, 5, h * P:(h + 1) * P], w[:, o:o + P], ident[:])
            for g in range(3):
                last = nc.tensor.transpose(ps[:, 6, g * P:(g + 1) * P], rot[s][:, 2 * g:2 * g + 2, :].rearrange("p h n -> p (h n)"), ident[:])
            last.then_inc(sem["tr_done"], 1)

        def up_tile(tt, s, first=False):
            pe.wait_ge(sem["ll_done"], after(tt))
            pe.wait_ge(sem["q_free"], 4 * tt + PRIME)
            for k in range(3):
                for c in range(2):
                    last = three(ps[:, c, 0:384], LH[s][:, k, :], LL[s][:, k, :], UQH[:, k, 384 * c:384 * (c + 1)], UQL[:, k, 384 * c:384 * (c + 1)], k == 0, k == 2)
            last.then_inc(sem["q_mm"], 1)
            pe.wait_ge(sem["kv_free"], 5 * tt + PRIME)
            pe.wait_ge(sem["kr_free"], after(tt - 1))
            nc.tensor.transpose(ps[:, 7, 0:P], krT(tt), ident[:])
            for k in range(2):
                for c in range(2):
                    last = three(ps[:, 2 + c, :], LH[s][:, 3 + k, :], LL[s][:, 3 + k, :], UKH[:, k, 512 * c:512 * (c + 1)], UKL[:, k, 512 * c:512 * (c + 1)], k == 0, k == 1)
            last.then_inc(sem["kv_mm"], 1)
            if not first:
                turn(tt - 1, 1 - s)

        def krT(tt):
            return lowT[:, 5, bass.ds(tt * P, P)]

        for tt in range(NT):
            up_tile(tt, tt % 2, first=(tt == 0))
        turn(NT - 1, 1)
        for tt in range(NT):
            if tt < 2:
                pe.wait_ge(sem["q_free"], 4 * NT + PRIME)
            else:
                pe.wait_ge(sem["vt_odd"] if tt % 2 else sem["vt_even"], tt // 2)
            for c in range(4):
                last = nc.tensor.transpose(ps[:, tt % 2, c * P:(c + 1) * P], vT[:, c, tt * P:(tt + 1) * P], ident[:])
            last.then_inc(sem["vt_mm"], 1)

        def attention(pre, i, scores, src, dst, V, width, group1=NG1):
            def turn_unit(v):
                u, b = i * NU + v, BLOCKS[v]
                for w in wready[pre]:
                    pe.wait_ge(sem[w], after(u))
                pe.wait_ge(sem[pre + "_ta"], after(u - 1))
                pe.wait_ge(sem[pre + "_tv"], i * NG1 + G1_BEFORE[v] + PRIME)
                for k in range(b):
                    bank, c = (4, k) if k < G0[v] else (5, k - G0[v])
                    last = nc.tensor.transpose(ps[:, bank, c * P:(c + 1) * P], src[v % 2][:, k * P:(k + 1) * P], ident[:])
                last.then_inc(sem[pre + "_tr"], 1)

            def values(v):
                u, b = i * NU + v, BLOCKS[v]
                e, qt = UNITS[v]
                pe.wait_ge(sem[pre + "_o"], after(u - 2))
                pe.wait_ge(sem[pre + "_ta"], after(u))
                for k in range(b):
                    if k == G0[v]:
                        pe.wait_ge(sem[pre + "_tv"], i * NG1 + G1_BEFORE[v + 1] + PRIME)
                    last = mm(ps[:, 6 + v % 2, 0:width], dst[v % 2][:, k * P:(k + 1) * P],
                              V[:, qt + k, bass.ds((2 * i + e) * width, width)], start=(k == 0), stop=(k == b - 1))
                last.then_inc(sem[pre + "_av"], 1)

            def qk(v):
                u, (e, qt), n = i * NU + v, UNITS[v], BLOCKS[v] * P
                pe.wait_ge(sem[sfree[pre]], after(u - 2))
                for c0 in range(0, n, 512):
                    w = min(512, n - c0)
                    k0 = qt * P + c0
                    last = scores(e, qt * P, ps[:, 2 * (v % 2) + c0 // 512, 0:w], k0, w, c0 == 0)
                last.then_inc(sem[pre + "_qk"], 1)

            qk(0)
            qk(1)
            for v in range(NU):
                turn_unit(v)
                if v + 2 < NU:
                    qk(v + 2)
                values(v)

        wready = {"m": ("m_exp",), "s": ("s_wd", "s_wp")}
        sfree = {"m": "m_exp", "s": "s_b"}

        def mla_scores(e, q0, out, k0, w, diagonal):
            q, k = slice(q0, q0 + P), slice(k0, k0 + w)
            three(out, mqH[e][:, q], mqL[e][:, q], mkH[e][:, k], mkL[e][:, k], True, False)
            last = three(out, mrH[:, q], mrL[:, q], KRH[e][:, k], KRL[e][:, k], False, not diagonal)
            if diagonal:
                last = mm(out[:, 0:P], identb[:], mask_mla[:], start=False, stop=True)
            return last

        pe.wait_ge(sem["kr_zero"], 4)
        pe.wait_ge(sem["kr_l"], 2)

        def mla(i):
            pe.wait_ge(sem["m_l"], 5 * i + 5)
            attention("m", i, mla_scores, pm, pmT, VM, VD)
        repeat(pe, MH // 2, mla)

        def sb_scores(e, q0, out, k0, w, diagonal):
            q, k = slice(q0, q0 + P), slice(k0, k0 + w)
            last = three(out, sqH[:, q], sqL[:, q], skH[e][:, k], skL[e][:, k], True, not diagonal)
            if diagonal:
                last = mm(out[:, 0:P], identb[:], mask_sb[:], start=False, stop=True)
            return last

        def stick(i):
            pe.wait_ge(sem["s_l"], 3 * i + 3)
            attention("s", i, sb_scores, beta, wT, VS, SBD)
        repeat(pe, 4, stick)

        for tt in range(NT):
            pe.wait_ge(sem["o_scaled"], 2 * tt + 2)
            if tt >= 2:
                pe.wait_ge(sem["mix_l"], tt - 1)
            for c in range(8):
                last = nc.tensor.transpose(ps[:, 2 * (tt % 2) + c // 4, c % 4 * P:(c % 4 + 1) * P], ostage[tt % 2][:, c // 4, c % 4 * P:(c % 4 + 1) * P], ident[:])
            last.then_inc(sem["o_mm"], 1)

        pe.wait_ge(sem["mix_l"], NT)

        def out_pair(i):
            for u in range(2):
                t = 2 * i + u
                pe.wait_ge(sem["x2_done"], after(t - 2))
                proj_tile(H_OUT + t, H_OUT + u, 2 * u, mixH, mixL)
        repeat(pe, N_OUT // 2, out_pair)
        pe.wait_ge(sem["sqa_done"], after(N_OUT - 1))
        token_sums(4, sqa, True, True).then_inc(sem["r2_mm"], 1)
        broadcast(3, diag2, 6)

        pe.wait_ge(sem["h2L_done"], KD)

        def gate(i):
            pe.wait_ge(sem["silu_done"], after(i - 1))
            proj_tile(H_GU + 2 * i, H_GU, 0, h2H, h2L)
            pe.wait_ge(sem["t_done"], after(i - 1))
            proj_tile(H_GU + 2 * i + 1, H_GU + 1, 2, h2H, h2L)
        repeat(pe, NF, gate)
        pe.wait_ge(sem["t_done"], after(NF - 1))

        def down_tile(hf, d, par, first=False, last_=False):
            pe.wait_ge(sem["split_l"], H_DN + d + N_UP + 1)
            pe.wait_ge(sem["tl_done"], d + 1)
            s = par % 2
            for o in range(KD):
                if first and hf == 1:
                    pe.wait_ge(sem["y_done"], o + 1)
                w = slice(o * P, (o + 1) * P)
                last = three(ps[:, o, :], WH[s][:, w], WL[s][:, w], TH[s][:], TL[s][:], first, last_)
                if last_ and o < KD - 1:
                    last.then_inc(sem["d_mm"], 1)
            last.then_inc(sem["pe_tile"], 1)

        for hf in range(2):
            d0 = hf * NF
            down_tile(hf, d0, H_DN, first=True)
            down_tile(hf, d0 + 1, H_DN + 1)

            def down(i, hf=hf, d0=d0):
                for u in range(2):
                    down_tile(hf, d0 + 2 + 2 * i + u, H_DN + u)
            repeat(pe, NF // 2 - 2, down)
            down_tile(hf, d0 + NF - 2, H_DN)
            down_tile(hf, d0 + NF - 1, H_DN + 1, last_=True)
    ctx.close()


def kernel(**inputs):
    import concourse.bacc as bacc
    from concourse.bass_utils import run_bass_kernel_spmd as run

    g = {k: np.asarray(v) for k, v in inputs.items()}

    def col(v):
        return v.reshape(-1, P).T

    c = np.ascontiguousarray
    win = g["w_in"][0].reshape(KD, P, -1)
    arrays = {
        "xT": c(g["x"][0, ::-1].T.reshape(KD, P, S)),
        "cols": c(np.concatenate([col(g["c"][0]), col(g["b_ada"][0]), col(g["norm_attn"][0]), col(g["norm_ffn"][0]),
                                  col(g["q_a_norm"][0]), col(g["kv_a_norm"][0]), col(g["k_nope_norm"][0])], axis=1)),
        "rows": c(np.broadcast_to(np.concatenate([g["q_norm"][0], g["k_rope_norm"][0],
                                                  (1.0 / (10000.0 ** (np.arange(HALF, dtype=np.float32) / HALF))).astype(np.float32)]), (P, NROW))),
        "grow": c(np.broadcast_to(np.stack([g["out_norm_sb"][0], g["out_norm_mla"][0]]), (P, 2, 512))),
        "pos": c(g["positions"][0, ::-1].reshape(NT, P).T),
        "ada1": c(g["w_ada"][0][:, 0:2 * D].reshape(KD, P, 2 * D)),
        "ada2": c(g["w_ada"][0][:, 2 * D:].reshape(KD, P, 4 * D)),
        "win": c(np.stack([win[:, :, w:w + P].transpose(1, 0, 2).reshape(P, D) for w in W_COLS])),
        "qup": c(g["w_q_up"][0].reshape(3, P, MH * QK)),
        "kvup": c(g["w_kv_up"][0].reshape(2, P, D)),
        "wout": c(g["w_out"][0].reshape(KD, P, KD, P).transpose(2, 1, 0, 3).reshape(KD, P, D)),
        "gu": c(np.stack([g["w_gate"][0], g["w_up"][0]]).reshape(2, KD, P, NF, P).transpose(3, 0, 2, 1, 4).reshape(2 * NF, P, D)),
        "down": c(g["w_down"][0].reshape(NF, P, D)),
    }
    nc = bacc.Bacc("TRN2", target_bir_lowering=False, num_devices=1)
    aps = {k: nc.dram_tensor(k, v.shape, mybir.dt.from_np(v.dtype), kind="ExternalInput").ap() for k, v in arrays.items()}
    x2_d = nc.dram_tensor("x2_spill_d", (KD, P, S), F32, kind="Internal").ap()
    out = nc.dram_tensor("out", (KD, P, S), F32, kind="ExternalOutput").ap()
    build(nc, aps["xT"], aps["cols"], aps["rows"], aps["grow"], aps["pos"], aps["ada1"], aps["ada2"], aps["win"], aps["qup"],
          aps["kvup"], aps["wout"], aps["gu"], aps["down"], x2_d, out)
    r = run(nc, [arrays], core_ids=[0])
    return c(r.results[0]["out"].reshape(D, S).T[::-1][None])
```

```python
import numpy as np
from contextlib import ExitStack
import concourse.bass as bass
from concourse import mybir

F32 = mybir.dt.float32
F32R = mybir.dt.float32r
BF16 = mybir.dt.bfloat16
I32 = mybir.dt.int32
ALU = mybir.AluOpType
ACT = mybir.ActivationFunctionType
AX = mybir.AxisListType

P = 128
S = 1024
D = 1024
NT = S // P
KD = D // P
SBH, SBD = 8, 64
MH, NOPE, ROPE, VD = 4, 128, 64, 128
QK = NOPE + ROPE
QR, KVR = 384, 256
DFF = 2816
NF = DFF // P
EPS = 1e-6
HALF = ROPE // 2
NEG = -1e30
PRIME = 2

C_C, C_B, C_GA, C_GF, C_QA, C_KVA, C_KN = 0, 8, 56, 64, 72, 75, 77
NCOL = 78
R_Q, R_KR, R_FREQ = 0, QK, QK + ROPE
NROW = R_FREQ + HALF

W_COLS = [1536, 1664, 1792, 1920, 2048, 2112] + [128 * t for t in range(12)]
N_IN = len(W_COLS)
N_UP = 5
N_OUT = KD
H_OUT = N_IN
H_GU = H_OUT + N_OUT
H_DN = H_GU + 2 * NF


def raw_index(h):
    return h if h < N_IN else h + N_UP


class Chain:

    def __init__(self, eng, sem):
        self.eng, self.sem, self.base, self.n, self.at = eng, sem, 0, 0, 0

    def __call__(self, instruction):
        instruction.then_inc(self.sem, 1)
        self.n += 1
        return instruction

    def sync(self):
        self.eng.wait_ge(self.sem, self.at + self.n)

    def begin(self, i, per):
        self.base, self.n = self.base + self.n, 0
        self.at = self.base + i * per

    def end(self, times, per):
        assert self.n == per, (self.n, per)
        self.base, self.n = self.base + times * per, 0
        self.at = self.base


ORDER0 = [7, 1, 5, 3, 2, 4, 0, 6]
ORDER1 = [6, 0, 4, 2, 3, 5, 1, 7]
UNITS = [(0, i) for i in ORDER0] + [(1, i) for i in ORDER1]
NU = len(UNITS)
LAG = 3
BLOCKS = [NT - i for _, i in UNITS]
G0 = [(b + 1) // 2 for b in BLOCKS]
G1_BEFORE = [sum(b > 1 for b in BLOCKS[:k]) for k in range(NU + 1)]
NG1 = G1_BEFORE[NU]
SPLIT1, SPLIT0 = 2, 12
SB_EARLY = 5


def build(nc, xT, cols_d, rows_d, grow_d, pos_d, ada1_d, ada2_d, win_d, qup_d, kvup_d, wout_d, gu_d, down_d, x2_d, out_d):
    ctx = ExitStack()
    base = 16512

    def at(name, shape, dt, kb):
        return nc.alloc_sbuf_tensor_at(name, shape, dt, offset=base + int(kb * 1024))

    ident = at("ident", [P, P], F32, 0)
    identb = at("identb", [P, P], BF16, 0.5)
    mask_sb = at("mask_sb", [P, P], BF16, 0.75)
    mask_mla = at("mask_mla", [P, P], BF16, 1.0)
    ones = at("ones", [P, P], F32, 1.5)
    cols = at("cols", [P, NCOL], F32, 2.0)
    rows = at("rows", [P, NROW], F32, 2.5)
    pos_i = at("pos_i", [P, NT], I32, 4.0)
    pos_f = at("pos_f", [P, NT], F32, 4.03125)
    trig = at("trig", [P, NT, 2, HALF], F32, 4.125)
    silu_c = at("silu_c", [P, KD], F32, 6.125)
    mod1 = at("mod1", [P, 16], F32, 6.25)
    a1 = at("a1", [P, KD], F32, 6.375)
    mod2 = at("mod2", [P, 32], F32, 6.5)
    a2 = at("a2", [P, KD], F32, 6.75)
    ssq = at("ssq", [P, 2, 16], F32, 7.0)
    rstd = at("rstd", [P, 2, 16], F32, 7.25)
    mx = at("mx", [P, NU], F32, 7.5)
    nmx = at("nmx", [P, NU], F32, 7.625)
    qms = at("qms", [P, 2, 16], F32, 8.125)
    den = at("den", [P, NU], F32, 7.75)
    rden = at("rden", [P, NU], F32, 7.875)
    oss = at("oss", [P, NT, 2], F32, 8.5)
    oms = at("oms", [P, NT, 2], F32, 8.5625)
    ors = at("ors", [P, NT, 2], F32, 8.625)
    nhalf = at("nhalf", [P, 16], F32, 9.75)
    ms = at("ms", [P, 4, NT], F32, 9.8125)
    rms = at("rms", [P, 4, NT], F32, 8.25)
    WH = [at(f"WH{s}", [P, D], F32R, 10 + 8 * s) for s in range(2)]
    WL = [at(f"WL{s}", [P, D], F32R, 14 + 8 * s) for s in range(2)]
    raw = [at(f"raw{s}", [P, D], F32, 26 + 4 * s) for s in range(2)]
    hH = at("hH", [P, KD, S], F32R, 142)
    hL = at("hL", [P, KD, S], F32R, 174)
    qkT = at("qkT", [P, 8, S], F32, 34)
    vT = at("vT", [P, 4, S], F32, 66)
    lowT = at("lowT", [P, 6, S], F32, 82)
    ada1 = at("ada1", [P, KD // 2, KD, 4 * P], F32, 34)
    acc1 = [at(f"acc1{s}", [P, 4 * P], F32, 102 + 2 * s) for s in range(2)]
    sqs = at("sqs", [P, S], F32, 194)
    x_in = at("x_in", [P, KD, S], F32, 106)
    sq = [at(f"sq{s}", [P, S], F32, 198 + 4 * s) for s in range(2)]
    diag1 = at("diag1", [P, NT, P], F32, 98)
    ang = at("ang", [P, NT, 2, HALF], F32, 190)
    turns = at("turns", [P, NT, 2, HALF], F32, 192)
    ada2 = at("ada2", [P, 4 * D], F32, 106)
    acc2 = at("acc2", [P, 4 * D], F32, 122)
    sql = [at(f"sql{s}", [P, S], F32, 66 + 4 * s) for s in range(3)]
    diagl = [at("diagl0", [P, NT, P], F32, 138), at("diagl1", [P, NT, P], F32, 78)]
    UQH = at("UQH", [P, 3, MH * QK], F32R, 106)
    UQL = at("UQL", [P, 3, MH * QK], F32R, 115)
    UKH = at("UKH", [P, 2, D], F32R, 124)
    UKL = at("UKL", [P, 2, D], F32R, 132)
    LH = [at(f"LH{s}", [P, 5, P], F32R, 10 + 2.5 * s) for s in range(2)]
    LL = [at(f"LL{s}", [P, 5, P], F32R, 15 + 2.5 * s) for s in range(2)]
    work = [at(f"work{s}", [P, 1408], F32, 20 + 5.5 * s) for s in range(2)]
    rot = [at("rot0", [P, 6, ROPE], F32, 140), at("rot1", [P, 6, ROPE], F32, 206)]
    rope_c = at("rope_c", [P, 5, 2, HALF], F32, 31)
    rope_s = at("rope_s", [P, 5, 2, HALF], F32, 32.25)
    QN = at("QN", [P, MH, S], F32, 142)
    KN = at("KN", [P, MH, S], F32, 158)
    VM = at("VM", [P, NT, MH * VD], F32, 174)
    QRK = at("QRK", [P, 3, S], F32, 190)
    VS = at("VS", [P, NT, SBH * SBD], F32, 82)
    pm = [at(f"pm{s}", [P, S], F32, 10 + 4 * s) for s in range(2)]
    pmT = [at(f"pmT{s}", [P, S], F32, 18 + 4 * s) for s in range(2)]
    KRH = [at("KRH0", [P, S], F32R, 26), at("KRH1", [P, S], F32R, 98)]
    KRL = [at("KRL0", [P, S], F32R, 30), at("KRL1", [P, S], F32R, 102)]
    mqH = [at(f"mqH{e}", [P, S], F32R, 106 + 16 * e) for e in range(2)]
    mqL = [at(f"mqL{e}", [P, S], F32R, 110 + 16 * e) for e in range(2)]
    mkH = [at(f"mkH{e}", [P, S], F32R, 114 + 16 * e) for e in range(2)]
    mkL = [at(f"mkL{e}", [P, S], F32R, 118 + 16 * e) for e in range(2)]
    mrH = [at("mrH0", [P, S], F32R, 138), at("mrH1", [P, S], F32R, 142)]
    mrL = [at("mrL0", [P, S], F32R, 202), at("mrL1", [P, S], F32R, 158)]
    o_mla = at("o_mla", [P, NT, MH * VD], F32, 66)
    skH = [at(f"skH{e}", [P, S], F32R, 106 + 16 * e) for e in range(2)]
    skL = [at(f"skL{e}", [P, S], F32R, 110 + 16 * e) for e in range(2)]
    sqH = [at(f"sqH{e}", [P, S], F32R, 114 + 16 * e) for e in range(2)]
    sqL = [at(f"sqL{e}", [P, S], F32R, 118 + 16 * e) for e in range(2)]
    beta = [at(f"beta{s}", [P, S], F32, 142 + 4 * s) for s in range(2)]
    omb = [at(f"omb{s}", [P, S], F32, 150 + 4 * s) for s in range(2)]
    left = [at(f"left{s}", [P, S + 8], F32, 158 + 4.5 * s) for s in range(2)]
    wT = [at(f"wT{s}", [P, S], F32, 167 + 4 * s) for s in range(2)]
    grow = at("grow", [P, 2, 512], F32, 176)
    o_sb = at("o_sb", [P, NT, SBH * SBD], F32, 190)
    mixH = at("mixH", [P, KD, S], F32R, 82)
    mixL = at("mixL", [P, KD, S], F32R, 114)
    junk = at("junk", [P, 512], F32, 98)
    ostage = [at(f"ostage{s}", [P, 2, 512], F32, 148 + 4 * s) for s in range(2)]
    x2 = at("x2", [P, KD, S], F32, 34)
    sq2 = [at(f"sq2{s}", [P, S], F32, 66 + 4 * s) for s in range(2)]
    sqa = at("sqa", [P, S], F32, 74)
    diag2 = at("diag2", [P, NT, P], F32, 78)
    xn2 = [at(f"xn2{s}", [P, 512], F32, 82 + 4 * s) for s in range(2)]
    h2H = at("h2H", [P, KD, S], F32R, 142)
    h2L = at("h2L", [P, KD, S], F32R, 174)
    t_all = at("t_all", [P, NF, S], F32, 34)
    gs = [at(f"gs{s}", [P, S], F32, 122 + 4 * s) for s in range(2)]
    TH = [at(f"TH{s}", [P, 512], F32R, 130 + 2 * s) for s in range(2)]
    TL = [at(f"TL{s}", [P, 512], F32R, 134 + 2 * s) for s in range(2)]
    xres = at("xres", [P, KD, 512], F32, 142)
    yst = at("yst", [P, KD, 512], F32, 158)

    ps = ctx.enter_context(nc.psum_tensor("ps", [P, 8, 512], F32))

    def pair(b, n=S):
        return ps[:, b:b + 2, :].rearrange("p b n -> p (b n)")[:, 0:n]

    names = """small_in pool_const trig_args trig_done silu_c_done x_sq x_add x_sums stat_ms stat_r stat_diag stat_bc acc1_done mod1_mm a1_done
        xr_done h_done hH_done hL_done split_h split_l pe_tile in_evac ada2_in ada_acc mod2_mm low_sq low_mm low_done
        up_h up_l dve lh_done ll_done q_mm kv_mm q_sq k_sq q_ms q_r k_ms q_free kr_free rk_done kv_free work_done tr_done
        t_act t_dve vt_mm vt_even vt_odd low_over kr_zero left_one kr_h kr_l
        m_h m_l m_qk m_max m_nm m_exp m_tr m_ta m_tv m_av m_o
        sk_zero s_h s_l s_qk s_nb s_b s_scan s_wd s_wp s_tr s_ta s_tv s_av s_o
        grow_in o_sq o_ms o_r o_scaled o_mm mix_h mix_l x2_in sqa_zero sqa_done x2_done x2_half half_mm x2_sq x2_spill r2_mm xn2_done h2H_done
        h2L_done silu_done t_done th_done tl_done d_mm xres_in y_done y_out""".split()
    sem = {n: ctx.enter_context(nc.semaphore(n)) for n in names}
    ada1_in = [ctx.enter_context(nc.semaphore(f"ada1_in{k}")) for k in range(KD // 2)]
    xin_in = [ctx.enter_context(nc.semaphore(f"xin_in{k}")) for k in range(4)]
    raw_in = [ctx.enter_context(nc.semaphore(f"raw_in{k}")) for k in range(2)]

    block = ctx.enter_context(nc.Block())

    def after(n):
        return n + 1 + PRIME

    def one(ap):
        return ap.rearrange("p o n -> p (o n)")

    def dve_share(n):
        return n // 2

    def mix_banks(tt):
        b = 2 * (tt % 2)
        return ps[:, b:b + 2, :].rearrange("p b (j n) -> p (b j) n", j=4)

    SEGMENTS = [(0, 1), (2, 2), (6, 1), (8, 1), (10, 1), (12, 1), (14, 1), (16, 1)]

    def ffn_tiles(eng, tile):
        tile(0, 0, 0)
        with eng.Fori(0, (NF - 2) // 2) as i:
            for u in range(2):
                tile(1 + u + 2 * i, 1 + u, i)
        tile(NF - 1, NF - 1, 0)

    def repeat(eng, n, body):
        if n == 1:
            body(0)
        else:
            with eng.Fori(0, n) as i:
                body(i)

    @block.sync
    def _(sp):
        def load_raw(r, par, i, src):
            if not (isinstance(r, int) and r < 2):
                sp.wait_ge(sem["split_h"], r - 1)
                sp.wait_ge(sem["split_l"], r - 1)
            sp.dma_start(raw[par % 2][:, 0:src.shape[-1]], src).then_inc(raw_in[par % 2], 16)

        sp.dma_start(cols[:], cols_d).then_inc(sem["small_in"], 16)
        sp.dma_start(rows[:], rows_d).then_inc(sem["small_in"], 16)
        sp.dma_start(pos_i[:], pos_d).then_inc(sem["small_in"], 16)
        for k in range(4):
            sp.dma_start(x_in[:, 2 * k:2 * k + 2, :], xT[2 * k:2 * k + 2].rearrange("j p n -> p j n")).then_inc(xin_in[k], 16)
        for j in range(2):
            load_raw(j, j, 0, win_d[j])
        for g in range(KD // 2):
            sp.dma_start(ada1[:, g], ada1_d[g]).then_inc(ada1_in[g], 16)
        step = 0
        for t0, n in SEGMENTS[:-1]:
            def body(i, t0=t0, step=step):
                for u in range(2):
                    load_raw(t0 + 2 + 2 * i + u, t0 + u, i, one(win_d[bass.ds(t0 + 2 + 2 * i + u, 1)].rearrange("o p n -> p o n")))
                sp.wait_ge(sem["ada_acc"], step + i + 1)
                sp.dma_start(ada2[:], one(ada2_d[bass.ds(step + i, 1)].rearrange("o p n -> p o n"))).then_inc(sem["ada2_in"], 16)
            repeat(sp, n, body)
            step += n
        for k in range(3):
            load_raw(N_IN + k, N_IN + k, 0, qup_d[k])
        for k in range(2):
            load_raw(N_IN + 3 + k, N_IN + 3 + k, 0, kvup_d[k])
        sp.wait_ge(sem["m_av"], after(2 * NU - 1))
        sp.dma_start(grow[:], grow_d).then_inc(sem["grow_in"], 16)
        for u in range(2):
            load_raw(raw_index(H_OUT) + u, raw_index(H_OUT) + u, 0, wout_d[u])
        sp.wait_ge(sem["s_h"], 2 * SBH)
        sp.wait_ge(sem["s_l"], 2 * SBH)
        sp.dma_start(x2[:], xT.rearrange("j p n -> p j n")).then_inc(sem["x2_in"], 16)
        with sp.Fori(0, N_OUT // 2 - 1) as i:
            for u in range(2):
                r = raw_index(H_OUT) + 2 + u
                load_raw(r + 2 * i, r, i, one(wout_d[bass.ds(2 + u + 2 * i, 1)].rearrange("o p n -> p o n")))
        for u in range(2):
            r = raw_index(H_GU) + u
            load_raw(r, r, 0, gu_d[u])
        sp.wait_ge(sem["x2_half"], 4)
        sp.dma_start(x2_d.rearrange("j p n -> p j n"), x2[:]).then_inc(sem["x2_spill"], 16)
        with sp.Fori(0, NF - 1) as i:
            for u in range(2):
                r = raw_index(H_GU) + 2 + u
                load_raw(r + 2 * i, r, i, one(gu_d[bass.ds(2 + u + 2 * i, 1)].rearrange("o p n -> p o n")))
        for hf in range(2):
            with sp.Fori(0, NF // 2) as i:
                for u in range(2):
                    r = raw_index(H_DN) + hf * NF + u
                    load_raw(r + 2 * i, r, i, one(down_d[bass.ds(u + 2 * i, 1)].rearrange("o p n -> p o n")))

    @block.gpsimd
    def _(pool):
        for n in ("s_wp", "q_r", "rk_done"):
            pool.sem_inc(sem[n], PRIME)
        k = 0

        def fill(ins):
            nonlocal k
            ins.then_inc(sem["pool_const"], 1)
            k += 1

        fill(pool.memset(ident[:], 0.0))
        fill(pool.memset(identb[:], 0.0))
        fill(pool.memset(mask_sb[:], 0.0))
        fill(pool.memset(mask_mla[:], 0.0))
        fill(pool.memset(ones[:], 1.0))
        fill(pool.memset(nhalf[:], -0.5))
        pool.wait_ge(sem["pool_const"], k)
        for m in (ident, identb):
            fill(pool.affine_select(out=m[:], in_=m[:], compare_op=ALU.not_equal, fill=1.0, base=0, pattern=[[-1, P]], channel_multiplier=1))
        fill(pool.affine_select(out=mask_sb[:], in_=mask_sb[:], compare_op=ALU.is_gt, fill=NEG, base=0, pattern=[[1, P]], channel_multiplier=-1))
        fill(pool.affine_select(out=mask_mla[:], in_=mask_mla[:], compare_op=ALU.is_ge, fill=NEG, base=0, pattern=[[1, P]], channel_multiplier=-1))

        def rsqrt(k, row, t0=0, t1=NT):
            pool.wait_ge(sem["stat_ms"], k + 1)
            nc.gpsimd.tensor_tensor(rms[:, row, t0:t1], ms[:, row, t0:t1], nhalf[:, t0:t1], ALU.pow).then_inc(sem["stat_r"], 1)

        pool.wait_ge(sem["pool_const"], k)
        rsqrt(0, 0)
        for j in range(KD):
            pool.wait_ge(sem["hH_done"], j + 1)
            nc.gpsimd.tensor_tensor(hL[:, j, :], x_in[:, j, :], hH[:, j, :], ALU.subtract).then_inc(sem["hL_done"], 1)
        pool.wait_ge(sem["hL_done"], KD)
        pool.memset(acc2[:], 0.0).then_inc(sem["ada_acc"], 1)
        rsqrt(1, 1)
        rsqrt(2, 2)

        def head_rsqrt(i):
            for u in range(2):
                tt = 2 * i + u
                pool.wait_ge(sem["q_ms"], tt + 1)
                nc.gpsimd.tensor_tensor(rstd[:, u, 0:4], qms[:, u, 0:4], nhalf[:, 0:4], ALU.pow).then_inc(sem["q_r"], 1)
                pool.wait_ge(sem["k_ms"], tt + 1)
                nc.gpsimd.tensor_tensor(rstd[:, u, 4:9], qms[:, u, 4:9], nhalf[:, 0:5], ALU.pow).then_inc(sem["rk_done"], 1)
        repeat(pool, NT // 2, head_rsqrt)
        pool.wait_ge(sem["low_over"], 1)
        for e in range(2):
            o = 64 * (1 - e)
            pool.memset(KRH[e][o:o + 64, :].bitcast(F32), 0.0).then_inc(sem["kr_zero"], 1)
            pool.memset(KRL[e][o:o + 64, :].bitcast(F32), 0.0).then_inc(sem["kr_zero"], 1)
        for e, u in ((0, NU + 7), (1, 2 * NU - 1)):
            pool.wait_ge(sem["m_qk"], after(u))
            o = 64 * (1 - e)
            pool.memset(skH[e][o:o + 64, :].bitcast(F32), 0.0).then_inc(sem["sk_zero"], 1)
            pool.memset(skL[e][o:o + 64, :].bitcast(F32), 0.0).then_inc(sem["sk_zero"], 1)
            pool.wait_ge(sem["sk_zero"], 2 * e + 2)
        for s in range(2):
            pool.memset(left[s][:, 0:1], 1.0).then_inc(sem["left_one"], 1)
        pool.wait_ge(sem["left_one"], 2)

        def weights(i):
            for v, b in enumerate(BLOCKS):
                n, u = b * P, i * NU + v
                pool.wait_ge(sem["s_scan"], after(u))
                pool.wait_ge(sem["s_b"], after(u))
                c = dve_share(n)
                nc.gpsimd.tensor_tensor(beta[v % 2][:, c:n], beta[v % 2][:, c:n], left[v % 2][:, c:n], ALU.mult).then_inc(sem["s_wp"], 1)
        repeat(pool, 4, weights)
        for tt in range(NT):
            pool.wait_ge(sem["o_ms"], tt + 1)
            nc.gpsimd.tensor_tensor(ors[:, ORDER1[tt], :], oms[:, ORDER1[tt], :], nhalf[:, 0:2], ALU.pow).then_inc(sem["o_r"], 1)
        pool.wait_ge(sem["mix_l"], NT)
        pool.memset(sqa[:], 0.0).then_inc(sem["sqa_zero"], 1)
        for hf in range(2):
            rsqrt(3 + hf, 3, 4 * hf, 4 * hf + 4)
        for hf in range(2):
            if hf == 0:
                pool.wait_ge(sem["pe_tile"], after(H_DN - 1))
                pool.wait_ge(sem["x2_spill"], 16)
            else:
                pool.wait_ge(sem["y_done"], KD)
            pool.dma_start(xres[:], x2_d[:, :, 512 * hf:512 * hf + 512].rearrange("j p n -> p j n")).then_inc(sem["xres_in"], 16)
            for o in range(KD):
                pool.wait_ge(sem["y_done"], hf * KD + o + 1)
                pool.dma_start(out_d[o, :, 512 * hf:512 * hf + 512], yst[:, o, :]).then_inc(sem["y_out"], 16)
            pool.wait_ge(sem["y_out"], 16 * KD * (hf + 1))

    @block.scalar
    def _(act):
        for n in ("in_evac", "lh_done", "q_sq", "k_sq", "kv_free", "t_act", "m_exp", "m_ta", "s_nb", "s_b", "s_ta", "silu_done"):
            act.sem_inc(sem[n], PRIME)
        A = nc.scalar.activation

        def split(h, par, i):
            r = raw_index(par)
            act.wait_ge(raw_in[r % 2], 16 * (r // 2 + 1) + 16 * i)
            act.wait_ge(sem["pe_tile"], after(h - 2))
            A(WH[par % 2][:], raw[r % 2][:], ACT.Copy).then_inc(sem["split_h"], 1)

        act.wait_ge(sem["small_in"], 48)
        A(silu_c[:], cols[:, C_C:C_C + KD], ACT.Silu).then_inc(sem["silu_c_done"], 1)
        for j in range(KD):
            act.wait_ge(xin_in[j // 2], 16)
            if j >= 3:
                act.wait_ge(sem["x_add"], j - 2)
            A(sq[j % 2][:] if j else sqs[:], x_in[:, j, :], ACT.Square).then_inc(sem["x_sq"], 1)
        split(0, 0, 0)
        split(1, 1, 0)
        act.wait_ge(sem["trig_args"], 1)
        A(trig[:], ang[:], ACT.Sin).then_inc(sem["trig_done"], 1)
        for j in range(KD):
            act.wait_ge(sem["xr_done"], j + 1)
            act.wait_ge(sem["a1_done"], j // 2 + 1)
            A(x_in[:, j, :], x_in[:, j, :], ACT.Identity, scale=a1[:, j:j + 1], bias=mod1[:, j:j + 1]).then_inc(sem["h_done"], 1)
            act.wait_ge(sem["h_done"], j + 1)
            A(hH[:, j, :], x_in[:, j, :], ACT.Copy).then_inc(sem["hH_done"], 1)

        def in_tile(t, par, i, dst, last=False):
            if not last:
                split(t + 1, par + 1, i)
            act.wait_ge(sem["pe_tile"], after(t))
            A(dst, pair(2 * (par % 2)), ACT.Copy).then_inc(sem["in_evac"], 1)

        def in_pair(t0, i):
            for u in range(2):
                t = t0 + 2 * i + u
                dst = one(lowT[:, bass.ds(t, 1), :]) if t0 < 6 else qkT[:, t - 6, :]
                in_tile(t, t0 + u, i, dst)

        split(2, 2, 0)
        in_tile(0, 0, 0, lowT[:, 0, :], last=True)
        in_tile(1, 1, 0, lowT[:, 1, :], last=True)
        repeat(act, 2, lambda i: in_pair(2, i))
        in_pair(6, 0)
        def low_square(k):
            if k >= 3:
                act.wait_ge(sem["low_mm"], k - 2)
            A(sql[k % 3][:], lowT[:, k, :], ACT.Square).then_inc(sem["low_sq"], 1)
        for k in range(3):
            low_square(k)
        in_pair(8, 0)
        for k in range(3, 5):
            low_square(k)
        in_pair(10, 0)
        in_pair(12, 0)
        split(15, 15, 0)
        act.wait_ge(sem["low_done"], 5)
        in_tile(14, 14, 0, vT[:, 0, :], last=True)
        split(16, 16, 0)
        in_tile(15, 15, 0, vT[:, 1, :], last=True)
        split(17, 17, 0)
        act.wait_ge(sem["mod2_mm"], 1)
        for k in range(N_UP):
            r = N_IN + k
            act.wait_ge(raw_in[r % 2], 16 * (r // 2 + 1))
            dst, src = (UQH[:, k, :], raw[r % 2][:, 0:MH * QK]) if k < 3 else (UKH[:, k - 3, :], raw[r % 2][:])
            A(dst, src, ACT.Copy).then_inc(sem["split_h"], 1)
        in_tile(16, 16, 0, vT[:, 2, :], last=True)
        in_tile(17, 17, 0, vT[:, 3, :], last=True)

        def low_split(tt, s):
            act.wait_ge(sem["kv_mm"], after(tt - 2))
            A(LH[s][:], lowT[:, 0:5, bass.ds(tt * P, P)], ACT.Copy).then_inc(sem["lh_done"], 1)

        def turn_out(tt):
            act.wait_ge(sem["tr_done"], after(tt))
            A(QN[:, :, bass.ds(tt * P, P)], ps[:, 4, :].rearrange("p (h n) -> p h n", h=MH), ACT.Copy).then_inc(sem["t_act"], 1)
            A(QRK[:, :, bass.ds(tt * P, P)], ps[:, 6, 0:3 * P].rearrange("p (h n) -> p h n", h=3), ACT.Copy).then_inc(sem["t_act"], 1)

        def up_tile(tt, s, first=False, last=False):
            act.wait_ge(sem["q_mm"], after(tt))
            act.wait_ge(sem["tr_done"], after(tt - 2))
            A(work[s][:, 0:MH * QK].rearrange("p (b n) -> p b n", b=2), ps[:, 0:2, 0:384], ACT.Square).then_inc(sem["q_sq"], 1)
            if not last:
                low_split(tt + 1, 1 - s)
            act.wait_ge(sem["kv_mm"], after(tt))
            kv = ps[:, 2:4, :].rearrange("p b (h c n) -> p (b h) c n", h=2, c=2)
            A(work[s][:, 768:1280].rearrange("p (h n) -> p h n", h=MH), kv[:, :, 0, :], ACT.Square).then_inc(sem["k_sq"], 1)
            A(work[s][:, 1280:1344], ps[:, 7, 64:128], ACT.Square).then_inc(sem["k_sq"], 1)
            A(one3(VM[:, bass.ds(tt, 1), :]), kv[:, :, 1, :], ACT.Copy).then_inc(sem["kv_free"], 1)
            act.wait_ge(sem["rk_done"], after(tt))
            for h in range(MH):
                o = 768 if h == 0 else 896 + 128 * h
                A(work[s][:, o:o + P], kv[:, h, 0, :], ACT.Copy, scale=rstd[:, s, 4 + h:5 + h]).then_inc(sem["kv_free"], 1)
            if not first:
                turn_out(tt - 1)

        def one3(ap):
            return ap.rearrange("p o (h n) -> p (o h) n", h=MH)

        act.wait_ge(sem["pe_tile"], after(N_IN - 1))
        act.wait_ge(sem["split_l"], N_IN + N_UP)
        low_split(0, 0)
        up_tile(0, 0, first=True)

        def up_pair(i):
            for u in range(2):
                up_tile(1 + 2 * i + u, (1 + u) % 2)
        repeat(act, 3, up_pair)
        up_tile(NT - 1, 1, last=True)
        turn_out(NT - 1)
        for tt in range(0, NT, 2):
            act.wait_ge(sem["vt_mm"], tt + 1)
            A(VS[:, tt, :], ps[:, 0, :], ACT.Copy).then_inc(sem["vt_even"], 1)
        act.wait_ge(sem["vt_even"], NT // 2)
        act.wait_ge(sem["vt_odd"], NT // 2)
        act.wait_ge(sem["t_act"], 2 * NT + PRIME)
        act.wait_ge(sem["t_dve"], after(NT - 1))
        act.sem_inc(sem["low_over"], 1)

        for e in range(2):
            o = 64 * e
            A(KRH[e][o:o + 64, :], QRK[o:o + 64, 2, :], ACT.Copy).then_inc(sem["kr_h"], 1)

        def copy_out(pre, u, v, dst, b0=4):
            act.wait_ge(sem[pre + "_tr"], after(u))
            act.wait_ge(sem[pre + "_av"], after(u - 2))
            n = G0[v] * P
            A(dst[v % 2][:, 0:n], ps[:, b0, 0:n], ACT.Copy).then_inc(sem[pre + "_ta"], 1)

        def mla_split(p, e):
            if p or e:
                act.wait_ge(sem["m_qk"], PRIME if p == 0 else after(NU * (p - 1) + (7 if e == 0 else NU - 1)))
            if e == 0:
                A(mrH[p][:], QRK[:, p, :], ACT.Copy).then_inc(sem["m_h"], 1)
            A(mqH[e][:], QN[:, 2 * p + e, :], ACT.Copy).then_inc(sem["m_h"], 1)
            A(mkH[e][:], KN[:, 2 * p + e, :], ACT.Copy).then_inc(sem["m_h"], 1)

        def stick_split(p, e, wait):
            act.wait_ge(*wait)
            o = 64 * e
            A(sqH[e][:], one(qkT[:, bass.ds(p, 1), :]), ACT.Copy).then_inc(sem["s_h"], 1)
            A(skH[e][o:o + 64, :], one(qkT[o:o + 64, bass.ds(4 + p, 1), :]), ACT.Copy).then_inc(sem["s_h"], 1)

        mla_split(0, 0)
        for p in range(MH // 2):
            for v in range(NU + 2):
                if v < NU:
                    u, n = p * NU + v, BLOCKS[v] * P
                    act.wait_ge(sem["m_nm"], after(u))
                    act.wait_ge(sem["m_tr"], after(u - 2))
                    A(pm[v % 2][:, 0:n], pair(2 * (v % 2), n), ACT.Exp, bias=nmx[:, v:v + 1], scale=QK ** -0.5,
                      accum_out=den[:, v:v + 1]).then_inc(sem["m_exp"], 1)
                if v >= 2:
                    copy_out("m", p * NU + v - 2, v - 2, pmT)
                if v == SPLIT1:
                    mla_split(p, 1)
                if v == SPLIT0:
                    if p == 0:
                        mla_split(1, 0)
                    else:
                        stick_split(0, 0, (sem["m_qk"], after(NU + 7)))

        def head_squares(g, o, tt):
            A(junk[:], o[:, tt, :], ACT.Square, accum_out=oss[:, tt, g:g + 1]).then_inc(sem["o_sq"], 1)

        def stick(i, last=False):
            for v in range(NU + 2):
                if last and v < 2:
                    split(H_OUT + v, H_OUT + v, 0)
                if last and v < NT:
                    if v:
                        act.wait_ge(sem["o_sq"], v)
                    head_squares(1, o_mla, v)
                if last and v >= NU - SB_EARLY + 1:
                    tt = v - (NU - SB_EARLY + 1)
                    act.wait_ge(sem["s_o"], after(i * NU + NT + tt))
                    act.wait_ge(sem["o_sq"], NT + tt)
                    head_squares(0, o_sb, ORDER1[tt])
                if v < NU:
                    u, n = i * NU + v, BLOCKS[v] * P
                    act.wait_ge(sem["s_qk"], after(u))
                    act.wait_ge(sem["s_scan"], after(u - 2))
                    A(omb[v % 2][:, 0:n], pair(2 * (v % 2), n), ACT.Sigmoid, scale=-(SBD ** -0.5)).then_inc(sem["s_nb"], 1)
                if v >= 2:
                    copy_out("s", i * NU + v - 2, v - 2, wT)
                if v < NU:
                    act.wait_ge(sem["s_tr"], after(u - 2))
                    A(beta[v % 2][:, 0:n], pair(2 * (v % 2), n), ACT.Sigmoid, scale=SBD ** -0.5).then_inc(sem["s_b"], 1)
                if v == SPLIT1:
                    stick_split(i, 1, (sem["s_qk"], i * NU + PRIME))
                if v == SPLIT0 and not last:
                    stick_split(i + 1, 0, (sem["s_qk"], after(i * NU + 7)))

        with act.Fori(0, SBH // 2 - 1) as i:
            stick(i)
        stick(SBH // 2 - 1, last=True)

        for tt in range(SB_EARLY + 1, NT):
            act.wait_ge(sem["s_o"], after(3 * NU + NT + tt))
            act.wait_ge(sem["o_sq"], NT + tt)
            head_squares(0, o_sb, ORDER1[tt])
        for tt in range(NT):
            if tt == 0:
                act.wait_ge(sem["o_sq"], 2 * NT)
            act.wait_ge(sem["o_mm"], tt + 1)
            A(mixH[:, :, tt * P:(tt + 1) * P], mix_banks(tt), ACT.Copy).then_inc(sem["mix_h"], 1)

        def out_tile(t, par, i):
            if par:
                split(H_OUT + t + 1, H_OUT + par + 1, i)
            act.wait_ge(sem["x2_done"], after(t))
            A(sq2[par % 2][:], one(x2[:, bass.ds(t, 1), :]), ACT.Square).then_inc(sem["x2_sq"], 1)

        act.wait_ge(sem["mix_l"], NT)
        out_tile(0, 0, 0)
        out_tile(1, 1, 0)

        def out_pair(i):
            for u in range(2):
                out_tile(2 + 2 * i + u, 2 + u, i)
        repeat(act, N_OUT // 2 - 2, out_pair)
        split(H_OUT + N_OUT - 1, H_OUT + N_OUT - 1, 0)

        def half_square(k):
            hf, u = k // 2, k % 2
            act.wait_ge(sem["x2_half"], k + 1)
            A(sq2[u][:, 512 * hf:512 * hf + 512], x2[:, KD - 2 + u, 512 * hf:512 * hf + 512], ACT.Square).then_inc(sem["x2_sq"], 1)

        for k in range(3):
            half_square(k)
        split(H_GU, H_GU, 0)
        for n in range(2 * KD):
            if n == 3:
                half_square(3)
                split(H_GU + 1, H_GU + 1, 0)
            hf, j = n // KD, n % KD
            act.wait_ge(sem["xn2_done"], n + 1)
            A(h2H[:, j, 512 * hf:512 * hf + 512], xn2[j % 2][:], ACT.Identity, bias=mod2[:, 8 + j:9 + j]).then_inc(sem["h2H_done"], 1)

        def gate(f, f0, i):
            if f0:
                split(H_GU + 2 * f + 1, H_GU + 2 * f0 + 1, 2 * i)
            else:
                split(H_GU + 2, H_GU + 2, 0)
            act.wait_ge(sem["pe_tile"], after(H_GU + 2 * f))
            act.wait_ge(sem["t_done"], after(f - 2))
            A(gs[f0 % 2][:], pair(4 * (f0 % 2)), ACT.Silu).then_inc(sem["silu_done"], 1)
            if f0:
                split(H_GU + 2 * f + 2, H_GU + 2 * f0 + 2, 2 * i)
        ffn_tiles(act, gate)

        def t_split(d, f, hf, s):
            act.wait_ge(sem["pe_tile"], after(H_DN + d - 2))
            A(TH[s][:], one(t_all[:, bass.ds(f, 1), 512 * hf:512 * hf + 512]), ACT.Copy).then_inc(sem["th_done"], 1)

        act.wait_ge(sem["t_done"], after(NF - 1))
        for hf in range(2):
            def down(i, hf=hf):
                for u in range(2):
                    d = hf * NF + 2 * i + u
                    t_split(d, 2 * i + u, hf, u)
                    split(H_DN + d + 1, H_DN + hf * NF + u + 1, i)
            if hf == 0:
                repeat(act, NF // 2, down)
            else:
                repeat(act, NF // 2 - 1, down)
                d = 2 * NF - 2
                t_split(d, NF - 2, 1, 0)
                split(H_DN + d + 1, H_DN + d + 1, 0)
                t_split(d + 1, NF - 1, 1, 1)

    @block.vector
    def _(dve):
        for n in ("q_free", "kr_free", "work_done", "t_dve", "m_max", "m_nm", "m_tv", "m_o", "s_scan", "s_wd", "s_tv", "s_o", "t_done", "ll_done", "x2_done", "sqa_done"):
            dve.sem_inc(sem[n], PRIME)
        V = nc.vector
        ch = Chain(dve, sem["dve"])

        dve.wait_ge(sem["small_in"], 48)
        ch(V.tensor_copy(pos_f[:], pos_i[:]))
        ch.sync()
        fr = rows[:, R_FREQ:R_FREQ + HALF]
        for tt in range(NT):
            ch(V.tensor_scalar(ang[:, tt, 0, :], fr, pos_f[:, tt:tt + 1], None, ALU.mult))
            ch(V.tensor_scalar(ang[:, tt, 1, :], fr, pos_f[:, tt:tt + 1], None, ALU.mult))
        ch.sync()
        for c, off in ((0, 0.25), (1, 0.0)):
            ch(V.tensor_scalar(turns[:, :, c, :], ang[:, :, c, :], float(np.float32(1 / (2 * np.pi))), off, ALU.mult, ALU.add))
        ch.sync()
        magic = 1.5 * 2.0 ** 23
        ch(V.tensor_scalar(turns[:], turns[:], magic, None, ALU.add))
        ch.sync()
        ch(V.tensor_scalar(turns[:], turns[:], magic, None, ALU.subtract))
        ch.sync()
        c1 = 6.28125
        c2 = float(np.float32(round((2 * np.pi - c1) * 2 ** 20) / 2 ** 20))
        c3 = float(np.float32(2 * np.pi - c1 - c2))
        for c in (c1, c2, c3):
            ch(V.scalar_tensor_tensor(ang[:], turns[:], -c, ang[:], ALU.mult, ALU.add))
            ch.sync()
        ch(V.tensor_scalar(ang[:, :, 0, :], ang[:, :, 0, :], float(np.pi / 2), None, ALU.add))
        ch.sync()
        V.tensor_scalar(ang[:], ang[:], 3.1415925, -3.1415925, ALU.min, ALU.max).then_inc(sem["trig_args"], 1)

        def mean_squares(row, bank, n, t0=0, t1=NT):
            V.tensor_scalar(ms[:, row, t0:t1], ps[:, bank, t0:t1], 1.0 / n, EPS, ALU.mult, ALU.add).then_inc(sem["stat_ms"], 1)

        def diagonals(k, row, diag, t0=0, t1=NT):
            dve.wait_ge(sem["stat_r"], k + 1)
            for tt in range(t0, t1):
                ins = V.tensor_scalar(diag[:, tt, :], ident[:], rms[:, row, tt:tt + 1], None, ALU.mult)
            ins.then_inc(sem["stat_diag"], 1)

        def wsplit(h, par):
            r = raw_index(par)
            dve.wait_ge(sem["split_h"], h + (r - par) + 1)
            V.tensor_tensor(WL[par % 2][:], raw[r % 2][:], WH[par % 2][:], ALU.subtract).then_inc(sem["split_l"], 1)

        for j in range(1, KD):
            dve.wait_ge(sem["x_sq"], j + 1)
            if j >= 2:
                dve.wait_ge(sem["x_add"], j - 1)
            V.tensor_tensor(sqs[:], sqs[:], sq[j % 2][:], ALU.add).then_inc(sem["x_add"], 1)

        def adaln1(g, between=None):
            if g == 0:
                dve.wait_ge(sem["silu_c_done"], 1)
            if g >= 2:
                dve.wait_ge(sem["mod1_mm"], g - 1)
            dve.wait_ge(ada1_in[g], 16)
            a = acc1[g % 2]
            ch(V.tensor_scalar(a[:], ada1[:, g, 0, :], silu_c[:, 0:1], None, ALU.mult))
            for k in range(1, KD - 1):
                if k == 4 and between:
                    between()
                ch.sync()
                ins = V.scalar_tensor_tensor(a[:], ada1[:, g, k, :], silu_c[:, k:k + 1], a[:], ALU.mult, ALU.add)
                if k < KD - 2:
                    ch(ins)
            ins.then_inc(sem["acc1_done"], 1)

        wsplit(0, 0)
        wsplit(1, 1)
        dve.wait_ge(sem["x_sums"], 1)
        mean_squares(0, 4, D)
        diagonals(0, 0, diag1)
        adaln1(0)

        def scale_shift(g):
            dve.wait_ge(sem["mod1_mm"], g + 1)
            j = slice(2 * g, 2 * g + 2)
            ch(V.tensor_tensor(mod1[:].rearrange("p (s j) -> p s j", s=2)[:, :, j], ps[:, 4 + g % 2, 0:4].rearrange("p (s j) -> p s j", s=2),
                               cols[:, C_B:C_B + 16].rearrange("p (s j) -> p s j", s=2)[:, :, j], ALU.add))
            ch.sync()
            V.scalar_tensor_tensor(a1[:, j], mod1[:, 8 + 2 * g:10 + 2 * g], 1.0, cols[:, C_GA + 2 * g:C_GA + 2 * g + 2], ALU.add, ALU.mult).then_inc(sem["a1_done"], 1)

        dve.wait_ge(sem["stat_bc"], 1)
        for g in range(KD // 2):
            for j in (2 * g, 2 * g + 1):
                V.tensor_tensor(x_in[:, j, :], x_in[:, j, :], pair(6), ALU.mult).then_inc(sem["xr_done"], 1)
            if g + 1 < KD // 2:
                adaln1(g + 1, lambda: scale_shift(g))
            else:
                scale_shift(g)

        def in_pair(t0, i, step=None):
            for u in range(2):
                wsplit(t0 + 2 * i + u + 1, t0 + u + 1)
            if step is not None:
                ada_step(step)

        def ada_step(step):
            dve.wait_ge(sem["ada2_in"], 16 * (step + 1))
            dve.wait_ge(sem["ada_acc"], step + 1)
            V.scalar_tensor_tensor(acc2[:], ada2[:], silu_c[:, bass.ds(step, 1)], acc2[:], ALU.mult, ALU.add).then_inc(sem["ada_acc"], 1)

        wsplit(2, 2)
        ada_step(0)
        repeat(dve, 2, lambda i: in_pair(2, i, i + 1))
        in_pair(6, 0, 3)
        in_pair(8, 0, 4)
        in_pair(10, 0, 5)
        dve.wait_ge(sem["low_mm"], 5)
        mean_squares(1, 6, QR)
        mean_squares(2, 7, KVR)
        diagonals(1, 1, diagl[0])
        diagonals(2, 2, diagl[1])
        in_pair(12, 0, 6)
        for k in range(5):
            g = 0 if k < 3 else 1
            dve.wait_ge(sem["stat_bc"], 2 + g)
            V.scalar_tensor_tensor(lowT[:, k, :], lowT[:, k, :], cols[:, C_QA + k:C_QA + k + 1], pair(4 + 2 * g), ALU.mult, ALU.mult).then_inc(sem["low_done"], 1)
        in_pair(14, 0, 7)
        wsplit(17, 17)
        dve.wait_ge(sem["mod2_mm"], 1)
        ch(V.tensor_tensor(mod2[:], ps[:, 4, 0:32], cols[:, C_B + 16:C_B + 48], ALU.add))
        ch.sync()
        ch(V.scalar_tensor_tensor(a2[:], mod2[:, 16:24], 1.0, cols[:, C_GF:C_GF + KD], ALU.add, ALU.mult))
        for k in range(N_UP):
            r = N_IN + k
            dve.wait_ge(sem["split_h"], r + 1)
            if k < 3:
                V.tensor_tensor(UQL[:, k, :], raw[r % 2][:, 0:MH * QK], UQH[:, k, :], ALU.subtract).then_inc(sem["split_l"], 1)
            else:
                V.tensor_tensor(UKL[:, k - 3, :], raw[r % 2][:], UKH[:, k - 3, :], ALU.subtract).then_inc(sem["split_l"], 1)

        def low_split(tt, s):
            dve.wait_ge(sem["lh_done"], after(tt))
            V.tensor_tensor(LL[s][:], lowT[:, 0:5, bass.ds(tt * P, P)], LH[s][:], ALU.subtract).then_inc(sem["ll_done"], 1)

        def turn_out(tt):
            dve.wait_ge(sem["tr_done"], after(tt))
            V.tensor_scalar(KN[:, :, bass.ds(tt * P, P)], ps[:, 5, :].rearrange("p (h n) -> p h n", h=MH), cols[:, C_KN:C_KN + 1], None, ALU.mult).then_inc(sem["t_dve"], 1)

        def up_tile(tt, s, first=False, last=False):
            w = work[s]
            dve.wait_ge(sem["q_sq"], after(tt))
            ch(V.reduce_sum(ssq[:, s, 0:4], w[:, 0:MH * QK].rearrange("p (h n) -> p h n", h=MH), axis=AX.X))
            ch.sync()
            V.tensor_scalar(qms[:, s, 0:4], ssq[:, s, 0:4], 1.0 / QK, EPS, ALU.mult, ALU.add).then_inc(sem["q_ms"], 1)
            dve.wait_ge(sem["q_r"], after(tt))
            for h in range(MH):
                o = QK * (h % 2)
                V.scalar_tensor_tensor(w[:, QK * h:QK * (h + 1)], ps[:, h // 2, o:o + QK], rstd[:, s, h:h + 1], rows[:, R_Q:R_Q + QK],
                                       ALU.mult, ALU.mult).then_inc(sem["q_free"], 1)
            if not last:
                low_split(tt + 1, 1 - s)
            dve.wait_ge(sem["k_sq"], 2 * tt + 2 + PRIME)
            ch(V.reduce_sum(ssq[:, s, 4:8], w[:, 768:1280].rearrange("p (h n) -> p h n", h=MH), axis=AX.X))
            ch(V.reduce_sum(ssq[:, s, 8:9], w[:, 1280:1344], axis=AX.X))
            ch.sync()
            V.tensor_scalar(qms[:, s, 4:8], ssq[:, s, 4:8], 1.0 / NOPE, EPS, ALU.mult, ALU.add)
            V.tensor_scalar(qms[:, s, 8:9], ssq[:, s, 8:9], 1.0 / ROPE, EPS, ALU.mult, ALU.add).then_inc(sem["k_ms"], 1)
            dve.wait_ge(sem["rk_done"], after(tt))
            V.scalar_tensor_tensor(w[:, 896:960], ps[:, 7, 64:128], rstd[:, s, 8:9], rows[:, R_KR:R_KR + ROPE], ALU.mult, ALU.mult).then_inc(sem["kr_free"], 1)
            dve.wait_ge(sem["kr_free"], after(tt))
            dve.wait_ge(sem["q_free"], 4 * tt + 4 + PRIME)
            x = w[:, 0:5 * QK].rearrange("p (h n) -> p h n", h=5)[:, :, NOPE:QK].rearrange("p h (c n) -> p h c n", c=2)
            for c, dst in ((0, rope_c), (1, rope_s)):
                for hv in range(2):
                    tab = one(trig[:, bass.ds(tt, 1), c, :]).unsqueeze(1).broadcast_to([P, 5, HALF])
                    ch(V.tensor_tensor(dst[:, :, hv, :], x[:, :, hv, :], tab, ALU.mult))
            ch.sync()
            ch(V.tensor_tensor(rot[s][:, 0:5, 0:HALF], rope_c[:, :, 0, :], rope_s[:, :, 1, :], ALU.subtract))
            ch(V.tensor_tensor(rot[s][:, 0:5, HALF:ROPE], rope_c[:, :, 1, :], rope_s[:, :, 0, :], ALU.add))
            ch.sync()
            V.tensor_copy(rot[s][:, 5, :], rot[s][:, 4, :]).then_inc(sem["work_done"], 1)
            if not first:
                turn_out(tt - 1)

        dve.wait_ge(sem["pe_tile"], after(N_IN - 1))
        low_split(0, 0)
        up_tile(0, 0, first=True)

        def up_pair(i):
            for u in range(2):
                up_tile(1 + 2 * i + u, (1 + u) % 2)

        UPC = 9
        with dve.Fori(0, 3) as i:
            ch.begin(i, 2 * UPC)
            up_pair(i)
        ch.end(3, 2 * UPC)
        up_tile(NT - 1, 1, last=True)
        turn_out(NT - 1)
        for tt in range(1, NT, 2):
            dve.wait_ge(sem["vt_mm"], tt + 1)
            V.tensor_copy(VS[:, tt, :], ps[:, 1, :]).then_inc(sem["vt_odd"], 1)

        for e in range(2):
            o = 64 * e
            dve.wait_ge(sem["kr_h"], e + 1)
            V.tensor_tensor(KRL[e][o:o + 64, :], QRK[o:o + 64, 2, :], KRH[e][o:o + 64, :], ALU.subtract).then_inc(sem["kr_l"], 1)

        def copy_out(pre, i, v, dst, b=5):
            if BLOCKS[v] > 1:
                dve.wait_ge(sem[pre + "_tr"], after(i * NU + v))
                dve.wait_ge(sem[pre + "_av"], after(i * NU + v - 2))
                n0, n = G0[v] * P, BLOCKS[v] * P
                V.tensor_copy(dst[v % 2][:, n0:n], ps[:, b, 0:n - n0]).then_inc(sem[pre + "_tv"], 1)

        def mla_split(p, e):
            ops = [(mqL[e], QN[:, 2 * p + e, :], mqH[e]), (mkL[e], KN[:, 2 * p + e, :], mkH[e])]
            if e == 0:
                ops = [(mrL[p], QRK[:, p, :], mrH[p])] + ops
            for k, (lo, x, hi) in enumerate(ops):
                dve.wait_ge(sem["m_h"], 5 * p + 3 * e + k + 1)
                V.tensor_tensor(lo[:], x, hi[:], ALU.subtract).then_inc(sem["m_l"], 1)

        def stick_split(p, e):
            o = 64 * e
            dve.wait_ge(sem["s_h"], 4 * p + 2 * e + 1)
            V.tensor_tensor(sqL[e][:], one(qkT[:, bass.ds(p, 1), :]), sqH[e][:], ALU.subtract).then_inc(sem["s_l"], 1)
            dve.wait_ge(sem["s_h"], 4 * p + 2 * e + 2)
            V.tensor_tensor(skL[e][o:o + 64, :], one(qkT[o:o + 64, bass.ds(4 + p, 1), :]), skH[e][o:o + 64, :], ALU.subtract).then_inc(sem["s_l"], 1)

        def maxima(p, done, recips):
            return 2 * NU * p + min(done, NU) + recips + PRIME

        mla_split(0, 0)
        for p in range(MH // 2):
            for v in range(NU + 3):
                if v < NU:
                    u, n = p * NU + v, BLOCKS[v] * P
                    dve.wait_ge(sem["m_qk"], after(u))
                    V.reduce_max(mx[:, v:v + 1], pair(2 * (v % 2), n), axis=AX.X).then_inc(sem["m_max"], 1)
                    dve.wait_ge(sem["m_max"], maxima(p, v + 1, max(0, v - 3)))
                    V.tensor_scalar(nmx[:, v:v + 1], mx[:, v:v + 1], -(QK ** -0.5), None, ALU.mult).then_inc(sem["m_nm"], 1)
                if 2 <= v < NU + 2:
                    copy_out("m", p, v - 2, pmT)
                if v >= 3:
                    k = v - 3
                    e, qt = UNITS[k]
                    dve.wait_ge(sem["m_av"], after(p * NU + k))
                    V.reciprocal(rden[:, k:k + 1], den[:, k:k + 1]).then_inc(sem["m_max"], 1)
                    dve.wait_ge(sem["m_max"], maxima(p, v + 1, k + 1))
                    V.tensor_scalar(o_mla[:, qt, (2 * p + e) * VD:(2 * p + e + 1) * VD], ps[:, 6 + k % 2, 0:VD], rden[:, k:k + 1], None, ALU.mult).then_inc(sem["m_o"], 1)
                if v == SPLIT1:
                    mla_split(p, 1)
                if v == SPLIT0:
                    if p == 0:
                        mla_split(1, 0)
                    else:
                        stick_split(0, 0)

        dve.wait_ge(sem["left_one"], 2)

        def stick(i, last=False):
            for v in range(NU + 3):
                if v < NU:
                    u, n = i * NU + v, BLOCKS[v] * P
                    dve.wait_ge(sem["s_nb"], after(u))
                    dve.wait_ge(sem["s_wp"], after(u - 2))
                    V.tensor_tensor_scan(left[v % 2][:, 1:n], omb[v % 2][:, 0:n - 1], omb[v % 2][:, 0:n - 1], 1.0, ALU.mult, ALU.bypass).then_inc(sem["s_scan"], 1)
                if 2 <= v < NU + 2:
                    copy_out("s", i, v - 2, wT)
                if v < NU:
                    dve.wait_ge(sem["s_b"], after(u))
                    dve.wait_ge(sem["s_scan"], after(u))
                    c = dve_share(n)
                    V.tensor_tensor(beta[v % 2][:, 0:c], beta[v % 2][:, 0:c], left[v % 2][:, 0:c], ALU.mult).then_inc(sem["s_wd"], 1)
                if v >= 3:
                    k = v - 3
                    e, qt = UNITS[k]
                    dve.wait_ge(sem["s_av"], after(i * NU + k))
                    V.tensor_copy(o_sb[:, qt, bass.ds((2 * i + e) * SBD, SBD)], ps[:, 6 + k % 2, 0:SBD]).then_inc(sem["s_o"], 1)
                if v == SPLIT1:
                    stick_split(i, 1)
                if v == SPLIT0 and not last:
                    stick_split(i + 1, 0)
                if last and v < 2:
                    wsplit(H_OUT + v, H_OUT + v)
                if last and v >= NU - SB_EARLY + 2:
                    head_mean_squares(v - (NU - SB_EARLY + 2))

        def head_mean_squares(tt):
            dve.wait_ge(sem["o_sq"], NT + tt + 1)
            V.tensor_scalar(oms[:, ORDER1[tt], :], oss[:, ORDER1[tt], :], 1.0 / 512, EPS, ALU.mult, ALU.add).then_inc(sem["o_ms"], 1)

        with dve.Fori(0, SBH // 2 - 1) as i:
            stick(i)
        stick(SBH // 2 - 1, last=True)

        dve.wait_ge(sem["grow_in"], 16)
        for tt in range(SB_EARLY + 1, NT):
            head_mean_squares(tt)
        for tt in range(NT + 1):
            if tt < NT:
                dve.wait_ge(sem["o_r"], ORDER1.index(tt) + 1)
                if tt >= 2:
                    dve.wait_ge(sem["o_mm"], tt - 1)
                for g, o in ((0, o_sb), (1, o_mla)):
                    V.scalar_tensor_tensor(ostage[tt % 2][:, g, :], o[:, tt, :], ors[:, tt, g:g + 1], grow[:, g, :], ALU.mult, ALU.mult).then_inc(sem["o_scaled"], 1)
            if tt >= 1:
                k = tt - 1
                dve.wait_ge(sem["mix_h"], k + 1)
                V.tensor_tensor(mixL[:, :, k * P:(k + 1) * P], mix_banks(k), mixH[:, :, k * P:(k + 1) * P], ALU.subtract).then_inc(sem["mix_l"], 1)

        dve.wait_ge(sem["x2_in"], 16)
        dve.wait_ge(sem["sqa_zero"], 1)

        def out_tile(t, par, b):
            if par:
                wsplit(H_OUT + t + 1, H_OUT + par + 1)
            dve.wait_ge(sem["pe_tile"], after(H_OUT + t))
            xt = one(x2[:, bass.ds(t, 1), :])
            V.scalar_tensor_tensor(xt, pair(b), mod2[:, bass.ds(t, 1)], xt, ALU.mult, ALU.add).then_inc(sem["x2_done"], 1)
            dve.wait_ge(sem["x2_sq"], t + 1)
            dve.wait_ge(sem["sqa_done"], after(t - 1))
            V.tensor_tensor(sqa[:], sqa[:], sq2[par % 2][:], ALU.add).then_inc(sem["sqa_done"], 1)

        out_tile(0, 0, 4)
        out_tile(1, 1, 6)

        def out_pair(i):
            for u in range(2):
                out_tile(2 + 2 * i + u, 2 + u, 2 * u)
        repeat(dve, N_OUT // 2 - 2, out_pair)
        wsplit(H_OUT + N_OUT - 1, H_OUT + N_OUT - 1)

        def half_residual(k):
            hf, u = k // 2, k % 2
            if hf == 0:
                dve.wait_ge(sem["half_mm"], u + 1)
            else:
                dve.wait_ge(sem["pe_tile"], after(H_OUT + N_OUT - 2 + u))
            t = slice(512 * hf, 512 * hf + 512)
            xt = x2[:, KD - 2 + u, t]
            V.scalar_tensor_tensor(xt, ps[:, 2 * u + hf, :], mod2[:, KD - 2 + u:KD - 1 + u], xt, ALU.mult, ALU.add).then_inc(sem["x2_half"], 1)

        def half_add(hf):
            t = slice(512 * hf, 512 * hf + 512)
            dve.wait_ge(sem["x2_sq"], N_OUT - 2 + 2 * hf + 1)
            dve.wait_ge(sem["sqa_done"], after(N_OUT - 3 + hf))
            V.tensor_tensor(sqa[:, t], sqa[:, t], sq2[0][:, t], ALU.add).then_inc(sem["sqa_done"], 1)

        def modulate_half(n):
            if n < 2 * KD:
                hf, j = n // KD, n % KD
                if j == 0:
                    dve.wait_ge(sem["stat_bc"], 4 + hf)
                if n >= 2:
                    dve.wait_ge(sem["h2L_done"], n - 1)
                V.scalar_tensor_tensor(xn2[j % 2][:], x2[:, j, 512 * hf:512 * hf + 512], a2[:, j:j + 1], ps[:, 6 + hf, :], ALU.mult, ALU.mult).then_inc(sem["xn2_done"], 1)
            if n >= 1:
                hf, j = (n - 1) // KD, (n - 1) % KD
                t = slice(512 * hf, 512 * hf + 512)
                dve.wait_ge(sem["h2H_done"], n)
                V.scalar_tensor_tensor(h2L[:, j, t], xn2[j % 2][:], mod2[:, 8 + j:9 + j], h2H[:, j, t], ALU.add, ALU.subtract).then_inc(sem["h2L_done"], 1)

        half_residual(0)
        half_add(0)
        half_residual(1)
        dve.wait_ge(sem["r2_mm"], 1)
        mean_squares(3, 4, D, 0, 4)
        half_residual(2)
        half_add(1)
        diagonals(3, 3, diag2, 0, 4)
        wsplit(H_GU, H_GU)
        for n in range(2 * KD + 1):
            if n == 3:
                half_residual(3)
            if n == 4:
                wsplit(H_GU + 1, H_GU + 1)
            if n == 5:
                dve.wait_ge(sem["r2_mm"], 2)
                mean_squares(3, 5, D, 4, NT)
            if n == 7:
                diagonals(4, 3, diag2, 4, NT)
            modulate_half(n)

        dve.wait_ge(sem["x2_spill"], 16)

        def gate(f, f0, i):
            if f0:
                wsplit(H_GU + 2 * f + 1, H_GU + 2 * f0 + 1)
            wsplit(H_GU + 2 * f + 2, H_GU + 2 * f0 + 2)
            dve.wait_ge(sem["silu_done"], after(f))
            dve.wait_ge(sem["pe_tile"], after(H_GU + 2 * f + 1))
            V.tensor_tensor(one(t_all[:, bass.ds(f, 1), :]), pair(4 * (f0 % 2) + 2), gs[f0 % 2][:], ALU.mult).then_inc(sem["t_done"], 1)
        ffn_tiles(dve, gate)

        def t_split(d, f, hf, s):
            dve.wait_ge(sem["th_done"], d + 1)
            V.tensor_tensor(TL[s][:], one(t_all[:, bass.ds(f, 1), 512 * hf:512 * hf + 512]), TH[s][:], ALU.subtract).then_inc(sem["tl_done"], 1)

        for hf in range(2):
            def down(i, hf=hf):
                for u in range(2):
                    d = hf * NF + 2 * i + u
                    t_split(d, 2 * i + u, hf, u)
                    wsplit(H_DN + d + 1, H_DN + hf * NF + u + 1)
            if hf == 0:
                repeat(dve, NF // 2, down)
            else:
                repeat(dve, NF // 2 - 1, down)
                d = 2 * NF - 2
                t_split(d, NF - 2, 1, 0)
                wsplit(H_DN + d + 1, H_DN + d + 1)
                t_split(d + 1, NF - 1, 1, 1)
            dve.wait_ge(sem["xres_in"], 16 * (hf + 1))
            if hf == 1:
                dve.wait_ge(sem["y_out"], 16 * KD)
            for o in range(KD):
                if o < KD - 1:
                    dve.wait_ge(sem["d_mm"], hf * (KD - 1) + o + 1)
                else:
                    dve.wait_ge(sem["pe_tile"], after(H_DN + (hf + 1) * NF - 1))
                V.scalar_tensor_tensor(yst[:, o, :], ps[:, o, :], mod2[:, 24 + o:25 + o], xres[:, o, :], ALU.mult, ALU.add).then_inc(sem["y_done"], 1)

    @block.tensor
    def _(pe):
        for n in ("pe_tile", "q_mm", "kv_mm", "tr_done", "m_qk", "m_tr", "m_av", "s_qk", "s_tr", "s_av"):
            pe.sem_inc(sem[n], PRIME)
        mm = nc.tensor.matmul

        def three(out, lh, ll, rh, rl, first, last):
            mm(out, lh, rh, start=first, stop=False)
            mm(out, lh, rl, start=False, stop=False)
            return mm(out, ll, rh, start=False, stop=last)

        def proj_tile(h, par, b, XH, XL):
            pe.wait_ge(sem["split_l"], h + (raw_index(par) - par) + 1)
            s = par % 2
            for j in range(KD):
                for k, (l, r) in enumerate(((WH, XH), (WH, XL), (WL, XH))):
                    for hf in range(2):
                        last = mm(ps[:, b + hf, :], l[s][:, j * P:(j + 1) * P], r[:, j, 512 * hf:512 * hf + 512],
                                  start=(j == 0 and k == 0), stop=(j == KD - 1 and k == 2))
            last.then_inc(sem["pe_tile"], 1)

        def half_chunk(s, b, hf, j, XH, XL):
            w, t = slice(j * P, (j + 1) * P), slice(512 * hf, 512 * hf + 512)
            return three(ps[:, b + hf, :], WH[s][:, w], WL[s][:, w], XH[:, j, t], XL[:, j, t], j == 0, j == KD - 1)

        def token_sums(bank, squares, first, last, t0=0, t1=NT):
            for tt in range(t0, t1):
                ins = mm(ps[:, bank, tt:tt + 1], squares[:, tt * P:(tt + 1) * P], ones[:, 0:1], start=(first and tt == t0), stop=last, skip_group_check=True)
            return ins

        def broadcast(k, diag, b, halves=(0, 1)):
            pe.wait_ge(sem["stat_diag"], k + 1)
            for hf in halves:
                ins = mm(ps[:, b + hf, :], ones[:], diag[:, 4 * hf:4 * hf + 4, :].rearrange("p t n -> p (t n)"), start=True, stop=True)
            ins.then_inc(sem["stat_bc"], 1)

        pe.wait_ge(sem["pool_const"], 10)
        pe.wait_ge(sem["x_add"], KD - 1)
        token_sums(4, sqs, True, True).then_inc(sem["x_sums"], 1)

        def adaln1(g):
            if g == 0:
                pe.wait_ge(sem["stat_ms"], 1)
            if g >= 2:
                pe.wait_ge(sem["a1_done"], g - 1)
            pe.wait_ge(ada1_in[g], 16)
            pe.wait_ge(sem["silu_c_done"], 1)
            pe.wait_ge(sem["acc1_done"], g + 1)
            for m in range(4):
                w = slice(m * P, (m + 1) * P)
                mm(ps[:, 4 + g % 2, m:m + 1], ada1[:, g, KD - 1, w], silu_c[:, KD - 1:KD], start=True, stop=False, skip_group_check=True)
                last = mm(ps[:, 4 + g % 2, m:m + 1], acc1[g % 2][:, w], ones[:, 0:1], start=False, stop=True, skip_group_check=True)
            last.then_inc(sem["mod1_mm"], 1)

        broadcast(0, diag1, 6)
        adaln1(0)

        def in_pair(t0, i):
            for u in range(2):
                t = t0 + 2 * i + u
                pe.wait_ge(sem["in_evac"], after(t - 2))
                proj_tile(t, t0 + u, 2 * u, hH, hL)

        pe.wait_ge(sem["split_l"], 2)
        for n in range(KD + LAG):
            if n % 2 == 0 and n // 2 + 1 < KD // 2:
                adaln1(n // 2 + 1)
            if n < KD:
                pe.wait_ge(sem["hL_done"], n + 1)
                for hf in range(2):
                    last = half_chunk(0, 0, hf, n, hH, hL)
                if n == KD - 1:
                    last.then_inc(sem["pe_tile"], 1)
            if n >= LAG:
                for hf in range(2):
                    last = half_chunk(1, 2, hf, n - LAG, hH, hL)
        last.then_inc(sem["pe_tile"], 1)
        repeat(pe, 2, lambda i: in_pair(2, i))
        in_pair(6, 0)
        def low_sums(ks):
            for k in ks:
                pe.wait_ge(sem["low_sq"], k + 1)
                token_sums(6 if k < 3 else 7, sql[k % 3], k in (0, 3), k in (2, 4)).then_inc(sem["low_mm"], 1)

        in_pair(8, 0)
        low_sums((0, 1, 2))
        in_pair(10, 0)
        low_sums((3, 4))
        in_pair(12, 0)
        broadcast(1, diagl[0], 4)
        broadcast(2, diagl[1], 6)
        in_pair(14, 0)
        pe.wait_ge(sem["ada_acc"], KD + 1)
        pe.wait_ge(sem["low_done"], 5)
        for m in range(32):
            last = mm(ps[:, 4, m:m + 1], acc2[:, m * P:(m + 1) * P], ones[:, 0:1], start=True, stop=True)
        last.then_inc(sem["mod2_mm"], 1)
        in_pair(16, 0)

        def turn(tt, s):
            pe.wait_ge(sem["work_done"], after(tt))
            pe.wait_ge(sem["kv_free"], 5 * tt + 5 + PRIME)
            pe.wait_ge(sem["t_act"], 2 * tt + PRIME)
            pe.wait_ge(sem["t_dve"], after(tt - 1))
            w = work[s]
            for h in range(MH):
                nc.tensor.transpose(ps[:, 4, h * P:(h + 1) * P], w[:, QK * h:QK * h + P], ident[:])
                o = 768 if h == 0 else 896 + 128 * h
                nc.tensor.transpose(ps[:, 5, h * P:(h + 1) * P], w[:, o:o + P], ident[:])
            for g in range(3):
                last = nc.tensor.transpose(ps[:, 6, g * P:(g + 1) * P], rot[s][:, 2 * g:2 * g + 2, :].rearrange("p h n -> p (h n)"), ident[:])
            last.then_inc(sem["tr_done"], 1)

        def up_tile(tt, s, first=False):
            pe.wait_ge(sem["ll_done"], after(tt))
            pe.wait_ge(sem["q_free"], 4 * tt + PRIME)
            for k in range(3):
                for c in range(2):
                    last = three(ps[:, c, 0:384], LH[s][:, k, :], LL[s][:, k, :], UQH[:, k, 384 * c:384 * (c + 1)], UQL[:, k, 384 * c:384 * (c + 1)], k == 0, k == 2)
            last.then_inc(sem["q_mm"], 1)
            pe.wait_ge(sem["kv_free"], 5 * tt + PRIME)
            pe.wait_ge(sem["kr_free"], after(tt - 1))
            nc.tensor.transpose(ps[:, 7, 0:P], krT(tt), ident[:])
            for k in range(2):
                for c in range(2):
                    last = three(ps[:, 2 + c, :], LH[s][:, 3 + k, :], LL[s][:, 3 + k, :], UKH[:, k, 512 * c:512 * (c + 1)], UKL[:, k, 512 * c:512 * (c + 1)], k == 0, k == 1)
            last.then_inc(sem["kv_mm"], 1)
            if not first:
                turn(tt - 1, 1 - s)

        def krT(tt):
            return lowT[:, 5, bass.ds(tt * P, P)]

        for tt in range(NT):
            up_tile(tt, tt % 2, first=(tt == 0))
        turn(NT - 1, 1)
        for tt in range(NT):
            if tt < 2:
                pe.wait_ge(sem["q_free"], 4 * NT + PRIME)
            else:
                pe.wait_ge(sem["vt_odd"] if tt % 2 else sem["vt_even"], tt // 2)
            for c in range(4):
                last = nc.tensor.transpose(ps[:, tt % 2, c * P:(c + 1) * P], vT[:, c, tt * P:(tt + 1) * P], ident[:])
            last.then_inc(sem["vt_mm"], 1)

        wready = {"m": ("m_exp",), "s": ("s_wd", "s_wp")}
        sfree = {"m": "m_exp", "s": "s_b"}

        def mla_scores(p, e, q0, out, k0, w, diagonal):
            q, k = slice(q0, q0 + P), slice(k0, k0 + w)
            three(out, mqH[e][:, q], mqL[e][:, q], mkH[e][:, k], mkL[e][:, k], True, False)
            last = three(out, mrH[p][:, q], mrL[p][:, q], KRH[e][:, k], KRL[e][:, k], False, not diagonal)
            if diagonal:
                last = mm(out[:, 0:P], identb[:], mask_mla[:], start=False, stop=True)
            return last

        def stick_scores(p, e, q0, out, k0, w, diagonal):
            q, k = slice(q0, q0 + P), slice(k0, k0 + w)
            last = three(out, sqH[e][:, q], sqL[e][:, q], skH[e][:, k], skL[e][:, k], True, not diagonal)
            if diagonal:
                last = mm(out[:, 0:P], identb[:], mask_sb[:], start=False, stop=True)
            return last

        def qk(pre, i, v, scores):
            (e, qt), n = UNITS[v], BLOCKS[v] * P
            for c0 in range(0, n, 512):
                w = min(512, n - c0)
                last = scores(i, e, qt * P, ps[:, 2 * (v % 2) + c0 // 512, 0:w], qt * P + c0, w, c0 == 0)
            last.then_inc(sem[pre + "_qk"], 1)

        def attention(pre, i, scores, src, dst, V, width, split_done, ahead):
            def turn_unit(v):
                u, b = i * NU + v, BLOCKS[v]
                for w in wready[pre]:
                    pe.wait_ge(sem[w], after(u))
                pe.wait_ge(sem[pre + "_ta"], after(u - 1))
                pe.wait_ge(sem[pre + "_tv"], i * NG1 + G1_BEFORE[v] + PRIME)
                for k in range(b):
                    bank, c = (4, k) if k < G0[v] else (5, k - G0[v])
                    last = nc.tensor.transpose(ps[:, bank, c * P:(c + 1) * P], src[v % 2][:, k * P:(k + 1) * P], ident[:])
                last.then_inc(sem[pre + "_tr"], 1)

            def values(v):
                u, b = i * NU + v, BLOCKS[v]
                e, qt = UNITS[v]
                pe.wait_ge(sem[pre + "_o"], after(u - 2))
                pe.wait_ge(sem[pre + "_ta"], after(u))
                if b > 1:
                    pe.wait_ge(sem[pre + "_tv"], i * NG1 + G1_BEFORE[v + 1] + PRIME)
                for k in range(b):
                    last = mm(ps[:, 6 + v % 2, 0:width], dst[v % 2][:, k * P:(k + 1) * P],
                              V[:, qt + k, bass.ds((2 * i + e) * width, width)], start=(k == 0), stop=(k == b - 1))
                last.then_inc(sem[pre + "_av"], 1)

            for v in range(NU):
                if v + 2 < NU:
                    if v + 2 == NU // 2:
                        pe.wait_ge(sem[pre + "_l"], split_done)
                    pe.wait_ge(sem[sfree[pre]], after(i * NU + v))
                    qk(pre, i, v + 2, scores)
                elif ahead:
                    pe.wait_ge(sem[sfree[pre]], after(i * NU + v))
                    ahead(v)
                turn_unit(v)
                if v >= 1:
                    values(v - 1)
            values(NU - 1)

        pe.wait_ge(sem["kr_zero"], 4)
        pe.wait_ge(sem["kr_l"], 2)
        pe.wait_ge(sem["m_l"], 3)
        for v in range(2):
            qk("m", 0, v, mla_scores)

        def mla_ahead(v):
            pe.wait_ge(sem["m_l"], 8)
            qk("m", 1, v + 2 - NU, mla_scores)

        def stick_ahead(i):
            def first(v):
                pe.wait_ge(sem["s_l"], 4 * i + 2)
                qk("s", i, v + 2 - NU, stick_scores)
            return first

        def stick_first(v):
            pe.wait_ge(sem["sk_zero"], 2)
            stick_ahead(0)(v)

        attention("m", 0, mla_scores, pm, pmT, VM, VD, 5, mla_ahead)
        attention("m", 1, mla_scores, pm, pmT, VM, VD, 10, stick_first)
        pe.wait_ge(sem["sk_zero"], 4)
        with pe.Fori(0, SBH // 2 - 1) as i:
            attention("s", i, stick_scores, beta, wT, VS, SBD, 4 * i + 4, stick_ahead(i + 1))
        i = SBH // 2 - 1
        attention("s", i, stick_scores, beta, wT, VS, SBD, 4 * i + 4, None)

        def mix(tt):
            pe.wait_ge(sem["o_scaled"], 2 * tt + 2)
            if tt >= 2:
                pe.wait_ge(sem["mix_l"], tt - 1)
            for c in range(8):
                last = nc.tensor.transpose(ps[:, 2 * (tt % 2) + c // 4, c % 4 * P:(c % 4 + 1) * P], ostage[tt % 2][:, c // 4, c % 4 * P:(c % 4 + 1) * P], ident[:])
            last.then_inc(sem["o_mm"], 1)

        for tt in range(NT // 2 + 1):
            mix(tt)

        mix_at = {(0, 4): 5, (1, 0): 6, (1, 4): 7}
        pe.wait_ge(sem["split_l"], raw_index(H_OUT) + 2)
        for hf in range(2):
            pe.wait_ge(sem["mix_l"], (hf + 1) * NT // 2)
            for u in range(2):
                for j in range(KD):
                    if hf == 0 and (u, j) in mix_at:
                        mix(mix_at[u, j])
                    last = half_chunk(u, 4 + 2 * u, hf, j, mixH, mixL)
                if hf == 1:
                    last.then_inc(sem["pe_tile"], 1)

        def out_pair(i):
            for u in range(2):
                t = 2 + 2 * i + u
                pe.wait_ge(sem["x2_done"], after(t - 2))
                proj_tile(H_OUT + t, H_OUT + 2 + u, 2 * u, mixH, mixL)
        repeat(pe, N_OUT // 2 - 2, out_pair)

        def residual_sums(hf):
            t0, t1 = 4 * hf, 4 * hf + 4
            pe.wait_ge(sem["sqa_done"], after(N_OUT - 2 + hf))
            token_sums(4 + hf, sqa, True, False, t0, t1)
            pe.wait_ge(sem["x2_sq"], N_OUT - 2 + 2 * hf + 2)
            token_sums(4 + hf, sq2[1], False, True, t0, t1).then_inc(sem["r2_mm"], 1)

        for hf in range(2):
            for u in range(2):
                if hf == 0:
                    pe.wait_ge(sem["split_l"], raw_index(H_OUT) + N_OUT - 1 + u)
                    pe.wait_ge(sem["x2_done"], after(N_OUT - 4 + u))
                for j in range(KD):
                    if (hf, u, j) == (1, 0, 3):
                        residual_sums(0)
                    if (hf, u, j) == (1, 1, 2):
                        broadcast(3, diag2, 6, (0,))
                    last = half_chunk(u, 2 * u, hf, j, mixH, mixL)
                last.then_inc(sem["pe_tile" if hf else "half_mm"], 1)

        for hf in range(2):
            for n in range(KD + LAG):
                if (hf, n) == (0, 3):
                    residual_sums(1)
                if (hf, n) == (0, 6):
                    broadcast(4, diag2, 6, (1,))
                if n < KD:
                    if n == 0:
                        pe.wait_ge(sem["split_l"], raw_index(H_GU) + 1)
                        pe.wait_ge(sem["x2_half"], 1 + 2 * hf)
                    pe.wait_ge(sem["h2L_done"], hf * KD + n + 1)
                    last = half_chunk(0, 0, hf, n, h2H, h2L)
                    if hf == 1 and n == KD - 1:
                        last.then_inc(sem["pe_tile"], 1)
                if n >= LAG:
                    if n == LAG:
                        pe.wait_ge(sem["split_l"], raw_index(H_GU) + 2)
                        pe.wait_ge(sem["x2_half"], 2 + 2 * hf)
                    last = half_chunk(1, 2, hf, n - LAG, h2H, h2L)
        last.then_inc(sem["pe_tile"], 1)

        def gate(f, f0, i):
            if f0 == 0:
                return
            b = 4 * (f0 % 2)
            pe.wait_ge(sem["silu_done"], after(f - 2))
            proj_tile(H_GU + 2 * f, H_GU + 2 * f0, b, h2H, h2L)
            pe.wait_ge(sem["t_done"], after(f - 2))
            proj_tile(H_GU + 2 * f + 1, H_GU + 2 * f0 + 1, b + 2, h2H, h2L)
        ffn_tiles(pe, gate)
        pe.wait_ge(sem["t_done"], after(NF - 1))

        def down_tile(hf, d, par, first=False, last_=False):
            pe.wait_ge(sem["split_l"], H_DN + d + N_UP + 1)
            pe.wait_ge(sem["tl_done"], d + 1)
            s = par % 2
            for o in range(KD):
                if first and hf == 1:
                    pe.wait_ge(sem["y_done"], o + 1)
                w = slice(o * P, (o + 1) * P)
                last = three(ps[:, o, :], WH[s][:, w], WL[s][:, w], TH[s][:], TL[s][:], first, last_)
                if last_ and o < KD - 1:
                    last.then_inc(sem["d_mm"], 1)
            last.then_inc(sem["pe_tile"], 1)

        for hf in range(2):
            d0 = hf * NF
            down_tile(hf, d0, H_DN, first=True)
            down_tile(hf, d0 + 1, H_DN + 1)

            def down(i, hf=hf, d0=d0):
                for u in range(2):
                    down_tile(hf, d0 + 2 + 2 * i + u, H_DN + u)
            repeat(pe, NF // 2 - 2, down)
            down_tile(hf, d0 + NF - 2, H_DN)
            down_tile(hf, d0 + NF - 1, H_DN + 1, last_=True)
    ctx.close()


def kernel(**inputs):
    import concourse.bacc as bacc
    from concourse.bass_utils import run_bass_kernel_spmd as run

    g = {k: np.asarray(v) for k, v in inputs.items()}

    def col(v):
        return v.reshape(-1, P).T

    c = np.ascontiguousarray
    win = g["w_in"][0].reshape(KD, P, -1)
    arrays = {
        "xT": c(g["x"][0, ::-1].T.reshape(KD, P, S)),
        "cols": c(np.concatenate([col(g["c"][0]), col(g["b_ada"][0]), col(g["norm_attn"][0]), col(g["norm_ffn"][0]),
                                  col(g["q_a_norm"][0]), col(g["kv_a_norm"][0]), col(g["k_nope_norm"][0])], axis=1)),
        "rows": c(np.broadcast_to(np.concatenate([g["q_norm"][0], g["k_rope_norm"][0],
                                                  (1.0 / (10000.0 ** (np.arange(HALF, dtype=np.float32) / HALF))).astype(np.float32)]), (P, NROW))),
        "grow": c(np.broadcast_to(np.stack([g["out_norm_sb"][0], g["out_norm_mla"][0]]), (P, 2, 512))),
        "pos": c(g["positions"][0, ::-1].reshape(NT, P).T),
        "ada1": c(g["w_ada"][0][:, 0:2 * D].reshape(KD, P, 2, KD // 2, 2 * P).transpose(3, 1, 0, 2, 4).reshape(KD // 2, P, KD, 4 * P)),
        "ada2": c(g["w_ada"][0][:, 2 * D:].reshape(KD, P, 4 * D)),
        "win": c(np.stack([win[:, :, w:w + P].transpose(1, 0, 2).reshape(P, D) for w in W_COLS])),
        "qup": c(g["w_q_up"][0].reshape(3, P, MH * QK)),
        "kvup": c(g["w_kv_up"][0].reshape(2, P, D)),
        "wout": c(g["w_out"][0].reshape(KD, P, KD, P).transpose(2, 1, 0, 3).reshape(KD, P, D)),
        "gu": c(np.stack([g["w_gate"][0], g["w_up"][0]]).reshape(2, KD, P, NF, P).transpose(3, 0, 2, 1, 4).reshape(2 * NF, P, D)),
        "down": c(g["w_down"][0].reshape(NF, P, D)),
    }
    nc = bacc.Bacc("TRN2", target_bir_lowering=False, num_devices=1)
    aps = {k: nc.dram_tensor(k, v.shape, mybir.dt.from_np(v.dtype), kind="ExternalInput").ap() for k, v in arrays.items()}
    x2_d = nc.dram_tensor("x2_spill_d", (KD, P, S), F32, kind="Internal").ap()
    out = nc.dram_tensor("out", (KD, P, S), F32, kind="ExternalOutput").ap()
    build(nc, aps["xT"], aps["cols"], aps["rows"], aps["grow"], aps["pos"], aps["ada1"], aps["ada2"], aps["win"], aps["qup"],
          aps["kvup"], aps["wout"], aps["gu"], aps["down"], x2_d, out)
    r = run(nc, [arrays], core_ids=[0])
    return c(r.results[0]["out"].reshape(D, S).T[::-1][None])
```

```python
import numpy as np
from contextlib import ExitStack
import concourse.bass as bass
from concourse import mybir

F32 = mybir.dt.float32
F32R = mybir.dt.float32r
BF16 = mybir.dt.bfloat16
I32 = mybir.dt.int32
ALU = mybir.AluOpType
ACT = mybir.ActivationFunctionType
AX = mybir.AxisListType

P = 128
S = 1024
D = 1024
NT = S // P
KD = D // P
SBH, SBD = 8, 64
MH, NOPE, ROPE, VD = 4, 128, 64, 128
QK = NOPE + ROPE
QR, KVR = 384, 256
DFF = 2816
NF = DFF // P
EPS = 1e-6
HALF = ROPE // 2
NEG = -1e30
PRIME = 2

C_C, C_B, C_GA, C_GF, C_QA, C_KVA, C_KN = 0, 8, 56, 64, 72, 75, 77
NCOL = 78
R_Q, R_KR, R_FREQ = 0, QK, QK + ROPE
NROW = R_FREQ + HALF

W_COLS = [1536, 1664, 1792, 1920, 2048, 2112] + [128 * t for t in range(12)]
N_IN = len(W_COLS)
N_UP = 5
N_OUT = KD
H_OUT = N_IN
H_GU = H_OUT + N_OUT
H_DN = H_GU + 2 * NF


def raw_index(h):
    return h if h < N_IN else h + N_UP


class Chain:

    def __init__(self, eng, sem):
        self.eng, self.sem, self.base, self.n, self.at = eng, sem, 0, 0, 0

    def __call__(self, instruction):
        instruction.then_inc(self.sem, 1)
        self.n += 1
        return instruction

    def sync(self):
        self.eng.wait_ge(self.sem, self.at + self.n)

    def begin(self, i, per):
        self.base, self.n = self.base + self.n, 0
        self.at = self.base + i * per

    def end(self, times, per):
        assert self.n == per, (self.n, per)
        self.base, self.n = self.base + times * per, 0
        self.at = self.base


ORDER0 = [7, 1, 5, 3, 2, 4, 0, 6]
ORDER1 = [6, 0, 4, 2, 3, 5, 1, 7]
UNITS = [(0, i) for i in ORDER0] + [(1, i) for i in ORDER1]
NU = len(UNITS)
LAG = 3
BLOCKS = [NT - i for _, i in UNITS]
G0 = [(b + 1) // 2 for b in BLOCKS]
G1_BEFORE = [sum(b > 1 for b in BLOCKS[:k]) for k in range(NU + 1)]
NG1 = G1_BEFORE[NU]
SPLIT1, SPLIT0 = 2, 12
SB_EARLY = 5


def build(nc, xT, cols_d, rows_d, grow_d, pos_d, ada1_d, ada2_d, win_d, qup_d, kvup_d, wout_d, gu_d, down_d, x2_d, out_d):
    ctx = ExitStack()
    base = 16512

    def at(name, shape, dt, kb):
        return nc.alloc_sbuf_tensor_at(name, shape, dt, offset=base + int(kb * 1024))

    ident = at("ident", [P, P], F32, 0)
    identb = at("identb", [P, P], BF16, 0.5)
    mask_sb = at("mask_sb", [P, P], BF16, 0.75)
    mask_mla = at("mask_mla", [P, P], BF16, 1.0)
    ones = at("ones", [P, P], F32, 1.5)
    cols = at("cols", [P, NCOL], F32, 2.0)
    rows = at("rows", [P, NROW], F32, 2.5)
    pos_i = at("pos_i", [P, NT], I32, 4.0)
    pos_f = at("pos_f", [P, NT], F32, 4.03125)
    trig = at("trig", [P, NT, 2, HALF], F32, 4.125)
    silu_c = at("silu_c", [P, KD], F32, 6.125)
    mod1 = at("mod1", [P, 16], F32, 6.25)
    a1 = at("a1", [P, KD], F32, 6.375)
    mod2 = at("mod2", [P, 32], F32, 6.5)
    a2 = at("a2", [P, KD], F32, 6.75)
    ssq = at("ssq", [P, 2, 16], F32, 7.0)
    rstd = at("rstd", [P, 2, 16], F32, 7.25)
    mx = at("mx", [P, NU], F32, 7.5)
    nmx = at("nmx", [P, NU], F32, 7.625)
    lss = at("lss", [P, 2, NT], F32, 9.0)
    rss = at("rss", [P, NT], F32, 9.0625)
    qms = at("qms", [P, 2, 16], F32, 8.125)
    den = at("den", [P, NU], F32, 7.75)
    rden = at("rden", [P, NU], F32, 7.875)
    oss = at("oss", [P, NT, 2], F32, 8.5)
    oms = at("oms", [P, NT, 2], F32, 8.5625)
    ors = at("ors", [P, NT, 2], F32, 8.625)
    nhalf = at("nhalf", [P, 16], F32, 9.75)
    ms = at("ms", [P, 4, NT], F32, 9.8125)
    rms = at("rms", [P, 4, NT], F32, 8.25)
    WH = [at(f"WH{s}", [P, D], F32R, 10 + 8 * s) for s in range(2)]
    WL = [at(f"WL{s}", [P, D], F32R, 14 + 8 * s) for s in range(2)]
    raw = [at(f"raw{s}", [P, D], F32, 26 + 4 * s) for s in range(2)]
    hH = at("hH", [P, KD, S], F32R, 142)
    hL = at("hL", [P, KD, S], F32R, 174)
    qkT = at("qkT", [P, 8, S], F32, 34)
    vT = at("vT", [P, 4, S], F32, 66)
    lowT = at("lowT", [P, 6, S], F32, 82)
    ada1 = at("ada1", [P, KD // 2, KD, 4 * P], F32, 34)
    acc1 = [at(f"acc1{s}", [P, 4 * P], F32, 102 + 2 * s) for s in range(2)]
    sqs = at("sqs", [P, S], F32, 194)
    x_in = at("x_in", [P, KD, S], F32, 106)
    sq = [at(f"sq{s}", [P, S], F32, 198 + 4 * s) for s in range(2)]
    diag1 = at("diag1", [P, NT, P], F32, 98)
    ang = at("ang", [P, NT, 2, HALF], F32, 190)
    turns = at("turns", [P, NT, 2, HALF], F32, 192)
    ada2 = at("ada2", [P, 4 * D], F32, 106)
    acc2 = at("acc2", [P, 4 * D], F32, 122)
    sql = [at(f"sql{s}", [P, S], F32, 66 + 4 * s) for s in range(3)]
    diagl = [at("diagl0", [P, NT, P], F32, 138), at("diagl1", [P, NT, P], F32, 78)]
    UQH = at("UQH", [P, 3, MH * QK], F32R, 106)
    UQL = at("UQL", [P, 3, MH * QK], F32R, 115)
    UKH = at("UKH", [P, 2, D], F32R, 124)
    UKL = at("UKL", [P, 2, D], F32R, 132)
    LH = [at(f"LH{s}", [P, 5, P], F32R, 10 + 2.5 * s) for s in range(2)]
    LL = [at(f"LL{s}", [P, 5, P], F32R, 15 + 2.5 * s) for s in range(2)]
    work = [at(f"work{s}", [P, 1408], F32, 20 + 5.5 * s) for s in range(2)]
    ksq = at("ksq", [P, 9 * ROPE], F32, 202)
    rot = [at("rot0", [P, 6, ROPE], F32, 140), at("rot1", [P, 6, ROPE], F32, 206)]
    rope_c = at("rope_c", [P, 5, 2, HALF], F32, 31)
    rope_s = at("rope_s", [P, 5, 2, HALF], F32, 32.25)
    QN = at("QN", [P, MH, S], F32, 142)
    KN = at("KN", [P, MH, S], F32, 158)
    VM = at("VM", [P, NT, MH * VD], F32, 174)
    QRK = at("QRK", [P, 3, S], F32, 190)
    VS = at("VS", [P, NT, SBH * SBD], F32, 82)
    pm = [at(f"pm{s}", [P, S], F32, 10 + 4 * s) for s in range(2)]
    pmT = [at(f"pmT{s}", [P, S], F32, 18 + 4 * s) for s in range(2)]
    KRH = [at("KRH0", [P, S], F32R, 26), at("KRH1", [P, S], F32R, 98)]
    KRL = [at("KRL0", [P, S], F32R, 30), at("KRL1", [P, S], F32R, 102)]
    mqH = [at(f"mqH{e}", [P, S], F32R, 106 + 16 * e) for e in range(2)]
    mqL = [at(f"mqL{e}", [P, S], F32R, 110 + 16 * e) for e in range(2)]
    mkH = [at(f"mkH{e}", [P, S], F32R, 114 + 16 * e) for e in range(2)]
    mkL = [at(f"mkL{e}", [P, S], F32R, 118 + 16 * e) for e in range(2)]
    mrH = [at("mrH0", [P, S], F32R, 138), at("mrH1", [P, S], F32R, 142)]
    mrL = [at("mrL0", [P, S], F32R, 202), at("mrL1", [P, S], F32R, 158)]
    o_mla = at("o_mla", [P, NT, MH * VD], F32, 66)
    skH = [at(f"skH{e}", [P, S], F32R, 106 + 16 * e) for e in range(2)]
    skL = [at(f"skL{e}", [P, S], F32R, 110 + 16 * e) for e in range(2)]
    sqH = [at(f"sqH{e}", [P, S], F32R, 114 + 16 * e) for e in range(2)]
    sqL = [at(f"sqL{e}", [P, S], F32R, 118 + 16 * e) for e in range(2)]
    beta = [at(f"beta{s}", [P, S], F32, 142 + 4 * s) for s in range(2)]
    omb = [at(f"omb{s}", [P, S], F32, 150 + 4 * s) for s in range(2)]
    left = [at(f"left{s}", [P, S + 8], F32, 158 + 4.5 * s) for s in range(2)]
    wT = [at(f"wT{s}", [P, S], F32, 167 + 4 * s) for s in range(2)]
    grow = at("grow", [P, 2, 512], F32, 176)
    o_sb = at("o_sb", [P, NT, SBH * SBD], F32, 190)
    mixH = at("mixH", [P, KD, S], F32R, 82)
    mixL = at("mixL", [P, KD, S], F32R, 114)
    junk = at("junk", [P, 512], F32, 98)
    ostage = [at(f"ostage{s}", [P, 2, 512], F32, 148 + 4 * s) for s in range(2)]
    x2 = at("x2", [P, KD, S], F32, 34)
    sq2 = [at(f"sq2{s}", [P, S], F32, 66 + 4 * s) for s in range(2)]
    sqa = at("sqa", [P, S], F32, 74)
    diag2 = at("diag2", [P, NT, P], F32, 78)
    xn2 = [at(f"xn2{s}", [P, 512], F32, 82 + 4 * s) for s in range(2)]
    h2H = at("h2H", [P, KD, S], F32R, 142)
    h2L = at("h2L", [P, KD, S], F32R, 174)
    t_all = at("t_all", [P, NF, S], F32, 34)
    gs = [at(f"gs{s}", [P, S], F32, 122 + 4 * s) for s in range(2)]
    TH = [at(f"TH{s}", [P, 512], F32R, 130 + 2 * s) for s in range(2)]
    TL = [at(f"TL{s}", [P, 512], F32R, 134 + 2 * s) for s in range(2)]
    xres = at("xres", [P, KD, 512], F32, 142)
    yst = at("yst", [P, KD, 512], F32, 158)

    ps = ctx.enter_context(nc.psum_tensor("ps", [P, 8, 512], F32))

    def pair(b, n=S):
        return ps[:, b:b + 2, :].rearrange("p b n -> p (b n)")[:, 0:n]

    names = """small_in pool_const trig_args trig_done silu_c_done x_sq x_add x_turned stat_ms stat_r stat_diag stat_bc acc1_done mod1_mm a1_done
        xr_done h_done hH_done hL_done split_h split_l pe_tile in_evac ada2_in ada_acc mod2_mm mod2_sum low_sq low_add low_mm low_done
        dve lh_done ll_done q_mm kv_mm q_sq k_sq q_ms q_r k_ms q_free kr_free rk_done kv_free k_scaled work_done tr_done
        t_act t_dve vt_mm vt_even vt_odd low_over kr_zero left_one kr_h kr_l
        m_h m_l m_qk m_max m_nm m_exp m_tr m_ta m_tv m_av m_o
        sk_zero s_h s_l s_qk s_nb s_b s_scan s_wd s_wp s_tr s_ta s_tv s_av s_o
        grow_in o_sq o_ms o_r o_scaled o_mm mix_h mix_l x2_in sqa_zero sqa_done x2_done x2_half half_mm x2_sq x2_spill r2_mm xn2_done h2H_done
        h2L_done silu_done t_done th_done tl_done d_mm xres_in y_done y_out""".split()
    sem = {n: ctx.enter_context(nc.semaphore(n)) for n in names}
    ada1_in = [ctx.enter_context(nc.semaphore(f"ada1_in{k}")) for k in range(KD // 2)]
    xin_in = [ctx.enter_context(nc.semaphore(f"xin_in{k}")) for k in range(4)]
    raw_in = [ctx.enter_context(nc.semaphore(f"raw_in{k}")) for k in range(2)]

    block = ctx.enter_context(nc.Block())

    def after(n):
        return n + 1 + PRIME

    def one(ap):
        return ap.rearrange("p o n -> p (o n)")

    def dve_share(n):
        return n // 2

    def mix_banks(tt):
        b = 2 * (tt % 2)
        return ps[:, b:b + 2, :].rearrange("p b (j n) -> p (b j) n", j=4)

    SEGMENTS = [(0, 1), (2, 2), (6, 1), (8, 1), (10, 1), (12, 1), (14, 1), (16, 1)]

    def ffn_tiles(eng, tile):
        tile(0, 0, 0)
        with eng.Fori(0, (NF - 2) // 2) as i:
            for u in range(2):
                tile(1 + u + 2 * i, 1 + u, i)
        tile(NF - 1, NF - 1, 0)

    def repeat(eng, n, body):
        if n == 1:
            body(0)
        else:
            with eng.Fori(0, n) as i:
                body(i)

    @block.sync
    def _(sp):
        def load_raw(r, par, i, src):
            if not (isinstance(r, int) and r < 2):
                sp.wait_ge(sem["split_h"], r - 1)
                sp.wait_ge(sem["split_l"], r - 1)
            sp.dma_start(raw[par % 2][:, 0:src.shape[-1]], src).then_inc(raw_in[par % 2], 16)

        sp.dma_start(cols[:], cols_d).then_inc(sem["small_in"], 16)
        sp.dma_start(rows[:], rows_d).then_inc(sem["small_in"], 16)
        sp.dma_start(pos_i[:], pos_d).then_inc(sem["small_in"], 16)
        for k in range(4):
            sp.dma_start(x_in[:, 2 * k:2 * k + 2, :], xT[2 * k:2 * k + 2].rearrange("j p n -> p j n")).then_inc(xin_in[k], 16)
        for j in range(2):
            load_raw(j, j, 0, win_d[j])
        for g in range(KD // 2):
            sp.dma_start(ada1[:, g], ada1_d[g]).then_inc(ada1_in[g], 16)
        step = 0
        for t0, n in SEGMENTS[:-1]:
            def body(i, t0=t0, step=step):
                for u in range(2):
                    load_raw(t0 + 2 + 2 * i + u, t0 + u, i, one(win_d[bass.ds(t0 + 2 + 2 * i + u, 1)].rearrange("o p n -> p o n")))
                sp.wait_ge(sem["ada_acc"], step + i + 1)
                sp.dma_start(ada2[:], one(ada2_d[bass.ds(step + i, 1)].rearrange("o p n -> p o n"))).then_inc(sem["ada2_in"], 16)
            repeat(sp, n, body)
            step += n
        for k in range(3):
            load_raw(N_IN + k, N_IN + k, 0, qup_d[k])
        for k in range(2):
            load_raw(N_IN + 3 + k, N_IN + 3 + k, 0, kvup_d[k])
        sp.wait_ge(sem["m_av"], after(2 * NU - 1))
        sp.dma_start(grow[:], grow_d).then_inc(sem["grow_in"], 16)
        for u in range(2):
            load_raw(raw_index(H_OUT) + u, raw_index(H_OUT) + u, 0, wout_d[u])
        sp.wait_ge(sem["s_h"], 2 * SBH)
        sp.wait_ge(sem["s_l"], 2 * SBH)
        sp.dma_start(x2[:], xT.rearrange("j p n -> p j n")).then_inc(sem["x2_in"], 16)
        with sp.Fori(0, N_OUT // 2 - 1) as i:
            for u in range(2):
                r = raw_index(H_OUT) + 2 + u
                load_raw(r + 2 * i, r, i, one(wout_d[bass.ds(2 + u + 2 * i, 1)].rearrange("o p n -> p o n")))
        for u in range(2):
            r = raw_index(H_GU) + u
            load_raw(r, r, 0, gu_d[u])
        sp.wait_ge(sem["x2_half"], 4)
        sp.dma_start(x2_d.rearrange("j p n -> p j n"), x2[:]).then_inc(sem["x2_spill"], 16)
        with sp.Fori(0, NF - 1) as i:
            for u in range(2):
                r = raw_index(H_GU) + 2 + u
                load_raw(r + 2 * i, r, i, one(gu_d[bass.ds(2 + u + 2 * i, 1)].rearrange("o p n -> p o n")))
        for hf in range(2):
            with sp.Fori(0, NF // 2) as i:
                for u in range(2):
                    r = raw_index(H_DN) + hf * NF + u
                    load_raw(r + 2 * i, r, i, one(down_d[bass.ds(u + 2 * i, 1)].rearrange("o p n -> p o n")))

    @block.gpsimd
    def _(pool):
        for n in ("s_wp", "q_r", "rk_done"):
            pool.sem_inc(sem[n], PRIME)
        k = 0

        def fill(ins):
            nonlocal k
            ins.then_inc(sem["pool_const"], 1)
            k += 1

        fill(pool.memset(ident[:], 0.0))
        fill(pool.memset(identb[:], 0.0))
        fill(pool.memset(mask_sb[:], 0.0))
        fill(pool.memset(mask_mla[:], 0.0))
        fill(pool.memset(ones[:], 1.0))
        fill(pool.memset(nhalf[:], -0.5))
        pool.wait_ge(sem["pool_const"], k)
        for m in (ident, identb):
            fill(pool.affine_select(out=m[:], in_=m[:], compare_op=ALU.not_equal, fill=1.0, base=0, pattern=[[-1, P]], channel_multiplier=1))
        fill(pool.affine_select(out=mask_sb[:], in_=mask_sb[:], compare_op=ALU.is_gt, fill=NEG, base=0, pattern=[[1, P]], channel_multiplier=-1))
        fill(pool.affine_select(out=mask_mla[:], in_=mask_mla[:], compare_op=ALU.is_ge, fill=NEG, base=0, pattern=[[1, P]], channel_multiplier=-1))

        def rsqrt(k, row, t0=0, t1=NT):
            pool.wait_ge(sem["stat_ms"], k + 1)
            nc.gpsimd.tensor_tensor(rms[:, row, t0:t1], ms[:, row, t0:t1], nhalf[:, t0:t1], ALU.pow).then_inc(sem["stat_r"], 1)

        pool.wait_ge(sem["pool_const"], k)
        rsqrt(0, 0)
        for j in range(KD):
            pool.wait_ge(sem["hH_done"], j + 1)
            nc.gpsimd.tensor_tensor(hL[:, j, :], x_in[:, j, :], hH[:, j, :], ALU.subtract).then_inc(sem["hL_done"], 1)
        pool.wait_ge(sem["hL_done"], KD)
        pool.memset(acc2[:], 0.0).then_inc(sem["ada_acc"], 1)
        for k, (a, b) in enumerate(((0, 1), (0, 2), (1, 2))):
            pool.wait_ge(sem["low_sq"], (2, 3, 5)[k])
            if k:
                pool.wait_ge(sem["low_add"], k)
            nc.gpsimd.tensor_tensor(sql[a][:], sql[a][:], sql[b][:], ALU.add).then_inc(sem["low_add"], 1)
        rsqrt(1, 1)
        rsqrt(2, 2)

        def head_rsqrt(i):
            for u in range(2):
                tt = 2 * i + u
                pool.wait_ge(sem["q_ms"], tt + 1)
                nc.gpsimd.tensor_tensor(rstd[:, u, 0:4], qms[:, u, 0:4], nhalf[:, 0:4], ALU.pow).then_inc(sem["q_r"], 1)
                pool.wait_ge(sem["k_ms"], tt + 1)
                nc.gpsimd.tensor_tensor(rstd[:, u, 4:9], qms[:, u, 4:9], nhalf[:, 0:5], ALU.pow).then_inc(sem["rk_done"], 1)
        repeat(pool, NT // 2, head_rsqrt)
        pool.wait_ge(sem["low_over"], 1)
        for e in range(2):
            o = 64 * (1 - e)
            pool.memset(KRH[e][o:o + 64, :].bitcast(F32), 0.0).then_inc(sem["kr_zero"], 1)
            pool.memset(KRL[e][o:o + 64, :].bitcast(F32), 0.0).then_inc(sem["kr_zero"], 1)
        for e, u in ((0, NU + 7), (1, 2 * NU - 1)):
            pool.wait_ge(sem["m_qk"], after(u))
            o = 64 * (1 - e)
            pool.memset(skH[e][o:o + 64, :].bitcast(F32), 0.0).then_inc(sem["sk_zero"], 1)
            pool.memset(skL[e][o:o + 64, :].bitcast(F32), 0.0).then_inc(sem["sk_zero"], 1)
            pool.wait_ge(sem["sk_zero"], 2 * e + 2)
        for s in range(2):
            pool.memset(left[s][:, 0:1], 1.0).then_inc(sem["left_one"], 1)
        pool.wait_ge(sem["left_one"], 2)

        def weights(i):
            for v, b in enumerate(BLOCKS):
                n, u = b * P, i * NU + v
                pool.wait_ge(sem["s_scan"], after(u))
                pool.wait_ge(sem["s_b"], after(u))
                c = dve_share(n)
                nc.gpsimd.tensor_tensor(beta[v % 2][:, c:n], beta[v % 2][:, c:n], left[v % 2][:, c:n], ALU.mult).then_inc(sem["s_wp"], 1)
        repeat(pool, 4, weights)
        for tt in range(NT):
            pool.wait_ge(sem["o_ms"], tt + 1)
            nc.gpsimd.tensor_tensor(ors[:, ORDER1[tt], :], oms[:, ORDER1[tt], :], nhalf[:, 0:2], ALU.pow).then_inc(sem["o_r"], 1)
        pool.wait_ge(sem["mix_l"], NT)
        pool.memset(sqa[:], 0.0).then_inc(sem["sqa_zero"], 1)
        for hf in range(2):
            rsqrt(3 + hf, 3, 4 * hf, 4 * hf + 4)
        for hf in range(2):
            if hf == 0:
                pool.wait_ge(sem["pe_tile"], after(H_DN - 1))
                pool.wait_ge(sem["x2_spill"], 16)
            else:
                pool.wait_ge(sem["y_done"], KD)
            pool.dma_start(xres[:], x2_d[:, :, 512 * hf:512 * hf + 512].rearrange("j p n -> p j n")).then_inc(sem["xres_in"], 16)
            for o in range(KD):
                pool.wait_ge(sem["y_done"], hf * KD + o + 1)
                pool.dma_start(out_d[o, :, 512 * hf:512 * hf + 512], yst[:, o, :]).then_inc(sem["y_out"], 16)
            pool.wait_ge(sem["y_out"], 16 * KD * (hf + 1))

    @block.scalar
    def _(act):
        for n in ("in_evac", "lh_done", "q_sq", "k_sq", "kv_free", "k_scaled", "t_act", "m_exp", "m_ta", "s_nb", "s_b", "s_ta", "silu_done"):
            act.sem_inc(sem[n], PRIME)
        A = nc.scalar.activation

        def split(h, par, i):
            r = raw_index(par)
            act.wait_ge(raw_in[r % 2], 16 * (r // 2 + 1) + 16 * i)
            act.wait_ge(sem["pe_tile"], after(h - 2))
            A(WH[par % 2][:], raw[r % 2][:], ACT.Copy).then_inc(sem["split_h"], 1)

        act.wait_ge(sem["small_in"], 48)
        A(silu_c[:], cols[:, C_C:C_C + KD], ACT.Silu).then_inc(sem["silu_c_done"], 1)
        for j in range(KD):
            act.wait_ge(xin_in[j // 2], 16)
            if j >= 3:
                act.wait_ge(sem["x_add"], j - 2)
            A(sq[j % 2][:] if j else sqs[:], x_in[:, j, :], ACT.Square).then_inc(sem["x_sq"], 1)
        split(0, 0, 0)
        split(1, 1, 0)
        act.wait_ge(sem["trig_args"], 1)
        A(trig[:], ang[:], ACT.Sin).then_inc(sem["trig_done"], 1)
        for j in range(KD):
            act.wait_ge(sem["xr_done"], j + 1)
            act.wait_ge(sem["a1_done"], j // 2 + 1)
            A(x_in[:, j, :], x_in[:, j, :], ACT.Identity, scale=a1[:, j:j + 1], bias=mod1[:, j:j + 1]).then_inc(sem["h_done"], 1)
            act.wait_ge(sem["h_done"], j + 1)
            A(hH[:, j, :], x_in[:, j, :], ACT.Copy).then_inc(sem["hH_done"], 1)

        def in_tile(t, par, i, dst, last=False):
            if not last:
                split(t + 1, par + 1, i)
            act.wait_ge(sem["pe_tile"], after(t))
            A(dst, pair(2 * (par % 2)), ACT.Copy).then_inc(sem["in_evac"], 1)

        def in_pair(t0, i):
            for u in range(2):
                t = t0 + 2 * i + u
                dst = one(lowT[:, bass.ds(t, 1), :]) if t0 < 6 else qkT[:, t - 6, :]
                in_tile(t, t0 + u, i, dst)

        split(2, 2, 0)
        in_tile(0, 0, 0, lowT[:, 0, :], last=True)
        in_tile(1, 1, 0, lowT[:, 1, :], last=True)
        repeat(act, 2, lambda i: in_pair(2, i))
        in_pair(6, 0)
        def low_square(k):
            if k >= 3:
                act.wait_ge(sem["low_add"], k - 2)
            A(sql[k if k < 3 else k - 2][:], lowT[:, k, :], ACT.Square).then_inc(sem["low_sq"], 1)
        for k in range(3):
            low_square(k)
        in_pair(8, 0)
        for k in range(3, 5):
            low_square(k)
        in_pair(10, 0)
        in_pair(12, 0)
        split(15, 15, 0)
        act.wait_ge(sem["low_done"], 5)
        in_tile(14, 14, 0, vT[:, 0, :], last=True)
        split(16, 16, 0)
        in_tile(15, 15, 0, vT[:, 1, :], last=True)
        split(17, 17, 0)

        def up_split(k):
            r = N_IN + k
            act.wait_ge(raw_in[r % 2], 16 * (r // 2 + 1))
            dst, src = (UQH[:, k, :], raw[r % 2][:, 0:MH * QK]) if k < 3 else (UKH[:, k - 3, :], raw[r % 2][:])
            A(dst, src, ACT.Copy).then_inc(sem["split_h"], 1)

        act.wait_ge(sem["ada_acc"], KD + 1)
        up_split(0)
        up_split(1)
        in_tile(16, 16, 0, vT[:, 2, :], last=True)
        up_split(2)
        act.wait_ge(sem["mod2_mm"], KD)
        up_split(3)
        up_split(4)
        in_tile(17, 17, 0, vT[:, 3, :], last=True)

        def low_split(tt, s):
            act.wait_ge(sem["kv_mm"], after(tt - 2))
            A(LH[s][:], lowT[:, 0:5, bass.ds(tt * P, P)], ACT.Copy).then_inc(sem["lh_done"], 1)

        def turn_out(tt):
            act.wait_ge(sem["tr_done"], after(tt))
            A(QN[:, :, bass.ds(tt * P, P)], ps[:, 4, :].rearrange("p (h n) -> p h n", h=MH), ACT.Copy).then_inc(sem["t_act"], 1)
            A(QRK[:, :, bass.ds(tt * P, P)], ps[:, 6, 0:3 * P].rearrange("p (h n) -> p h n", h=3), ACT.Copy).then_inc(sem["t_act"], 1)

        def up_tile(tt, s, first=False, last=False):
            act.wait_ge(sem["q_mm"], after(tt))
            act.wait_ge(sem["tr_done"], after(tt - 2))
            A(work[s][:, 0:MH * QK].rearrange("p (b n) -> p b n", b=2), ps[:, 0:2, 0:384], ACT.Square).then_inc(sem["q_sq"], 1)
            if not last:
                low_split(tt + 1, 1 - s)
            act.wait_ge(sem["kv_mm"], after(tt))
            act.wait_ge(sem["k_ms"], tt)
            kv = ps[:, 2:4, :].rearrange("p b (h c n) -> p (b h) c n", h=2, c=2)
            A(ksq[:, 0:512].rearrange("p (h n) -> p h n", h=MH), kv[:, :, 0, :], ACT.Square).then_inc(sem["k_sq"], 1)
            A(ksq[:, 512:576], ps[:, 7, 64:128], ACT.Square).then_inc(sem["k_sq"], 1)
            A(work[s][:, 768:896], kv[:, 0, 0, :], ACT.Copy).then_inc(sem["kv_free"], 1)
            A(work[s][:, 1024:1408].rearrange("p (h n) -> p h n", h=3), kv[:, 1:MH, 0, :], ACT.Copy).then_inc(sem["kv_free"], 1)
            A(one3(VM[:, bass.ds(tt, 1), :]), kv[:, :, 1, :], ACT.Copy).then_inc(sem["kv_free"], 1)
            if not first:
                turn_out(tt - 1)
            act.wait_ge(sem["rk_done"], after(tt))
            act.wait_ge(sem["kv_free"], 3 * tt + 3 + PRIME)
            for h in range(MH):
                o = 768 if h == 0 else 896 + 128 * h
                A(work[s][:, o:o + P], work[s][:, o:o + P], ACT.Copy, scale=rstd[:, s, 4 + h:5 + h]).then_inc(sem["k_scaled"], 1)

        def one3(ap):
            return ap.rearrange("p o (h n) -> p (o h) n", h=MH)

        act.wait_ge(sem["pe_tile"], after(N_IN - 1))
        act.wait_ge(sem["split_l"], N_IN + N_UP)
        low_split(0, 0)
        up_tile(0, 0, first=True)

        def up_pair(i):
            for u in range(2):
                up_tile(1 + 2 * i + u, (1 + u) % 2)
        repeat(act, 3, up_pair)
        up_tile(NT - 1, 1, last=True)

        def values_out(tt):
            act.wait_ge(sem["vt_mm"], tt + 1)
            A(VS[:, tt, :], ps[:, tt, :], ACT.Copy).then_inc(sem["vt_even"], 1)

        def mla_split(p, e, t=slice(0, S)):
            if p or e:
                act.wait_ge(sem["m_qk"], PRIME if p == 0 else after(NU * (p - 1) + (7 if e == 0 else NU - 1)))
            if e == 0:
                A(mrH[p][:, t], QRK[:, p, t], ACT.Copy).then_inc(sem["m_h"], 1)
            A(mqH[e][:, t], QN[:, 2 * p + e, t], ACT.Copy).then_inc(sem["m_h"], 1)
            A(mkH[e][:, t], KN[:, 2 * p + e, t], ACT.Copy).then_inc(sem["m_h"], 1)

        act.wait_ge(sem["ll_done"], after(NT - 1))
        values_out(0)
        values_out(2)
        act.wait_ge(sem["t_act"], 2 * (NT - 1) + PRIME)
        act.wait_ge(sem["t_dve"], after(NT - 2))
        mla_split(0, 0, slice(0, S - P))
        turn_out(NT - 1)
        act.wait_ge(sem["t_act"], 2 * NT + PRIME)
        act.wait_ge(sem["t_dve"], after(NT - 1))
        act.sem_inc(sem["low_over"], 1)
        mla_split(0, 0, slice(S - P, S))

        for e in range(2):
            o = 64 * e
            A(KRH[e][o:o + 64, :], QRK[o:o + 64, 2, :], ACT.Copy).then_inc(sem["kr_h"], 1)
            values_out(4 + 2 * e)

        def copy_out(pre, u, v, dst, b0=4):
            act.wait_ge(sem[pre + "_tr"], after(u))
            act.wait_ge(sem[pre + "_av"], after(u - 2))
            n = G0[v] * P
            A(dst[v % 2][:, 0:n], ps[:, b0, 0:n], ACT.Copy).then_inc(sem[pre + "_ta"], 1)

        def stick_split(p, e, wait):
            act.wait_ge(*wait)
            o = 64 * e
            A(sqH[e][:], one(qkT[:, bass.ds(p, 1), :]), ACT.Copy).then_inc(sem["s_h"], 1)
            A(skH[e][o:o + 64, :], one(qkT[o:o + 64, bass.ds(4 + p, 1), :]), ACT.Copy).then_inc(sem["s_h"], 1)

        for p in range(MH // 2):
            for v in range(NU + 2):
                if v < NU:
                    u, n = p * NU + v, BLOCKS[v] * P
                    act.wait_ge(sem["m_nm"], after(u))
                    act.wait_ge(sem["m_tr"], after(u - 2))
                    A(pm[v % 2][:, 0:n], pair(2 * (v % 2), n), ACT.Exp, bias=nmx[:, v:v + 1], scale=QK ** -0.5,
                      accum_out=den[:, v:v + 1]).then_inc(sem["m_exp"], 1)
                if v >= 2:
                    copy_out("m", p * NU + v - 2, v - 2, pmT)
                if v == SPLIT1:
                    mla_split(p, 1)
                if v == SPLIT0:
                    if p == 0:
                        mla_split(1, 0)
                    else:
                        stick_split(0, 0, (sem["m_qk"], after(NU + 7)))

        def head_squares(g, o, tt):
            A(junk[:], o[:, tt, :], ACT.Square, accum_out=oss[:, tt, g:g + 1]).then_inc(sem["o_sq"], 1)

        def stick(i, last=False):
            for v in range(NU + 2):
                if last and v < 2:
                    split(H_OUT + v, H_OUT + v, 0)
                if last and v < NT:
                    if v:
                        act.wait_ge(sem["o_sq"], v)
                    head_squares(1, o_mla, v)
                if last and v >= NU - SB_EARLY + 1:
                    tt = v - (NU - SB_EARLY + 1)
                    act.wait_ge(sem["s_o"], after(i * NU + NT + tt))
                    act.wait_ge(sem["o_sq"], NT + tt)
                    head_squares(0, o_sb, ORDER1[tt])
                if v < NU:
                    u, n = i * NU + v, BLOCKS[v] * P
                    act.wait_ge(sem["s_qk"], after(u))
                    act.wait_ge(sem["s_scan"], after(u - 2))
                    A(omb[v % 2][:, 0:n], pair(2 * (v % 2), n), ACT.Sigmoid, scale=-(SBD ** -0.5)).then_inc(sem["s_nb"], 1)
                if v >= 2:
                    copy_out("s", i * NU + v - 2, v - 2, wT)
                if v < NU:
                    act.wait_ge(sem["s_tr"], after(u - 2))
                    A(beta[v % 2][:, 0:n], pair(2 * (v % 2), n), ACT.Sigmoid, scale=SBD ** -0.5).then_inc(sem["s_b"], 1)
                if v == SPLIT1:
                    stick_split(i, 1, (sem["s_qk"], i * NU + PRIME))
                if v == SPLIT0 and not last:
                    stick_split(i + 1, 0, (sem["s_qk"], after(i * NU + 7)))

        with act.Fori(0, SBH // 2 - 1) as i:
            stick(i)
        stick(SBH // 2 - 1, last=True)

        for tt in range(SB_EARLY + 1, NT):
            act.wait_ge(sem["s_o"], after(3 * NU + NT + tt))
            act.wait_ge(sem["o_sq"], NT + tt)
            head_squares(0, o_sb, ORDER1[tt])
        for tt in range(NT):
            if tt == 0:
                act.wait_ge(sem["o_sq"], 2 * NT)
            act.wait_ge(sem["o_mm"], tt + 1)
            A(mixH[:, :, tt * P:(tt + 1) * P], mix_banks(tt), ACT.Copy).then_inc(sem["mix_h"], 1)

        def out_tile(t, par, i):
            if par:
                split(H_OUT + t + 1, H_OUT + par + 1, i)
            act.wait_ge(sem["x2_done"], after(t))
            A(sq2[par % 2][:], one(x2[:, bass.ds(t, 1), :]), ACT.Square).then_inc(sem["x2_sq"], 1)

        act.wait_ge(sem["mix_l"], NT)
        out_tile(0, 0, 0)
        out_tile(1, 1, 0)

        def out_pair(i):
            for u in range(2):
                out_tile(2 + 2 * i + u, 2 + u, i)
        repeat(act, N_OUT // 2 - 2, out_pair)
        split(H_OUT + N_OUT - 1, H_OUT + N_OUT - 1, 0)

        def half_square(k):
            hf, u = k // 2, k % 2
            act.wait_ge(sem["x2_half"], k + 1)
            A(sq2[u][:, 512 * hf:512 * hf + 512], x2[:, KD - 2 + u, 512 * hf:512 * hf + 512], ACT.Square).then_inc(sem["x2_sq"], 1)

        for k in range(3):
            half_square(k)
        split(H_GU, H_GU, 0)
        for n in range(2 * KD):
            if n == 3:
                half_square(3)
                split(H_GU + 1, H_GU + 1, 0)
            hf, j = n // KD, n % KD
            act.wait_ge(sem["xn2_done"], n + 1)
            A(h2H[:, j, 512 * hf:512 * hf + 512], xn2[j % 2][:], ACT.Identity, bias=mod2[:, 8 + j:9 + j]).then_inc(sem["h2H_done"], 1)

        def gate(f, f0, i):
            if f0:
                split(H_GU + 2 * f + 1, H_GU + 2 * f0 + 1, 2 * i)
            else:
                split(H_GU + 2, H_GU + 2, 0)
            act.wait_ge(sem["pe_tile"], after(H_GU + 2 * f))
            act.wait_ge(sem["t_done"], after(f - 2))
            A(gs[f0 % 2][:], pair(4 * (f0 % 2)), ACT.Silu).then_inc(sem["silu_done"], 1)
            if f0:
                split(H_GU + 2 * f + 2, H_GU + 2 * f0 + 2, 2 * i)
        ffn_tiles(act, gate)

        def t_split(d, f, hf, s):
            act.wait_ge(sem["pe_tile"], after(H_DN + d - 2))
            A(TH[s][:], one(t_all[:, bass.ds(f, 1), 512 * hf:512 * hf + 512]), ACT.Copy).then_inc(sem["th_done"], 1)

        def down(d0, i, splits=2):
            for u in range(2):
                d, f = d0 + 2 * i + u, d0 % NF + 2 * i + u
                t_split(d, f, d0 // NF, u)
                if u < splits:
                    split(H_DN + d + 1, H_DN + d0 + u + 1, i)

        for hf in range(2):
            down(hf * NF, 0)
            repeat(act, NF // 2 - 2, lambda i: down(hf * NF + 2, i))
            down(hf * NF + NF - 2, 0, splits=2 - hf)

    @block.vector
    def _(dve):
        for n in ("q_free", "kr_free", "work_done", "t_dve", "m_max", "m_nm", "m_tv", "m_o", "s_scan", "s_wd", "s_tv", "s_o", "t_done", "ll_done", "x2_done", "sqa_done"):
            dve.sem_inc(sem[n], PRIME)
        V = nc.vector
        ch = Chain(dve, sem["dve"])

        dve.wait_ge(sem["small_in"], 48)
        ch(V.tensor_copy(pos_f[:], pos_i[:]))
        ch.sync()
        fr = rows[:, R_FREQ:R_FREQ + HALF]
        for tt in range(NT):
            ch(V.tensor_scalar(ang[:, tt, 0, :], fr, pos_f[:, tt:tt + 1], None, ALU.mult))
            ch(V.tensor_scalar(ang[:, tt, 1, :], fr, pos_f[:, tt:tt + 1], None, ALU.mult))
        ch.sync()
        for c, off in ((0, 0.25), (1, 0.0)):
            ch(V.tensor_scalar(turns[:, :, c, :], ang[:, :, c, :], float(np.float32(1 / (2 * np.pi))), off, ALU.mult, ALU.add))
        ch.sync()
        magic = 1.5 * 2.0 ** 23
        ch(V.tensor_scalar(turns[:], turns[:], magic, None, ALU.add))
        ch.sync()
        ch(V.tensor_scalar(turns[:], turns[:], magic, None, ALU.subtract))
        ch.sync()
        c1 = 6.28125
        c2 = float(np.float32(round((2 * np.pi - c1) * 2 ** 20) / 2 ** 20))
        c3 = float(np.float32(2 * np.pi - c1 - c2))
        for c in (c1, c2, c3):
            ch(V.scalar_tensor_tensor(ang[:], turns[:], -c, ang[:], ALU.mult, ALU.add))
            ch.sync()
        ch(V.tensor_scalar(ang[:, :, 0, :], ang[:, :, 0, :], float(np.pi / 2), None, ALU.add))
        ch.sync()
        V.tensor_scalar(ang[:], ang[:], 3.1415925, -3.1415925, ALU.min, ALU.max).then_inc(sem["trig_args"], 1)

        def diagonals(k, row, diag, t0=0, t1=NT):
            dve.wait_ge(sem["stat_r"], k + 1)
            for tt in range(t0, t1):
                ins = V.tensor_scalar(diag[:, tt, :], ident[:], rms[:, row, tt:tt + 1], None, ALU.mult)
            ins.then_inc(sem["stat_diag"], 1)

        def wsplit(h, par):
            r = raw_index(par)
            dve.wait_ge(sem["split_h"], h + (r - par) + 1)
            V.tensor_tensor(WL[par % 2][:], raw[r % 2][:], WH[par % 2][:], ALU.subtract).then_inc(sem["split_l"], 1)

        for j in range(1, KD):
            dve.wait_ge(sem["x_sq"], j + 1)
            if j >= 2:
                dve.wait_ge(sem["x_add"], j - 1)
            V.tensor_tensor(sqs[:], sqs[:], sq[j % 2][:], ALU.add).then_inc(sem["x_add"], 1)

        def adaln1(g, between=None):
            if g == 0:
                dve.wait_ge(sem["silu_c_done"], 1)
            if g >= 2:
                dve.wait_ge(sem["mod1_mm"], g - 1)
            dve.wait_ge(ada1_in[g], 16)
            a = acc1[g % 2]
            ch(V.tensor_scalar(a[:], ada1[:, g, 0, :], silu_c[:, 0:1], None, ALU.mult))
            for k in range(1, KD - 1):
                if k == 4 and between:
                    between()
                ch.sync()
                ins = V.scalar_tensor_tensor(a[:], ada1[:, g, k, :], silu_c[:, k:k + 1], a[:], ALU.mult, ALU.add)
                if k < KD - 2:
                    ch(ins)
            ins.then_inc(sem["acc1_done"], 1)

        wsplit(0, 0)
        wsplit(1, 1)
        dve.wait_ge(sem["x_turned"], 1)
        ch(V.reduce_sum(rss[:], pair(4).rearrange("p (t n) -> p t n", t=NT), axis=AX.X))
        ch.sync()
        V.tensor_scalar(ms[:, 0, :], rss[:], 1.0 / D, EPS, ALU.mult, ALU.add).then_inc(sem["stat_ms"], 1)
        diagonals(0, 0, diag1)
        adaln1(0)

        def scale_shift(g):
            dve.wait_ge(sem["mod1_mm"], g + 1)
            j = slice(2 * g, 2 * g + 2)
            ch(V.tensor_tensor(mod1[:].rearrange("p (s j) -> p s j", s=2)[:, :, j], ps[:, 4 + g % 2, 0:4].rearrange("p (s j) -> p s j", s=2),
                               cols[:, C_B:C_B + 16].rearrange("p (s j) -> p s j", s=2)[:, :, j], ALU.add))
            ch.sync()
            V.scalar_tensor_tensor(a1[:, j], mod1[:, 8 + 2 * g:10 + 2 * g], 1.0, cols[:, C_GA + 2 * g:C_GA + 2 * g + 2], ALU.add, ALU.mult).then_inc(sem["a1_done"], 1)

        dve.wait_ge(sem["stat_bc"], 1)
        for g in range(KD // 2):
            for j in (2 * g, 2 * g + 1):
                V.tensor_tensor(x_in[:, j, :], x_in[:, j, :], pair(6), ALU.mult).then_inc(sem["xr_done"], 1)
            if g + 1 < KD // 2:
                adaln1(g + 1, lambda: scale_shift(g))
            else:
                scale_shift(g)

        def in_pair(t0, i, step=None):
            for u in range(2):
                wsplit(t0 + 2 * i + u + 1, t0 + u + 1)
            if step is not None:
                ada_step(step)

        def ada_step(step):
            dve.wait_ge(sem["ada2_in"], 16 * (step + 1))
            dve.wait_ge(sem["ada_acc"], step + 1)
            V.scalar_tensor_tensor(acc2[:], ada2[:], silu_c[:, bass.ds(step, 1)], acc2[:], ALU.mult, ALU.add).then_inc(sem["ada_acc"], 1)

        wsplit(2, 2)
        ada_step(0)
        repeat(dve, 2, lambda i: in_pair(2, i, i + 1))
        in_pair(6, 0, 3)
        in_pair(8, 0, 4)
        in_pair(10, 0, 5)
        for k, (b, n) in enumerate(((6, QR), (4, KVR))):
            dve.wait_ge(sem["low_mm"], k + 1)
            ch(V.reduce_sum(lss[:, k, :], pair(b).rearrange("p (t n) -> p t n", t=NT), axis=AX.X))
            ch.sync()
            V.tensor_scalar(ms[:, 1 + k, :], lss[:, k, :], 1.0 / n, EPS, ALU.mult, ALU.add).then_inc(sem["stat_ms"], 1)
        diagonals(1, 1, diagl[0])
        diagonals(2, 2, diagl[1])
        in_pair(12, 0, 6)
        for k in range(5):
            g = 0 if k < 3 else 1
            dve.wait_ge(sem["stat_bc"], 2 + g)
            V.scalar_tensor_tensor(lowT[:, k, :], lowT[:, k, :], cols[:, C_QA + k:C_QA + k + 1], pair(4 + 2 * g), ALU.mult, ALU.mult).then_inc(sem["low_done"], 1)
        in_pair(14, 0, 7)
        def mod2_sum(g):
            dve.wait_ge(sem["mod2_mm"], g + 1)
            V.reduce_sum(mod2[:, 4 * g:4 * g + 4], ps[:, 4 + g % 4, :].rearrange("p (m n) -> p m n", m=4), axis=AX.X).then_inc(sem["mod2_sum"], 1)

        def up_split(k):
            r = N_IN + k
            dve.wait_ge(sem["split_h"], r + 1)
            if k < 3:
                V.tensor_tensor(UQL[:, k, :], raw[r % 2][:, 0:MH * QK], UQH[:, k, :], ALU.subtract).then_inc(sem["split_l"], 1)
            else:
                V.tensor_tensor(UKL[:, k - 3, :], raw[r % 2][:], UKH[:, k - 3, :], ALU.subtract).then_inc(sem["split_l"], 1)

        for g in range(4):
            mod2_sum(g)
        wsplit(17, 17)
        up_split(0)
        up_split(1)
        for g in range(4, KD):
            mod2_sum(g)
        dve.wait_ge(sem["mod2_sum"], KD)
        ch(V.tensor_tensor(mod2[:], mod2[:], cols[:, C_B + 16:C_B + 48], ALU.add))
        ch.sync()
        ch(V.scalar_tensor_tensor(a2[:], mod2[:, 16:24], 1.0, cols[:, C_GF:C_GF + KD], ALU.add, ALU.mult))
        for k in range(2, N_UP):
            up_split(k)

        def low_split(tt, s):
            dve.wait_ge(sem["lh_done"], after(tt))
            V.tensor_tensor(LL[s][:], lowT[:, 0:5, bass.ds(tt * P, P)], LH[s][:], ALU.subtract).then_inc(sem["ll_done"], 1)

        def turn_out(tt):
            dve.wait_ge(sem["tr_done"], after(tt))
            V.tensor_scalar(KN[:, :, bass.ds(tt * P, P)], ps[:, 5, :].rearrange("p (h n) -> p h n", h=MH), cols[:, C_KN:C_KN + 1], None, ALU.mult).then_inc(sem["t_dve"], 1)

        def up_tile(tt, s, first=False, last=False):
            w = work[s]
            dve.wait_ge(sem["q_sq"], after(tt))
            ch(V.reduce_sum(ssq[:, s, 0:4], w[:, 0:MH * QK].rearrange("p (h n) -> p h n", h=MH), axis=AX.X))
            ch.sync()
            V.tensor_scalar(qms[:, s, 0:4], ssq[:, s, 0:4], 1.0 / QK, EPS, ALU.mult, ALU.add).then_inc(sem["q_ms"], 1)
            if not last:
                low_split(tt + 1, 1 - s)
            dve.wait_ge(sem["q_r"], after(tt))
            for h in range(MH):
                o = QK * (h % 2)
                V.scalar_tensor_tensor(w[:, QK * h:QK * (h + 1)], ps[:, h // 2, o:o + QK], rstd[:, s, h:h + 1], rows[:, R_Q:R_Q + QK],
                                       ALU.mult, ALU.mult).then_inc(sem["q_free"], 1)
            dve.wait_ge(sem["k_sq"], 2 * tt + 2 + PRIME)
            ch(V.reduce_sum(ssq[:, s, 4:8], ksq[:, 0:512].rearrange("p (h n) -> p h n", h=MH), axis=AX.X))
            ch(V.reduce_sum(ssq[:, s, 8:9], ksq[:, 512:576], axis=AX.X))
            ch.sync()
            V.tensor_scalar(qms[:, s, 4:8], ssq[:, s, 4:8], 1.0 / NOPE, EPS, ALU.mult, ALU.add)
            V.tensor_scalar(qms[:, s, 8:9], ssq[:, s, 8:9], 1.0 / ROPE, EPS, ALU.mult, ALU.add).then_inc(sem["k_ms"], 1)
            if not first:
                turn_out(tt - 1)
            dve.wait_ge(sem["rk_done"], after(tt))
            V.scalar_tensor_tensor(w[:, 896:960], ps[:, 7, 64:128], rstd[:, s, 8:9], rows[:, R_KR:R_KR + ROPE], ALU.mult, ALU.mult).then_inc(sem["kr_free"], 1)
            dve.wait_ge(sem["kr_free"], after(tt))
            dve.wait_ge(sem["q_free"], 4 * tt + 4 + PRIME)
            x = w[:, 0:5 * QK].rearrange("p (h n) -> p h n", h=5)[:, :, NOPE:QK].rearrange("p h (c n) -> p h c n", c=2)
            for c, dst in ((0, rope_c), (1, rope_s)):
                for hv in range(2):
                    tab = one(trig[:, bass.ds(tt, 1), c, :]).unsqueeze(1).broadcast_to([P, 5, HALF])
                    ch(V.tensor_tensor(dst[:, :, hv, :], x[:, :, hv, :], tab, ALU.mult))
            ch.sync()
            ch(V.tensor_tensor(rot[s][:, 0:5, 0:HALF], rope_c[:, :, 0, :], rope_s[:, :, 1, :], ALU.subtract))
            ch(V.tensor_tensor(rot[s][:, 0:5, HALF:ROPE], rope_c[:, :, 1, :], rope_s[:, :, 0, :], ALU.add))
            ch.sync()
            V.tensor_copy(rot[s][:, 5, :], rot[s][:, 4, :]).then_inc(sem["work_done"], 1)

        dve.wait_ge(sem["trig_done"], 1)
        dve.wait_ge(sem["pe_tile"], after(N_IN - 1))
        low_split(0, 0)
        up_tile(0, 0, first=True)

        def up_pair(i):
            for u in range(2):
                up_tile(1 + 2 * i + u, (1 + u) % 2)

        UPC = 9
        with dve.Fori(0, 3) as i:
            ch.begin(i, 2 * UPC)
            up_pair(i)
        ch.end(3, 2 * UPC)
        up_tile(NT - 1, 1, last=True)

        def values_out(tt):
            dve.wait_ge(sem["vt_mm"], tt + 1)
            V.tensor_copy(VS[:, tt, :], ps[:, tt, :]).then_inc(sem["vt_odd"], 1)

        def mla_split(p, e, t=slice(0, S), done=3):
            ops = [(mqL[e], QN[:, 2 * p + e, t], mqH[e]), (mkL[e], KN[:, 2 * p + e, t], mkH[e])]
            if e == 0:
                ops = [(mrL[p], QRK[:, p, t], mrH[p])] + ops
            for k, (lo, x, hi) in enumerate(ops):
                dve.wait_ge(sem["m_h"], done + 5 * p + 3 * e + k + 1)
                V.tensor_tensor(lo[:, t], x, hi[:, t], ALU.subtract).then_inc(sem["m_l"], 1)

        values_out(1)
        values_out(3)
        mla_split(0, 0, slice(0, S - P), 0)
        turn_out(NT - 1)
        mla_split(0, 0, slice(S - P, S))

        dve.wait_ge(sem["low_over"], 1)
        for e in range(2):
            o = 64 * e
            dve.wait_ge(sem["kr_h"], e + 1)
            V.tensor_tensor(KRL[e][o:o + 64, :], QRK[o:o + 64, 2, :], KRH[e][o:o + 64, :], ALU.subtract).then_inc(sem["kr_l"], 1)
            values_out(5 + 2 * e)

        def copy_out(pre, i, v, dst, b=5):
            if BLOCKS[v] > 1:
                dve.wait_ge(sem[pre + "_tr"], after(i * NU + v))
                dve.wait_ge(sem[pre + "_av"], after(i * NU + v - 2))
                n0, n = G0[v] * P, BLOCKS[v] * P
                V.tensor_copy(dst[v % 2][:, n0:n], ps[:, b, 0:n - n0]).then_inc(sem[pre + "_tv"], 1)

        def stick_split(p, e):
            o = 64 * e
            dve.wait_ge(sem["s_h"], 4 * p + 2 * e + 1)
            V.tensor_tensor(sqL[e][:], one(qkT[:, bass.ds(p, 1), :]), sqH[e][:], ALU.subtract).then_inc(sem["s_l"], 1)
            dve.wait_ge(sem["s_h"], 4 * p + 2 * e + 2)
            V.tensor_tensor(skL[e][o:o + 64, :], one(qkT[o:o + 64, bass.ds(4 + p, 1), :]), skH[e][o:o + 64, :], ALU.subtract).then_inc(sem["s_l"], 1)

        def maxima(p, done, recips):
            return 2 * NU * p + min(done, NU) + recips + PRIME

        for p in range(MH // 2):
            for v in range(NU + 3):
                if v < NU:
                    u, n = p * NU + v, BLOCKS[v] * P
                    dve.wait_ge(sem["m_qk"], after(u))
                    V.reduce_max(mx[:, v:v + 1], pair(2 * (v % 2), n), axis=AX.X).then_inc(sem["m_max"], 1)
                    dve.wait_ge(sem["m_max"], maxima(p, v + 1, max(0, v - 3)))
                    V.tensor_scalar(nmx[:, v:v + 1], mx[:, v:v + 1], -(QK ** -0.5), None, ALU.mult).then_inc(sem["m_nm"], 1)
                if 2 <= v < NU + 2:
                    copy_out("m", p, v - 2, pmT)
                if v >= 3:
                    k = v - 3
                    e, qt = UNITS[k]
                    dve.wait_ge(sem["m_av"], after(p * NU + k))
                    V.reciprocal(rden[:, k:k + 1], den[:, k:k + 1]).then_inc(sem["m_max"], 1)
                    dve.wait_ge(sem["m_max"], maxima(p, v + 1, k + 1))
                    V.tensor_scalar(o_mla[:, qt, (2 * p + e) * VD:(2 * p + e + 1) * VD], ps[:, 6 + k % 2, 0:VD], rden[:, k:k + 1], None, ALU.mult).then_inc(sem["m_o"], 1)
                if v == SPLIT1:
                    mla_split(p, 1)
                if v == SPLIT0:
                    if p == 0:
                        mla_split(1, 0)
                    else:
                        stick_split(0, 0)

        dve.wait_ge(sem["left_one"], 2)

        def stick(i, last=False):
            for v in range(NU + 3):
                if v < NU:
                    u, n = i * NU + v, BLOCKS[v] * P
                    dve.wait_ge(sem["s_nb"], after(u))
                    dve.wait_ge(sem["s_wp"], after(u - 2))
                    V.tensor_tensor_scan(left[v % 2][:, 1:n], omb[v % 2][:, 0:n - 1], omb[v % 2][:, 0:n - 1], 1.0, ALU.mult, ALU.bypass).then_inc(sem["s_scan"], 1)
                if 2 <= v < NU + 2:
                    copy_out("s", i, v - 2, wT)
                if v < NU:
                    dve.wait_ge(sem["s_b"], after(u))
                    dve.wait_ge(sem["s_scan"], after(u))
                    c = dve_share(n)
                    V.tensor_tensor(beta[v % 2][:, 0:c], beta[v % 2][:, 0:c], left[v % 2][:, 0:c], ALU.mult).then_inc(sem["s_wd"], 1)
                if v >= 3:
                    k = v - 3
                    e, qt = UNITS[k]
                    dve.wait_ge(sem["s_av"], after(i * NU + k))
                    V.tensor_copy(o_sb[:, qt, bass.ds((2 * i + e) * SBD, SBD)], ps[:, 6 + k % 2, 0:SBD]).then_inc(sem["s_o"], 1)
                if v == SPLIT1:
                    stick_split(i, 1)
                if v == SPLIT0 and not last:
                    stick_split(i + 1, 0)
                if last and v < 2:
                    wsplit(H_OUT + v, H_OUT + v)
                if last and v >= NU - SB_EARLY + 2:
                    head_mean_squares(v - (NU - SB_EARLY + 2))

        def head_mean_squares(tt):
            dve.wait_ge(sem["o_sq"], NT + tt + 1)
            V.tensor_scalar(oms[:, ORDER1[tt], :], oss[:, ORDER1[tt], :], 1.0 / 512, EPS, ALU.mult, ALU.add).then_inc(sem["o_ms"], 1)

        with dve.Fori(0, SBH // 2 - 1) as i:
            stick(i)
        stick(SBH // 2 - 1, last=True)

        dve.wait_ge(sem["grow_in"], 16)
        for tt in range(SB_EARLY + 1, NT):
            head_mean_squares(tt)
        for tt in range(NT + 1):
            if tt < NT:
                dve.wait_ge(sem["o_r"], ORDER1.index(tt) + 1)
                if tt >= 2:
                    dve.wait_ge(sem["o_mm"], tt - 1)
                for g, o in ((0, o_sb), (1, o_mla)):
                    V.scalar_tensor_tensor(ostage[tt % 2][:, g, :], o[:, tt, :], ors[:, tt, g:g + 1], grow[:, g, :], ALU.mult, ALU.mult).then_inc(sem["o_scaled"], 1)
            if tt >= 1:
                k = tt - 1
                dve.wait_ge(sem["mix_h"], k + 1)
                V.tensor_tensor(mixL[:, :, k * P:(k + 1) * P], mix_banks(k), mixH[:, :, k * P:(k + 1) * P], ALU.subtract).then_inc(sem["mix_l"], 1)

        dve.wait_ge(sem["x2_in"], 16)
        dve.wait_ge(sem["sqa_zero"], 1)

        def out_tile(t, par, b):
            if par:
                wsplit(H_OUT + t + 1, H_OUT + par + 1)
            dve.wait_ge(sem["pe_tile"], after(H_OUT + t))
            xt = one(x2[:, bass.ds(t, 1), :])
            V.scalar_tensor_tensor(xt, pair(b), mod2[:, bass.ds(t, 1)], xt, ALU.mult, ALU.add).then_inc(sem["x2_done"], 1)
            dve.wait_ge(sem["x2_sq"], t + 1)
            dve.wait_ge(sem["sqa_done"], after(t - 1))
            V.tensor_tensor(sqa[:], sqa[:], sq2[par % 2][:], ALU.add).then_inc(sem["sqa_done"], 1)

        out_tile(0, 0, 4)
        out_tile(1, 1, 6)

        def out_pair(i):
            for u in range(2):
                out_tile(2 + 2 * i + u, 2 + u, 2 * u)
        repeat(dve, N_OUT // 2 - 2, out_pair)
        wsplit(H_OUT + N_OUT - 1, H_OUT + N_OUT - 1)

        def half_residual(k):
            hf, u = k // 2, k % 2
            if hf == 0:
                dve.wait_ge(sem["half_mm"], u + 1)
            else:
                dve.wait_ge(sem["pe_tile"], after(H_OUT + N_OUT - 2 + u))
            t = slice(512 * hf, 512 * hf + 512)
            xt = x2[:, KD - 2 + u, t]
            V.scalar_tensor_tensor(xt, ps[:, 2 * u + hf, :], mod2[:, KD - 2 + u:KD - 1 + u], xt, ALU.mult, ALU.add).then_inc(sem["x2_half"], 1)

        def half_add(k):
            t = slice(512 * (k // 2), 512 * (k // 2) + 512)
            dve.wait_ge(sem["x2_sq"], N_OUT - 2 + k + 1)
            dve.wait_ge(sem["sqa_done"], after(N_OUT - 3 + k))
            V.tensor_tensor(sqa[:, t], sqa[:, t], sq2[k % 2][:, t], ALU.add).then_inc(sem["sqa_done"], 1)

        def modulate_half(n):
            if n < 2 * KD:
                hf, j = n // KD, n % KD
                if j == 0:
                    dve.wait_ge(sem["stat_bc"], 4 + hf)
                if n >= 2:
                    dve.wait_ge(sem["h2L_done"], n - 1)
                V.scalar_tensor_tensor(xn2[j % 2][:], x2[:, j, 512 * hf:512 * hf + 512], a2[:, j:j + 1], ps[:, 6 + hf, :], ALU.mult, ALU.mult).then_inc(sem["xn2_done"], 1)
            if n >= 1:
                hf, j = (n - 1) // KD, (n - 1) % KD
                t = slice(512 * hf, 512 * hf + 512)
                dve.wait_ge(sem["h2H_done"], n)
                V.scalar_tensor_tensor(h2L[:, j, t], xn2[j % 2][:], mod2[:, 8 + j:9 + j], h2H[:, j, t], ALU.add, ALU.subtract).then_inc(sem["h2L_done"], 1)

        def half_means(hf):
            dve.wait_ge(sem["r2_mm"], hf + 1)
            t = slice(4 * hf, 4 * hf + 4)
            ch(V.reduce_sum(rss[:, t], ps[:, 4 + hf, :].rearrange("p (t n) -> p t n", t=4), axis=AX.X))
            ch.sync()
            V.tensor_scalar(ms[:, 3, t], rss[:, t], 1.0 / D, EPS, ALU.mult, ALU.add).then_inc(sem["stat_ms"], 1)

        half_residual(0)
        half_add(0)
        half_residual(1)
        half_add(1)
        half_means(0)
        half_residual(2)
        half_add(2)
        diagonals(3, 3, diag2, 0, 4)
        wsplit(H_GU, H_GU)
        for n in range(2 * KD + 1):
            if n == 3:
                half_residual(3)
                half_add(3)
            if n == 4:
                wsplit(H_GU + 1, H_GU + 1)
            if n == 5:
                half_means(1)
            if n == 7:
                diagonals(4, 3, diag2, 4, NT)
            modulate_half(n)

        dve.wait_ge(sem["x2_spill"], 16)

        def t_split(d, f, hf, s):
            dve.wait_ge(sem["th_done"], d + 1)
            V.tensor_tensor(TL[s][:], one(t_all[:, bass.ds(f, 1), 512 * hf:512 * hf + 512]), TH[s][:], ALU.subtract).then_inc(sem["tl_done"], 1)

        def gate(f, f0, i):
            if f0:
                wsplit(H_GU + 2 * f + 1, H_GU + 2 * f0 + 1)
            wsplit(H_GU + 2 * f + 2, H_GU + 2 * f0 + 2)
            if f0 == NF - 1:
                t_split(0, 0, 0, 0)
            dve.wait_ge(sem["silu_done"], after(f))
            dve.wait_ge(sem["pe_tile"], after(H_GU + 2 * f + 1))
            V.tensor_tensor(one(t_all[:, bass.ds(f, 1), :]), pair(4 * (f0 % 2) + 2), gs[f0 % 2][:], ALU.mult).then_inc(sem["t_done"], 1)
        ffn_tiles(dve, gate)

        def down(d0, i, ahead=0, splits=2):
            for u in range(2):
                d, f = d0 + 2 * i + u, d0 % NF + 2 * i + u
                if u >= ahead:
                    t_split(d, f, d0 // NF, u)
                if u < splits:
                    wsplit(H_DN + d + 1, H_DN + d0 + u + 1)

        def result(hf, o):
            if o < KD - 1:
                dve.wait_ge(sem["d_mm"], hf * (KD - 1) + o + 1)
            else:
                dve.wait_ge(sem["pe_tile"], after(H_DN + (hf + 1) * NF - 1))
            V.scalar_tensor_tensor(yst[:, o, :], ps[:, o, :], mod2[:, 24 + o:25 + o], xres[:, o, :], ALU.mult, ALU.add).then_inc(sem["y_done"], 1)

        for hf in range(2):
            if hf == 0:
                down(0, 0, ahead=1)
            else:
                wsplit(H_DN + NF + 2, H_DN + NF + 2)
            repeat(dve, NF // 2 - 2, lambda i: down(hf * NF + 2, i))
            down(hf * NF + NF - 2, 0, splits=2 - hf)
            dve.wait_ge(sem["xres_in"], 16 * (hf + 1))
            if hf == 1:
                dve.wait_ge(sem["y_out"], 16 * KD)
            else:
                t_split(NF, 0, 1, 0)
            for o in range(KD):
                if hf == 0 and o == 4:
                    down(NF, 0, ahead=1, splits=1)
                result(hf, o)

    @block.tensor
    def _(pe):
        for n in ("pe_tile", "q_mm", "kv_mm", "tr_done", "m_qk", "m_tr", "m_av", "s_qk", "s_tr", "s_av"):
            pe.sem_inc(sem[n], PRIME)
        mm = nc.tensor.matmul

        def three(out, lh, ll, rh, rl, first, last):
            mm(out, lh, rh, start=first, stop=False)
            mm(out, lh, rl, start=False, stop=False)
            return mm(out, ll, rh, start=False, stop=last)

        def proj_tile(h, par, b, XH, XL):
            pe.wait_ge(sem["split_l"], h + (raw_index(par) - par) + 1)
            s = par % 2
            for j in range(KD):
                for k, (l, r) in enumerate(((WH, XH), (WH, XL), (WL, XH))):
                    for hf in range(2):
                        last = mm(ps[:, b + hf, :], l[s][:, j * P:(j + 1) * P], r[:, j, 512 * hf:512 * hf + 512],
                                  start=(j == 0 and k == 0), stop=(j == KD - 1 and k == 2))
            last.then_inc(sem["pe_tile"], 1)

        def half_chunk(s, b, hf, j, XH, XL):
            w, t = slice(j * P, (j + 1) * P), slice(512 * hf, 512 * hf + 512)
            return three(ps[:, b + hf, :], WH[s][:, w], WL[s][:, w], XH[:, j, t], XL[:, j, t], j == 0, j == KD - 1)

        def broadcast(k, diag, b, halves=(0, 1)):
            pe.wait_ge(sem["stat_diag"], k + 1)
            for hf in halves:
                ins = mm(ps[:, b + hf, :], ones[:], diag[:, 4 * hf:4 * hf + 4, :].rearrange("p t n -> p (t n)"), start=True, stop=True)
            ins.then_inc(sem["stat_bc"], 1)

        pe.wait_ge(sem["pool_const"], 10)
        pe.wait_ge(sem["x_add"], KD - 1)
        for tt in range(NT):
            last = nc.tensor.transpose(ps[:, 4 + tt // 4, tt % 4 * P:(tt % 4 + 1) * P], sqs[:, tt * P:(tt + 1) * P], ident[:])
        last.then_inc(sem["x_turned"], 1)

        def adaln1(g):
            if g == 0:
                pe.wait_ge(sem["stat_ms"], 1)
            if g >= 2:
                pe.wait_ge(sem["a1_done"], g - 1)
            pe.wait_ge(ada1_in[g], 16)
            pe.wait_ge(sem["silu_c_done"], 1)
            pe.wait_ge(sem["acc1_done"], g + 1)
            for m in range(4):
                w = slice(m * P, (m + 1) * P)
                mm(ps[:, 4 + g % 2, m:m + 1], ada1[:, g, KD - 1, w], silu_c[:, KD - 1:KD], start=True, stop=False, skip_group_check=True)
                last = mm(ps[:, 4 + g % 2, m:m + 1], acc1[g % 2][:, w], ones[:, 0:1], start=False, stop=True, skip_group_check=True)
            last.then_inc(sem["mod1_mm"], 1)

        broadcast(0, diag1, 6)
        adaln1(0)

        def in_pair(t0, i):
            for u in range(2):
                t = t0 + 2 * i + u
                pe.wait_ge(sem["in_evac"], after(t - 2))
                proj_tile(t, t0 + u, 2 * u, hH, hL)

        pe.wait_ge(sem["split_l"], 2)
        for n in range(KD + LAG):
            if n % 2 == 0 and n // 2 + 1 < KD // 2:
                adaln1(n // 2 + 1)
            if n < KD:
                pe.wait_ge(sem["hL_done"], n + 1)
                for hf in range(2):
                    last = half_chunk(0, 0, hf, n, hH, hL)
                if n == KD - 1:
                    last.then_inc(sem["pe_tile"], 1)
            if n >= LAG:
                for hf in range(2):
                    last = half_chunk(1, 2, hf, n - LAG, hH, hL)
        last.then_inc(sem["pe_tile"], 1)
        repeat(pe, 2, lambda i: in_pair(2, i))
        in_pair(6, 0)
        def low_sums(k):
            pe.wait_ge(sem["low_add"], 2 + k)
            for tt in range(NT):
                last = nc.tensor.transpose(ps[:, 6 - 2 * k + tt // 4, tt % 4 * P:(tt % 4 + 1) * P], sql[k][:, tt * P:(tt + 1) * P], ident[:])
            last.then_inc(sem["low_mm"], 1)

        in_pair(8, 0)
        low_sums(0)
        in_pair(10, 0)
        low_sums(1)
        in_pair(12, 0)
        broadcast(1, diagl[0], 4)
        broadcast(2, diagl[1], 6)
        in_pair(14, 0)
        pe.wait_ge(sem["ada_acc"], KD + 1)
        pe.wait_ge(sem["low_done"], 5)

        def mod2_turn(g):
            if g >= 4:
                pe.wait_ge(sem["mod2_sum"], g - 3)
            for m in range(4):
                last = nc.tensor.transpose(ps[:, 4 + g % 4, m * P:(m + 1) * P], acc2[:, (4 * g + m) * P:(4 * g + m + 1) * P], ident[:])
            last.then_inc(sem["mod2_mm"], 1)

        for u in range(2):
            for g in range(4 * u, 4 * u + 4):
                mod2_turn(g)
            pe.wait_ge(sem["in_evac"], after(14 + u))
            proj_tile(16 + u, 16 + u, 2 * u, hH, hL)

        def turn(tt, s):
            pe.wait_ge(sem["work_done"], after(tt))
            pe.wait_ge(sem["k_scaled"], 4 * tt + 4 + PRIME)
            pe.wait_ge(sem["t_act"], 2 * tt + PRIME)
            pe.wait_ge(sem["t_dve"], after(tt - 1))
            w = work[s]
            for h in range(MH):
                nc.tensor.transpose(ps[:, 4, h * P:(h + 1) * P], w[:, QK * h:QK * h + P], ident[:])
                o = 768 if h == 0 else 896 + 128 * h
                nc.tensor.transpose(ps[:, 5, h * P:(h + 1) * P], w[:, o:o + P], ident[:])
            for g in range(3):
                last = nc.tensor.transpose(ps[:, 6, g * P:(g + 1) * P], rot[s][:, 2 * g:2 * g + 2, :].rearrange("p h n -> p (h n)"), ident[:])
            last.then_inc(sem["tr_done"], 1)

        def up_tile(tt, s, first=False):
            pe.wait_ge(sem["ll_done"], after(tt))
            pe.wait_ge(sem["q_free"], 4 * tt + PRIME)
            for k in range(3):
                for c in range(2):
                    last = three(ps[:, c, 0:384], LH[s][:, k, :], LL[s][:, k, :], UQH[:, k, 384 * c:384 * (c + 1)], UQL[:, k, 384 * c:384 * (c + 1)], k == 0, k == 2)
            last.then_inc(sem["q_mm"], 1)
            pe.wait_ge(sem["kv_free"], 3 * tt + PRIME)
            for k in range(2):
                for c in range(2):
                    last = three(ps[:, 2 + c, :], LH[s][:, 3 + k, :], LL[s][:, 3 + k, :], UKH[:, k, 512 * c:512 * (c + 1)], UKL[:, k, 512 * c:512 * (c + 1)], k == 0, k == 1)
            pe.wait_ge(sem["kr_free"], after(tt - 1))
            nc.tensor.transpose(ps[:, 7, 0:P], krT(tt), ident[:]).then_inc(sem["kv_mm"], 1)
            if not first:
                turn(tt - 1, 1 - s)

        def krT(tt):
            return lowT[:, 5, bass.ds(tt * P, P)]

        for tt in range(NT):
            up_tile(tt, tt % 2, first=(tt == 0))
        def values_turn(tt):
            for c in range(4):
                last = nc.tensor.transpose(ps[:, tt, c * P:(c + 1) * P], vT[:, c, tt * P:(tt + 1) * P], ident[:])
            last.then_inc(sem["vt_mm"], 1)

        pe.wait_ge(sem["q_free"], 4 * NT + PRIME)
        values_turn(0)
        values_turn(1)
        pe.wait_ge(sem["kv_free"], 3 * NT + PRIME)
        values_turn(2)
        values_turn(3)
        turn(NT - 1, 1)
        pe.wait_ge(sem["t_act"], 2 * NT + PRIME)
        pe.wait_ge(sem["t_dve"], after(NT - 1))
        for tt in range(4, NT):
            values_turn(tt)

        wready = {"m": ("m_exp",), "s": ("s_wd", "s_wp")}
        sfree = {"m": "m_exp", "s": "s_b"}

        def mla_scores(p, e, q0, out, k0, w, diagonal):
            q, k = slice(q0, q0 + P), slice(k0, k0 + w)
            three(out, mqH[e][:, q], mqL[e][:, q], mkH[e][:, k], mkL[e][:, k], True, False)
            last = three(out, mrH[p][:, q], mrL[p][:, q], KRH[e][:, k], KRL[e][:, k], False, not diagonal)
            if diagonal:
                last = mm(out[:, 0:P], identb[:], mask_mla[:], start=False, stop=True)
            return last

        def stick_scores(p, e, q0, out, k0, w, diagonal):
            q, k = slice(q0, q0 + P), slice(k0, k0 + w)
            last = three(out, sqH[e][:, q], sqL[e][:, q], skH[e][:, k], skL[e][:, k], True, not diagonal)
            if diagonal:
                last = mm(out[:, 0:P], identb[:], mask_sb[:], start=False, stop=True)
            return last

        def qk(pre, i, v, scores):
            (e, qt), n = UNITS[v], BLOCKS[v] * P
            for c0 in range(0, n, 512):
                w = min(512, n - c0)
                last = scores(i, e, qt * P, ps[:, 2 * (v % 2) + c0 // 512, 0:w], qt * P + c0, w, c0 == 0)
            last.then_inc(sem[pre + "_qk"], 1)

        def attention(pre, i, scores, src, dst, V, width, split_done, ahead):
            def turn_unit(v):
                u, b = i * NU + v, BLOCKS[v]
                for w in wready[pre]:
                    pe.wait_ge(sem[w], after(u))
                pe.wait_ge(sem[pre + "_ta"], after(u - 1))
                pe.wait_ge(sem[pre + "_tv"], i * NG1 + G1_BEFORE[v] + PRIME)
                for k in range(b):
                    bank, c = (4, k) if k < G0[v] else (5, k - G0[v])
                    last = nc.tensor.transpose(ps[:, bank, c * P:(c + 1) * P], src[v % 2][:, k * P:(k + 1) * P], ident[:])
                last.then_inc(sem[pre + "_tr"], 1)

            def values(v):
                u, b = i * NU + v, BLOCKS[v]
                e, qt = UNITS[v]
                pe.wait_ge(sem[pre + "_o"], after(u - 2))
                pe.wait_ge(sem[pre + "_ta"], after(u))
                if b > 1:
                    pe.wait_ge(sem[pre + "_tv"], i * NG1 + G1_BEFORE[v + 1] + PRIME)
                for k in range(b):
                    last = mm(ps[:, 6 + v % 2, 0:width], dst[v % 2][:, k * P:(k + 1) * P],
                              V[:, qt + k, bass.ds((2 * i + e) * width, width)], start=(k == 0), stop=(k == b - 1))
                last.then_inc(sem[pre + "_av"], 1)

            for v in range(NU):
                if v + 2 < NU:
                    if v + 2 == NU // 2:
                        pe.wait_ge(sem[pre + "_l"], split_done)
                    pe.wait_ge(sem[sfree[pre]], after(i * NU + v))
                    qk(pre, i, v + 2, scores)
                elif ahead:
                    pe.wait_ge(sem[sfree[pre]], after(i * NU + v))
                    ahead(v)
                turn_unit(v)
                if v >= 1:
                    values(v - 1)
            values(NU - 1)

        pe.wait_ge(sem["vt_even"], 2)
        pe.wait_ge(sem["vt_odd"], 2)
        pe.wait_ge(sem["kr_zero"], 2)
        pe.wait_ge(sem["kr_l"], 1)
        pe.wait_ge(sem["m_l"], 6)
        for v in range(2):
            qk("m", 0, v, mla_scores)

        def mla_ahead(v):
            pe.wait_ge(sem["m_l"], 11)
            qk("m", 1, v + 2 - NU, mla_scores)

        def stick_ahead(i):
            def first(v):
                pe.wait_ge(sem["s_l"], 4 * i + 2)
                qk("s", i, v + 2 - NU, stick_scores)
            return first

        def stick_first(v):
            pe.wait_ge(sem["sk_zero"], 2)
            stick_ahead(0)(v)

        pe.wait_ge(sem["kr_zero"], 4)
        pe.wait_ge(sem["kr_l"], 2)
        pe.wait_ge(sem["vt_even"], NT // 2)
        pe.wait_ge(sem["vt_odd"], NT // 2)
        attention("m", 0, mla_scores, pm, pmT, VM, VD, 8, mla_ahead)
        attention("m", 1, mla_scores, pm, pmT, VM, VD, 13, stick_first)
        pe.wait_ge(sem["sk_zero"], 4)
        with pe.Fori(0, SBH // 2 - 1) as i:
            attention("s", i, stick_scores, beta, wT, VS, SBD, 4 * i + 4, stick_ahead(i + 1))
        i = SBH // 2 - 1
        attention("s", i, stick_scores, beta, wT, VS, SBD, 4 * i + 4, None)

        def mix(tt):
            pe.wait_ge(sem["o_scaled"], 2 * tt + 2)
            if tt >= 2:
                pe.wait_ge(sem["mix_l"], tt - 1)
            for c in range(8):
                last = nc.tensor.transpose(ps[:, 2 * (tt % 2) + c // 4, c % 4 * P:(c % 4 + 1) * P], ostage[tt % 2][:, c // 4, c % 4 * P:(c % 4 + 1) * P], ident[:])
            last.then_inc(sem["o_mm"], 1)

        for tt in range(NT // 2 + 1):
            mix(tt)

        mix_at = {(0, 4): 5, (1, 0): 6, (1, 4): 7}
        pe.wait_ge(sem["split_l"], raw_index(H_OUT) + 2)
        for hf in range(2):
            pe.wait_ge(sem["mix_l"], (hf + 1) * NT // 2)
            for u in range(2):
                for j in range(KD):
                    if hf == 0 and (u, j) in mix_at:
                        mix(mix_at[u, j])
                    last = half_chunk(u, 4 + 2 * u, hf, j, mixH, mixL)
                if hf == 1:
                    last.then_inc(sem["pe_tile"], 1)

        def out_pair(i):
            for u in range(2):
                t = 2 + 2 * i + u
                pe.wait_ge(sem["x2_done"], after(t - 2))
                proj_tile(H_OUT + t, H_OUT + 2 + u, 2 * u, mixH, mixL)
        repeat(pe, N_OUT // 2 - 2, out_pair)

        def residual_sums(hf):
            pe.wait_ge(sem["sqa_done"], after(N_OUT - 1 + 2 * hf))
            for tt in range(4 * hf, 4 * hf + 4):
                last = nc.tensor.transpose(ps[:, 4 + hf, tt % 4 * P:(tt % 4 + 1) * P], sqa[:, tt * P:(tt + 1) * P], ident[:])
            last.then_inc(sem["r2_mm"], 1)

        for hf in range(2):
            for u in range(2):
                if hf == 0:
                    pe.wait_ge(sem["split_l"], raw_index(H_OUT) + N_OUT - 1 + u)
                    pe.wait_ge(sem["x2_done"], after(N_OUT - 4 + u))
                for j in range(KD):
                    if (hf, u, j) == (1, 0, 3):
                        residual_sums(0)
                    if (hf, u, j) == (1, 1, 2):
                        broadcast(3, diag2, 6, (0,))
                    last = half_chunk(u, 2 * u, hf, j, mixH, mixL)
                last.then_inc(sem["pe_tile" if hf else "half_mm"], 1)

        for hf in range(2):
            for n in range(KD + LAG):
                if (hf, n) == (0, 3):
                    residual_sums(1)
                if (hf, n) == (0, 6):
                    broadcast(4, diag2, 6, (1,))
                if n < KD:
                    if n == 0:
                        pe.wait_ge(sem["split_l"], raw_index(H_GU) + 1)
                        pe.wait_ge(sem["x2_half"], 1 + 2 * hf)
                    pe.wait_ge(sem["h2L_done"], hf * KD + n + 1)
                    last = half_chunk(0, 0, hf, n, h2H, h2L)
                    if hf == 1 and n == KD - 1:
                        last.then_inc(sem["pe_tile"], 1)
                if n >= LAG:
                    if n == LAG:
                        pe.wait_ge(sem["split_l"], raw_index(H_GU) + 2)
                        pe.wait_ge(sem["x2_half"], 2 + 2 * hf)
                    last = half_chunk(1, 2, hf, n - LAG, h2H, h2L)
        last.then_inc(sem["pe_tile"], 1)

        def gate(f, f0, i):
            if f0 == 0:
                return
            b = 4 * (f0 % 2)
            pe.wait_ge(sem["silu_done"], after(f - 2))
            proj_tile(H_GU + 2 * f, H_GU + 2 * f0, b, h2H, h2L)
            pe.wait_ge(sem["t_done"], after(f - 2))
            proj_tile(H_GU + 2 * f + 1, H_GU + 2 * f0 + 1, b + 2, h2H, h2L)
        ffn_tiles(pe, gate)

        def down_tile(hf, d, par, first=False, last_=False):
            pe.wait_ge(sem["split_l"], H_DN + d + N_UP + 1)
            pe.wait_ge(sem["tl_done"], d + 1)
            s = par % 2
            for o in range(KD):
                if first and hf == 1:
                    pe.wait_ge(sem["y_done"], o + 1)
                elif first and o % 4 == 0:
                    pe.wait_ge(sem["t_done"], after(NF - 2 + o // 4))
                w = slice(o * P, (o + 1) * P)
                last = three(ps[:, o, :], WH[s][:, w], WL[s][:, w], TH[s][:], TL[s][:], first, last_)
                if last_ and o < KD - 1:
                    last.then_inc(sem["d_mm"], 1)
            last.then_inc(sem["pe_tile"], 1)

        for hf in range(2):
            d0 = hf * NF
            down_tile(hf, d0, H_DN, first=True)
            down_tile(hf, d0 + 1, H_DN + 1)

            def down(i, hf=hf, d0=d0):
                for u in range(2):
                    down_tile(hf, d0 + 2 + 2 * i + u, H_DN + u)
            repeat(pe, NF // 2 - 2, down)
            down_tile(hf, d0 + NF - 2, H_DN)
            down_tile(hf, d0 + NF - 1, H_DN + 1, last_=True)
    ctx.close()


def kernel(**inputs):
    import concourse.bacc as bacc
    from concourse.bass_utils import run_bass_kernel_spmd as run

    g = {k: np.asarray(v) for k, v in inputs.items()}

    def col(v):
        return v.reshape(-1, P).T

    c = np.ascontiguousarray
    win = g["w_in"][0].reshape(KD, P, -1)
    arrays = {
        "xT": c(g["x"][0, ::-1].T.reshape(KD, P, S)),
        "cols": c(np.concatenate([col(g["c"][0]), col(g["b_ada"][0]), col(g["norm_attn"][0]), col(g["norm_ffn"][0]),
                                  col(g["q_a_norm"][0]), col(g["kv_a_norm"][0]), col(g["k_nope_norm"][0])], axis=1)),
        "rows": c(np.broadcast_to(np.concatenate([g["q_norm"][0], g["k_rope_norm"][0],
                                                  (1.0 / (10000.0 ** (np.arange(HALF, dtype=np.float32) / HALF))).astype(np.float32)]), (P, NROW))),
        "grow": c(np.broadcast_to(np.stack([g["out_norm_sb"][0], g["out_norm_mla"][0]]), (P, 2, 512))),
        "pos": c(g["positions"][0, ::-1].reshape(NT, P).T),
        "ada1": c(g["w_ada"][0][:, 0:2 * D].reshape(KD, P, 2, KD // 2, 2 * P).transpose(3, 1, 0, 2, 4).reshape(KD // 2, P, KD, 4 * P)),
        "ada2": c(g["w_ada"][0][:, 2 * D:].reshape(KD, P, 4 * D)),
        "win": c(np.stack([win[:, :, w:w + P].transpose(1, 0, 2).reshape(P, D) for w in W_COLS])),
        "qup": c(g["w_q_up"][0].reshape(3, P, MH * QK)),
        "kvup": c(g["w_kv_up"][0].reshape(2, P, D)),
        "wout": c(g["w_out"][0].reshape(KD, P, KD, P).transpose(2, 1, 0, 3).reshape(KD, P, D)),
        "gu": c(np.stack([g["w_gate"][0], g["w_up"][0]]).reshape(2, KD, P, NF, P).transpose(3, 0, 2, 1, 4).reshape(2 * NF, P, D)),
        "down": c(g["w_down"][0].reshape(NF, P, D)),
    }
    nc = bacc.Bacc("TRN2", target_bir_lowering=False, num_devices=1)
    aps = {k: nc.dram_tensor(k, v.shape, mybir.dt.from_np(v.dtype), kind="ExternalInput").ap() for k, v in arrays.items()}
    x2_d = nc.dram_tensor("x2_spill_d", (KD, P, S), F32, kind="Internal").ap()
    out = nc.dram_tensor("out", (KD, P, S), F32, kind="ExternalOutput").ap()
    build(nc, aps["xT"], aps["cols"], aps["rows"], aps["grow"], aps["pos"], aps["ada1"], aps["ada2"], aps["win"], aps["qup"],
          aps["kvup"], aps["wout"], aps["gu"], aps["down"], x2_d, out)
    r = run(nc, [arrays], core_ids=[0])
    return c(r.results[0]["out"].reshape(D, S).T[::-1][None])
```
